# Optimizing a Trainium2 kernel written in Bass

```python
import math
import jax, jax.numpy as jnp
from jax import lax
import numpy as np

D_MODEL = 1024
BATCH = 1
SEQ = 256
DEPTH = 2

N_A_LAYERS = DEPTH // 2
N_B_LAYERS = DEPTH - N_A_LAYERS
D_SSM = D_MODEL
SSM_GROUP = 16
N_GROUPS = D_SSM // SSM_GROUP
STATE = 64
N_HEADS = 16
HEAD_DIM = 64
D_ATT = N_HEADS * HEAD_DIM
D_FF = 2816
CONV_W = 3
Q_BLOCK = 128
EPS = 1e-6
DT_MIN = 1e-3
DT_MAX = 1e-1


def rms_norm(x, g):
    xf = x.astype(jnp.float32)
    y = xf * lax.rsqrt(jnp.mean(xf * xf, axis=-1, keepdims=True) + EPS)
    return (y * g.astype(jnp.float32)).astype(x.dtype)

def s5_mixer(h, w_in, a_re, a_im, log_dt, b_re, b_im, c_re, c_im, d_skip, w_glu):
    bsz, seq, _ = h.shape
    f32 = jnp.float32
    u = (h @ w_in).astype(f32).reshape(bsz, seq, N_GROUPS, SSM_GROUP)
    a_re = a_re.astype(f32)
    a_im = a_im.astype(f32)
    dt = jnp.exp(log_dt.astype(f32))[:, None]
    mag = jnp.exp(a_re * dt)
    ab_re = mag * jnp.cos(a_im * dt)
    ab_im = mag * jnp.sin(a_im * dt)
    den = a_re * a_re + a_im * a_im
    f_re = ((ab_re - 1.0) * a_re + ab_im * a_im) / den
    f_im = (ab_im * a_re - (ab_re - 1.0) * a_im) / den
    b_re = b_re.astype(f32)
    b_im = b_im.astype(f32)
    bb_re = f_re[..., None] * b_re - f_im[..., None] * b_im
    bb_im = f_re[..., None] * b_im + f_im[..., None] * b_re
    bu_re = jnp.einsum('blgh,gph->blgp', u, bb_re)
    bu_im = jnp.einsum('blgh,gph->blgp', u, bb_im)
    shape_a = (1, seq, N_GROUPS, STATE)
    a_seq_re = jnp.broadcast_to(ab_re[None, None], shape_a)
    a_seq_im = jnp.broadcast_to(ab_im[None, None], shape_a)

    def combine(e1, e2):
        a1r, a1i, b1r, b1i = e1
        a2r, a2i, b2r, b2i = e2
        return (a2r * a1r - a2i * a1i,
                a2r * a1i + a2i * a1r,
                a2r * b1r - a2i * b1i + b2r,
                a2r * b1i + a2i * b1r + b2i)

    _, _, s_re, s_im = lax.associative_scan(
        combine, (a_seq_re, a_seq_im, bu_re, bu_im), axis=1)
    y = (jnp.einsum('blgp,ghp->blgh', s_re, c_re.astype(f32))
         - jnp.einsum('blgp,ghp->blgh', s_im, c_im.astype(f32))
         + d_skip.astype(f32) * u)
    y = jax.nn.gelu(y.reshape(bsz, seq, D_SSM)).astype(h.dtype)
    z = y @ w_glu
    return z[..., :D_MODEL] * jax.nn.sigmoid(z[..., D_MODEL:])

def stick_breaking_attention(h, w_q, k, v, w_o):
    bsz, seq, _ = h.shape
    scale = HEAD_DIM ** -0.5
    q = (h @ w_q).reshape(bsz, seq, N_HEADS, HEAD_DIM).transpose(0, 2, 1, 3) * scale
    outs = []
    for blk in range(seq // Q_BLOCK):
        t0 = blk * Q_BLOCK
        nk = t0 + Q_BLOCK
        qb = q[:, :, t0:nk]
        kb = k[:, :, :nk]
        vb = v[:, :, :nk]
        z = jnp.einsum('bhqd,bhkd->bhqk', qb, kb).astype(jnp.float32)
        t_idx = t0 + jnp.arange(Q_BLOCK)[:, None]
        s_idx = jnp.arange(nk)[None, :]
        causal = s_idx < t_idx
        log_beta = jax.nn.log_sigmoid(z)
        log_one_minus = jnp.where(causal, log_beta - z, 0.0)
        rem = lax.cumsum(log_one_minus, axis=3, reverse=True) - log_one_minus
        w = jnp.where(causal, jnp.exp(log_beta + rem), 0.0)
        outs.append(jnp.einsum('bhqk,bhkd->bhqd', w.astype(vb.dtype), vb))
    o = jnp.concatenate(outs, axis=2).transpose(0, 2, 1, 3).reshape(bsz, seq, D_ATT)
    return o @ w_o

def conv_ffn(h, w_up, conv_w, conv_b, w_down):
    gu = h @ w_up
    g = gu[..., :D_FF]
    u = gu[..., D_FF:]
    g = lax.conv_general_dilated(
        g, conv_w, window_strides=(1,), padding=[(CONV_W - 1, 0)],
        dimension_numbers=('NWC', 'WIO', 'NWC'), feature_group_count=D_FF) + conv_b
    return (jax.nn.silu(g) * u) @ w_down

def first_inputs(seed: int = 0) -> dict:
    key = jax.random.key(seed)
    ks = jax.random.split(key, 24)
    f32 = jnp.float32
    nrm = lambda k, shape, s: jax.random.normal(k, shape, f32) * s
    n_idx = jnp.arange(STATE, dtype=f32)
    return {
        "x": jax.random.normal(ks[0], (BATCH, SEQ, D_MODEL), f32),
        "norm_mix": 1.0 + nrm(ks[1], (DEPTH, D_MODEL), 0.02),
        "norm_ffn": 1.0 + nrm(ks[2], (DEPTH, D_MODEL), 0.02),
        "norm_kv": 1.0 + nrm(ks[3], (D_MODEL,), 0.02),
        "norm_final": 1.0 + nrm(ks[4], (D_MODEL,), 0.02),
        "ssm_w_in": nrm(ks[5], (N_A_LAYERS, D_MODEL, D_SSM), D_MODEL ** -0.5),
        "ssm_a_re": -0.5 * jnp.exp(nrm(ks[6], (N_A_LAYERS, N_GROUPS, STATE), 0.05)),
        "ssm_a_im": math.pi * n_idx + nrm(ks[7], (N_A_LAYERS, N_GROUPS, STATE), 0.01),
        "ssm_log_dt": jax.random.uniform(ks[8], (N_A_LAYERS, N_GROUPS), f32,
                                         minval=math.log(DT_MIN), maxval=math.log(DT_MAX)),
        "ssm_b_re": nrm(ks[9], (N_A_LAYERS, N_GROUPS, STATE, SSM_GROUP), (2 * SSM_GROUP) ** -0.5),
        "ssm_b_im": nrm(ks[10], (N_A_LAYERS, N_GROUPS, STATE, SSM_GROUP), (2 * SSM_GROUP) ** -0.5),
        "ssm_c_re": nrm(ks[11], (N_A_LAYERS, N_GROUPS, SSM_GROUP, STATE), (2 * STATE) ** -0.5),
        "ssm_c_im": nrm(ks[12], (N_A_LAYERS, N_GROUPS, SSM_GROUP, STATE), (2 * STATE) ** -0.5),
        "ssm_d": nrm(ks[13], (N_A_LAYERS, N_GROUPS, SSM_GROUP), 1.0),
        "ssm_w_glu": nrm(ks[14], (N_A_LAYERS, D_SSM, 2 * D_MODEL), D_SSM ** -0.5),
        "kv_w": nrm(ks[15], (D_MODEL, 2 * D_ATT), D_MODEL ** -0.5),
        "attn_w_q": nrm(ks[16], (N_B_LAYERS, D_MODEL, D_ATT), D_MODEL ** -0.5),
        "attn_w_o": nrm(ks[17], (N_B_LAYERS, D_ATT, D_MODEL), D_ATT ** -0.5),
        "ffn_w_up": nrm(ks[18], (DEPTH, D_MODEL, 2 * D_FF), D_MODEL ** -0.5),
        "ffn_conv_w": nrm(ks[19], (DEPTH, CONV_W, 1, D_FF), CONV_W ** -0.5),
        "ffn_conv_b": nrm(ks[20], (DEPTH, D_FF), 0.01),
        "ffn_w_down": nrm(ks[21], (DEPTH, D_FF, D_MODEL), D_FF ** -0.5),
    }

def first_block(x, norm_mix, norm_ffn, norm_kv, norm_final,
              ssm_w_in, ssm_a_re, ssm_a_im, ssm_log_dt, ssm_b_re, ssm_b_im,
              ssm_c_re, ssm_c_im, ssm_d, ssm_w_glu,
              kv_w, attn_w_q, attn_w_o,
              ffn_w_up, ffn_conv_w, ffn_conv_b, ffn_w_down):
    bsz, seq, _ = x.shape
    k_shared = None
    v_shared = None
    for layer in range(DEPTH):
        h = rms_norm(x, norm_mix[layer])
        if layer < N_A_LAYERS:
            x = x + s5_mixer(h, ssm_w_in[layer], ssm_a_re[layer], ssm_a_im[layer],
                             ssm_log_dt[layer], ssm_b_re[layer], ssm_b_im[layer],
                             ssm_c_re[layer], ssm_c_im[layer], ssm_d[layer],
                             ssm_w_glu[layer])
        else:
            j = layer - N_A_LAYERS
            x = x + stick_breaking_attention(h, attn_w_q[j], k_shared, v_shared, attn_w_o[j])
        x = x + conv_ffn(rms_norm(x, norm_ffn[layer]), ffn_w_up[layer],
                         ffn_conv_w[layer], ffn_conv_b[layer], ffn_w_down[layer])
        if layer == N_A_LAYERS - 1:
            kv = rms_norm(x, norm_kv) @ kv_w
            k_shared = kv[..., :D_ATT].reshape(bsz, seq, N_HEADS, HEAD_DIM).transpose(0, 2, 1, 3)
            v_shared = kv[..., D_ATT:].reshape(bsz, seq, N_HEADS, HEAD_DIM).transpose(0, 2, 1, 3)
    return rms_norm(x, norm_final)


N_HEADS_A = 16
N_KV_A = 4
HEAD_DIM_A = 64
WINDOW = 128
N_HEADS_B = 8
KEY_DIM_B = 128
VAL_DIM_B = 128
CONV_K = 4
CHUNK = 64
NUM_BUCKETS = 32
MAX_DISTANCE = 128
DN_ALPHA = (2 * DEPTH) ** 0.25
DN_BETA = (8 * DEPTH) ** -0.25
LN_EPS = 1e-5
NORM_EPS = 1e-6
NEG_INF = -1e30

Q_A = N_HEADS_A * HEAD_DIM_A
KV_W = N_KV_A * HEAD_DIM_A
QK_B = N_HEADS_B * KEY_DIM_B
V_B = N_HEADS_B * VAL_DIM_B
CONV_CH = 2 * QK_B + V_B
SPLIT_SIZES = (Q_A, KV_W, KV_W, CONV_CH, N_HEADS_B, N_HEADS_B, V_B, 2 * D_MODEL)
N_IN = sum(SPLIT_SIZES)
SPLIT_POINTS = tuple(int(s) for s in np.cumsum(SPLIT_SIZES)[:-1])


def layernorm(x, g, b):
    xf = x.astype(jnp.float32)
    mu = xf.mean(-1, keepdims=True)
    var = jnp.square(xf - mu).mean(-1, keepdims=True)
    y = (xf - mu) * lax.rsqrt(var + LN_EPS) * g.astype(jnp.float32) + b.astype(jnp.float32)
    return y.astype(x.dtype)

def swiglu(x, w13, w2):
    gate, up = jnp.split(x @ w13, 2, axis=-1)
    return (jax.nn.silu(gate) * up) @ w2

def t5_bucket(rel):
    n = jnp.maximum(rel, 0)
    max_exact = NUM_BUCKETS // 2
    nf = jnp.maximum(n, 1).astype(jnp.float32)
    large = max_exact + (jnp.log(nf / max_exact) / math.log(MAX_DISTANCE / max_exact)
                         * (NUM_BUCKETS - max_exact)).astype(jnp.int32)
    large = jnp.minimum(large, NUM_BUCKETS - 1)
    return jnp.where(n < max_exact, n, large)

def band_rel():
    r = jnp.arange(WINDOW)[:, None]
    j = jnp.arange(2 * WINDOW)[None, :]
    return r + WINDOW - j

def sliding_window_attention(q, k, v, pos_bias, sink):
    b, l = q.shape[:2]
    nb = l // WINDOW
    grp = N_HEADS_A // N_KV_A
    qb = (q.astype(jnp.float32) * HEAD_DIM_A ** -0.5).reshape(b, nb, WINDOW, N_KV_A, grp, HEAD_DIM_A)
    kb = k.astype(jnp.float32).reshape(b, nb, WINDOW, N_KV_A, HEAD_DIM_A)
    vb = v.astype(jnp.float32).reshape(b, nb, WINDOW, N_KV_A, HEAD_DIM_A)

    def with_prev(t):
        prev = jnp.concatenate([jnp.zeros_like(t[:, :1]), t[:, :-1]], axis=1)
        return jnp.concatenate([prev, t], axis=2)

    kk, vv = with_prev(kb), with_prev(vb)
    rel = band_rel()
    in_band = (rel >= 0) & (rel < WINDOW)
    key_in_own_block = jnp.arange(2 * WINDOW) >= WINDOW
    bias = pos_bias.reshape(N_KV_A, grp, WINDOW, 2 * WINDOW)
    sk = sink.astype(jnp.float32).reshape(N_KV_A, grp, 1, 1)

    def one_block(args):
        qi, ki, vi, i = args
        s = jnp.einsum('bqkgd,bskd->bkgqs', qi, ki) + bias
        valid = in_band & ((i > 0) | key_in_own_block)
        s = jnp.where(valid, s, NEG_INF)
        m = jnp.maximum(s.max(-1, keepdims=True), sk)
        p = jnp.exp(s - m)
        p = p / (p.sum(-1, keepdims=True) + jnp.exp(sk - m))
        return jnp.einsum('bkgqs,bskd->bqkgd', p, vi)

    o = lax.map(one_block, (jnp.moveaxis(qb, 1, 0), jnp.moveaxis(kk, 1, 0),
                            jnp.moveaxis(vv, 1, 0), jnp.arange(nb)))
    return jnp.moveaxis(o, 0, 1).reshape(b, l, Q_A)

def causal_depthwise_conv(u, w):
    return lax.conv_general_dilated(u, w[:, None, :].astype(u.dtype), window_strides=(1,),
                                    padding=[(CONV_K - 1, 0)],
                                    dimension_numbers=('NWC', 'WIO', 'NWC'),
                                    feature_group_count=u.shape[-1])

def l2norm(t):
    t = t.astype(jnp.float32)
    return t * lax.rsqrt(jnp.sum(t * t, -1, keepdims=True) + NORM_EPS)

def gated_delta_rule(q, k, v, g, beta):
    b, l, h, dk = q.shape
    dv = v.shape[-1]
    n = l // CHUNK

    def chunked(t):
        return t.reshape(b, n, CHUNK, h, t.shape[-1]).transpose(0, 3, 1, 2, 4)

    q = chunked(q * dk ** -0.5)
    k = chunked(k)
    v = chunked(v)
    g = jnp.cumsum(g.reshape(b, n, CHUNK, h).transpose(0, 3, 1, 2), axis=-1)
    beta = beta.reshape(b, n, CHUNK, h).transpose(0, 3, 1, 2)[..., None]
    kb, vb = k * beta, v * beta

    causal = jnp.tril(jnp.ones((CHUNK, CHUNK), bool))
    strict = jnp.tril(jnp.ones((CHUNK, CHUNK), bool), -1)
    decay = jnp.exp(jnp.where(causal, g[..., :, None] - g[..., None, :], NEG_INF))
    lower = jnp.where(strict, jnp.einsum('bhncd,bhnmd->bhncm', kb, k) * decay, 0.0)
    eye = jnp.eye(CHUNK, dtype=jnp.float32)
    t_inv = lax.linalg.triangular_solve(lower + eye, jnp.broadcast_to(eye, lower.shape),
                                        left_side=True, lower=True, unit_diagonal=True)
    u = t_inv @ vb
    w = t_inv @ (kb * jnp.exp(g)[..., None])
    a_intra = jnp.where(causal, jnp.einsum('bhncd,bhnmd->bhncm', q, k) * decay, 0.0)
    g_last = g[..., -1]
    k_tail = k * jnp.exp(g_last[..., None] - g)[..., None]
    q_dec = q * jnp.exp(g)[..., None]

    def step(s, xs):
        qd, kt, uc, wc, ac, gl = xs
        v_new = uc - jnp.einsum('bhcd,bhde->bhce', wc, s)
        o = jnp.einsum('bhcd,bhde->bhce', qd, s) + jnp.einsum('bhcm,bhme->bhce', ac, v_new)
        s = s * jnp.exp(gl)[..., None, None] + jnp.einsum('bhcd,bhce->bhde', kt, v_new)
        return s, o

    xs = tuple(jnp.moveaxis(t, 2, 0) for t in (q_dec, k_tail, u, w, a_intra, g_last))
    s0 = jnp.zeros((b, h, dk, dv), jnp.float32)
    _, o = lax.scan(step, s0, xs)
    return o.transpose(1, 0, 3, 2, 4).reshape(b, l, h, dv)

def hybrid_mixer(x, w_in, conv_w, a_log, dt_bias, dn_norm_g, sink,
                 w_branch_a, w_branch_b, w_out, pos_bias):
    b, l, _ = x.shape
    hcat = x @ w_in
    qa, ka, va, qkv_b, beta_raw, dt_raw, z, gate_raw = jnp.split(hcat, SPLIT_POINTS, axis=-1)

    ya = sliding_window_attention(qa.reshape(b, l, N_HEADS_A, HEAD_DIM_A),
                                  ka.reshape(b, l, N_KV_A, HEAD_DIM_A),
                                  va.reshape(b, l, N_KV_A, HEAD_DIM_A), pos_bias, sink)
    ya = ya.astype(x.dtype) @ w_branch_a

    qkv_b = jax.nn.silu(causal_depthwise_conv(qkv_b, conv_w))
    qb, kb, vb = jnp.split(qkv_b, (QK_B, 2 * QK_B), axis=-1)
    qb = l2norm(qb.reshape(b, l, N_HEADS_B, KEY_DIM_B))
    kb = l2norm(kb.reshape(b, l, N_HEADS_B, KEY_DIM_B))
    vb = vb.reshape(b, l, N_HEADS_B, VAL_DIM_B).astype(jnp.float32)
    beta = jax.nn.sigmoid(beta_raw.astype(jnp.float32))
    g = -jnp.exp(a_log.astype(jnp.float32)) * jax.nn.softplus(
        dt_raw.astype(jnp.float32) + dt_bias.astype(jnp.float32))
    o = gated_delta_rule(qb, kb, vb, g, beta)
    o = (o * lax.rsqrt(jnp.mean(o * o, -1, keepdims=True) + NORM_EPS)
         * dn_norm_g.astype(jnp.float32)
         * jax.nn.silu(z.reshape(b, l, N_HEADS_B, VAL_DIM_B).astype(jnp.float32)))
    yb = o.reshape(b, l, V_B).astype(x.dtype) @ w_branch_b

    gate_a, gate_b = jnp.split(jax.nn.sigmoid(gate_raw), 2, axis=-1)
    return (gate_a * ya + gate_b * yb) @ w_out

def second_inputs(seed: int = 0) -> dict:
    key = jax.random.key(seed)
    ks = jax.random.split(key, 16)
    f32 = jnp.float32

    def nrm(k, shape, scale):
        return jax.random.normal(k, shape, f32) * scale

    dt = jnp.exp(jax.random.uniform(ks[9], (DEPTH, N_HEADS_B), f32, math.log(1e-3), math.log(1e-1)))
    return {
        "x": nrm(ks[0], (BATCH, SEQ, D_MODEL), 1.0),
        "rel_bias": nrm(ks[1], (NUM_BUCKETS, N_HEADS_A), 0.5),
        "ln_g": 1.0 + nrm(ks[2], (DEPTH, 3, D_MODEL), 0.05),
        "ln_b": nrm(ks[3], (DEPTH, 3, D_MODEL), 0.02),
        "ffn_w13": nrm(ks[4], (DEPTH, 2, D_MODEL, 2 * D_FF), D_MODEL ** -0.5),
        "ffn_w2": nrm(ks[5], (DEPTH, 2, D_FF, D_MODEL), DN_BETA * D_FF ** -0.5),
        "w_in": nrm(ks[6], (DEPTH, D_MODEL, N_IN), D_MODEL ** -0.5),
        "conv_w": nrm(ks[7], (DEPTH, CONV_K, CONV_CH), CONV_K ** -0.5),
        "a_log": jnp.log(jax.random.uniform(ks[8], (DEPTH, N_HEADS_B), f32, 1.0, 16.0)),
        "dt_bias": dt + jnp.log(-jnp.expm1(-dt)),
        "dn_norm_g": 1.0 + nrm(ks[10], (DEPTH, VAL_DIM_B), 0.05),
        "sinks": nrm(ks[11], (DEPTH, N_HEADS_A), 0.5),
        "w_branch_a": nrm(ks[12], (DEPTH, Q_A, D_MODEL), Q_A ** -0.5),
        "w_branch_b": nrm(ks[13], (DEPTH, V_B, D_MODEL), V_B ** -0.5),
        "w_out": nrm(ks[14], (DEPTH, D_MODEL, D_MODEL), DN_BETA * D_MODEL ** -0.5),
    }

def second_block(x, rel_bias, ln_g, ln_b, ffn_w13, ffn_w2, w_in, conv_w, a_log, dt_bias,
              dn_norm_g, sinks, w_branch_a, w_branch_b, w_out):
    pos_bias = jnp.transpose(rel_bias[t5_bucket(band_rel())], (2, 0, 1)).astype(jnp.float32)
    for i in range(DEPTH):
        x = layernorm(DN_ALPHA * x + 0.5 * swiglu(x, ffn_w13[i, 0], ffn_w2[i, 0]), ln_g[i, 0], ln_b[i, 0])
        y = hybrid_mixer(x, w_in[i], conv_w[i], a_log[i], dt_bias[i], dn_norm_g[i], sinks[i],
                         w_branch_a[i], w_branch_b[i], w_out[i], pos_bias)
        x = layernorm(DN_ALPHA * x + y, ln_g[i, 1], ln_b[i, 1])
        x = layernorm(DN_ALPHA * x + 0.5 * swiglu(x, ffn_w13[i, 1], ffn_w2[i, 1]), ln_g[i, 2], ln_b[i, 2])
    return x


def setup_inputs(seed=0):
    out = dict(first_inputs(seed))
    for name, value in second_inputs(seed + 1).items():
        if name != "x":
            out[name + "_2"] = value
    return out


def reference(
    x, norm_mix, norm_ffn, norm_kv, norm_final, ssm_w_in, ssm_a_re, ssm_a_im, ssm_log_dt,
    ssm_b_re, ssm_b_im, ssm_c_re, ssm_c_im, ssm_d, ssm_w_glu, kv_w, attn_w_q, attn_w_o,
    ffn_w_up, ffn_conv_w, ffn_conv_b, ffn_w_down, rel_bias_2, ln_g_2, ln_b_2, ffn_w13_2,
    ffn_w2_2, w_in_2, conv_w_2, a_log_2, dt_bias_2, dn_norm_g_2, sinks_2, w_branch_a_2,
    w_branch_b_2, w_out_2,
):
    x = first_block(
        x, norm_mix, norm_ffn, norm_kv, norm_final, ssm_w_in, ssm_a_re, ssm_a_im, ssm_log_dt,
        ssm_b_re, ssm_b_im, ssm_c_re, ssm_c_im, ssm_d, ssm_w_glu, kv_w, attn_w_q, attn_w_o,
        ffn_w_up, ffn_conv_w, ffn_conv_b, ffn_w_down,
    )
    return second_block(
        x, rel_bias_2, ln_g_2, ln_b_2, ffn_w13_2, ffn_w2_2, w_in_2, conv_w_2, a_log_2,
        dt_bias_2, dn_norm_g_2, sinks_2, w_branch_a_2, w_branch_b_2, w_out_2,
    )


_drawn_inputs = setup_inputs


def setup_inputs(seed=0):
    import zlib

    import numpy as np

    out = dict(_drawn_inputs(seed))
    spreads = {}
    factors = {'norm_mix': 5.139,
     'norm_ffn': 2.668,
     'norm_kv': 5.112,
     'norm_final': 2.723,
     'ssm_a_re': 8.0,
     'ssm_b_re': 3.231,
     'ssm_b_im': 3.204,
     'ssm_c_re': 3.255,
     'ssm_c_im': 3.207,
     'ffn_conv_b': 7.917,
     'dn_norm_g_2': 6.942,
     'sinks_2': 8.0,
     'rel_bias_2': 3.131}
    for name, (base, spread) in spreads.items():
        noise = np.random.default_rng([zlib.crc32(name.encode()), seed]).standard_normal(out[name].shape)
        drawn = base * np.exp(spread * noise) if base else spread * noise
        out[name] = __import__('jax').numpy.asarray(drawn.astype(out[name].dtype))
    for name, factor in factors.items():
        out[name] = (out[name] * factor).astype(out[name].dtype)
    return out
```

```python
import math
from contextlib import ExitStack

import numpy as np

import concourse.bass as bass
from concourse import mybir

F32 = mybir.dt.float32
F32R = mybir.dt.float32r
ALU = mybir.AluOpType
ACT = mybir.ActivationFunctionType
AX_X = mybir.AxisListType.X

P = 128
SEQ = 256
D = 1024
KT = D // P
TT = SEQ // P
D_FF = 2816
FT = D_FF // P
DEPTH = 2
EPS = 1e-6
LN_EPS = 1e-5
NORM_EPS = 1e-6
ALPHA = (2 * DEPTH) ** 0.25
NEG_INF = -1e30
GROUPS, GH, ST = 64, 16, 64
PAIRS = GROUPS // 2
Q = 8
NC_ = SEQ // Q
HEADS, HD = 16, 64
KV_HEADS = 4
DH, DK = 8, 128
CONV_T = 3 * DH
LEVELS = 7
N_IN = 7696
BUCKETS = 32

PK, PN = 4, 512
RAW, SPL = 2, 3

TWO_PI = 2 * math.pi
MAGIC = 1.5 * 2 ** 23


def two_pi_parts():
    c1 = float(np.float32(6.28125))
    c2 = float(np.float32(round((TWO_PI - c1) * 2 ** 22) / 2 ** 22))
    return c1, c2, TWO_PI - c1 - c2


C_ID, C_LE, C_LT, C_GT, C_ONE = (i * P for i in range(5))
C_LVL = 5 * P
C_PAIR = C_LVL + LEVELS * P
C_NEGU = C_PAIR + 8
C_NEGL = C_NEGU + P
C_EPS = C_NEGL + P
N_CONST = C_EPS + 1


def constants():
    i, j = np.arange(P)[:, None], np.arange(P)[None, :]
    c = np.zeros((P, N_CONST), np.float32)
    c[:, C_ID:C_ID + P] = i == j
    c[:, C_LE:C_LE + P] = i <= j
    c[:, C_LT:C_LT + P] = i < j
    c[:, C_GT:C_GT + P] = i > j
    c[:, C_ONE:C_ONE + P] = 1
    for lv in range(LEVELS):
        b = 1 << lv
        c[:, C_LVL + lv * P:C_LVL + (lv + 1) * P] = (i // (2 * b) == j // (2 * b)) & (i // b % 2 == 1) & (j // b % 2 == 0)
    c[:, C_PAIR:C_PAIR + 8] = i // GH == np.arange(8)[None, :]
    c[:, C_NEGU:C_NEGU + P] = np.where(j > i, NEG_INF, 0)
    c[:, C_NEGL:C_NEGL + P] = np.where(j <= i, NEG_INF, 0)
    c[:, C_EPS] = NORM_EPS
    return c


def bucket_pattern():
    n = np.arange(P)
    exact = BUCKETS // 2
    nf = np.maximum(n, 1).astype(np.float32)
    large = exact + (np.log(nf / np.float32(exact)) / np.float32(math.log(P / exact)) * np.float32(BUCKETS - exact)).astype(np.int32)
    b = np.where(n < exact, n, np.minimum(large, BUCKETS - 1))
    return (np.arange(BUCKETS)[:, None] == b[::-1][None, :]).astype(np.float32)


def plan():
    panels, gemms = [], {}

    def add(name, w, index, ktiles, columns):
        cols = []
        for c0, c1 in columns:
            ps = []
            for k0 in range(0, ktiles, PK):
                ps.append(len(panels))
                panels.append((w, index, k0, min(PK, ktiles - k0), (c0, c1)))
            cols.append(ps)
        gemms[name] = cols

    def straight(n, start=0):
        return [(start + c, start + c + PN // 2) for c in range(0, n, PN)]

    def paired(n):
        return [(c, n + c) for c in range(0, n, PN // 2)]

    def ffn(f, up, down, index):
        add(f"up{f}", up, index, KT, paired(D_FF))
        add(f"down{f}", down, index, FT, straight(D))

    add("ssm_in", "ssm_w_in", (0,), KT, straight(D))
    add("glu", "ssm_w_glu", (0,), KT, paired(D))
    ffn(0, "ffn_w_up", "ffn_w_down", (0,))
    add("kv", "kv_w", (), KT, straight(2 * D))
    add("q", "attn_w_q", (0,), KT, straight(D))
    add("o", "attn_w_o", (0,), KT, straight(D))
    ffn(1, "ffn_w_up", "ffn_w_down", (1,))
    for i in range(DEPTH):
        ffn(2 + 2 * i, "ffn_w13_2", "ffn_w2_2", (i, 0))
        add(f"win{i}", "w_in_2", (i,), KT, straight(1536 + 3072) + straight(3072, 4624))
        add(f"brA{i}", "w_branch_a_2", (i,), KT, straight(D))
        add(f"brB{i}", "w_branch_b_2", (i,), KT, straight(D))
        add(f"wo{i}", "w_out_2", (i,), KT, straight(D))
        ffn(3 + 2 * i, "ffn_w13_2", "ffn_w2_2", (i, 1))
    return panels, gemms


COLUMN_TILES = [
    [("norm_mix", 16), ("norm_ffn", 16), ("norm_kv", 8), ("ssm_d", 8), ("ln_g_2", 48), ("norm_final", 8)],
    [("ln_b_2", 48), ("ffn_conv_b", 44)],
    [("ffn_conv_w", 66, 0)],
    [("ffn_conv_w", 66, 66)],
    [("conv_w_2", 96, 0)],
    [("conv_w_2", 96, 96)],
]

def build(nc, T, out):
    panels, gemms = plan()
    n_panels = len(panels)

    es = ExitStack()
    with es:
        def sb(name, shape, dt=F32, stack=es):
            return stack.enter_context(nc.sbuf_tensor(name, shape, dt))

        sems = {}

        def sem(name):
            if name not in sems:
                sems[name] = es.enter_context(nc.semaphore(name))
            return sems[name]

        raw = sb("raw", [P, RAW, PK, PN])
        w_hi = sb("w_hi", [P, SPL, PK, PN], F32R)
        w_lo = sb("w_lo", [P, SPL, PK, PN], F32R)
        xT_hi = sb("xT_hi", [P, KT, SEQ], F32R)
        xT_lo = sb("xT_lo", [P, KT, SEQ], F32R)
        x = sb("x", [P, TT, D])
        xn = sb("xn", [P, TT, D])
        cst = sb("cst", [P, N_CONST])
        cols = sb("cols", [P, 6, 104])
        bdw_hi = sb("bdw_hi", [P, DEPTH, KT, 16], F32R)
        bdw_lo = sb("bdw_lo", [P, DEPTH, KT, 16], F32R)
        stat = sb("stat", [P, TT, 2, 6])
        mv = sb("mv", [P, TT, 2])
        nrm = sb("nrm", [P, 4, TT])
        row = sb("row", [P, DEPTH, 2, 8])
        snk = sb("snk", [P, DEPTH, HEADS])
        dng = sb("dng", [P, DEPTH, DK])

        def const(at, n=P):
            return cst[:, at:at + n]

        ident = const(C_ID)

        gb = sb("gb", [P, 2, D])
        tb = sb("tb", [P, 2, SEQ])

        s1 = ExitStack()
        uT = sb("uT", [P, KT, SEQ], F32, s1)
        Bm = sb("Bm", [P, 2, PAIRS, 32], F32, s1)
        pT = sb("pT", [P, 9, PAIRS], F32, s1)
        tmpv = sb("tmpv", [P, 2, 1024], F32, s1)
        CT = sb("CT", [P, 2, PAIRS, GH], F32, s1)
        tmpp = sb("tmpp", [P, 2, 2, 4, NC_], F32, s1)
        s1a = ExitStack()
        bsel = sb("bsel", [BUCKETS, P], F32, s1a)
        relb = sb("relb", [BUCKETS, HEADS], F32, s1a)
        ftab = sb("ftab", [HEADS, P], F32, s1a)
        stage = sb("stage", [P, 6, P], F32, s1a)
        bdw = sb("bdw", [P, DEPTH, KT, 16], F32, s1a)
        c_n = sb("c_n", [P, 2, 8, 2, ST], F32, s1a)
        b_n = sb("b_n", [P, 2, PAIRS, GH], F32, s1a)
        BT = sb("BT", [P, 8, 2, P], F32, s1a)
        pn = sb("pn", [PAIRS, 20, P], F32, s1a)
        bu = sb("bu", [P, 2, 2, 4, SEQ], F32, s1a)
        s1a.close()
        s1b = ExitStack()
        CA = sb("CA", [P, Q, 2, PAIRS, GH], F32, s1b)
        CAm = sb("CAm", [P, 2, 2, Q, 4, 32], F32, s1b)
        Kbd = sb("Kbd", [P, 2, Q, P], F32, s1b)
        s1b.close()
        s1.close()
        E = xn[:, :, :].rearrange("p t (k c) -> p t k c", c=NC_)
        V = gb[:, :, :].rearrange("p t (k c) -> p t k c", c=NC_)

        s2 = ExitStack()
        hT_hi = sb("hT_hi", [P, FT, SEQ], F32R, s2)
        hT_lo = sb("hT_lo", [P, FT, SEQ], F32R, s2)
        hbuf = sb("hbuf", [P, 2, 2, SEQ], F32, s2)
        s2.close()

        s3 = ExitStack()
        kT = sb("kT", [P, KT, SEQ], F32, s3)
        qT = sb("qT", [P, KT, SEQ], F32, s3)
        vn_ = sb("vnat", [P, TT, D], F32, s3)
        SW = 3 * P
        zS = sb("zS", [P, HEADS, SW], F32, s3)
        spS = sb("spS", [P, HEADS, SW], F32, s3)
        s3.close()

        s4 = ExitStack()
        qkT = sb("qkT", [P, CONV_T, SEQ], F32, s4)
        sz = sb("sz", [P, TT, D], F32, s4)
        gates = sb("gates", [P, TT, 2, D], F32, s4)
        sm = sb("sm", [P, 12, TT, 8], F32, s4)
        s4a = ExitStack()
        qaT = sb("qaT", [P, KT, SEQ], F32, s4a)
        kaT = sb("kaT", [P, KV_HEADS, SEQ], F32, s4a)
        va = sb("va", [P, TT, 256], F32, s4a)
        biasL = sb("biasL", [P, HEADS, P], F32, s4a)
        biasU = sb("biasU", [P, HEADS, P], F32, s4a)
        zA = sb("zA", [P, 2, 2, 2, P], F32, s4a)
        zB = sb("zB", [P, 2, 2, P], F32, s4a)
        pT3 = sb("pT3", [P, 2, 3, P], F32, s4a)
        red = sb("red", [P, 4, 4], F32, s4a)
        s4a.close()
        s4b = ExitStack()
        L = sb("L", [P, TT, 8, P], F32, s4b)
        AT = sb("AT", [P, TT, 8, P], F32, s4b)
        Ti = sb("Ti", [P, TT, 8, P], F32, s4b)
        U = sb("U", [P, TT, 8, P], F32, s4b)
        kbg = sb("kbg", [P, 8, P], F32, s4b)
        ktl = sb("ktl", [P, 8, P], F32, s4b)
        s4b.close()
        s4.close()
        vb = xn[:, :, :].rearrange("p t (h d) -> p t h d", d=DK)
        qh, kh, vh = qkT[:, 0:8], qkT[:, 8:16], qkT[:, 16:24]
        Xm = kh.rearrange("p a b -> p (a b)").rearrange("p (t h m) -> p t h m", t=TT, h=8)
        Yp = vh.rearrange("p a b -> p (a b)").rearrange("p (t h m) -> p t h m", t=TT, h=8)

        acc = [es.enter_context(nc.psum_tensor(f"acc{i}", [P, 1024], F32)) for i in range(2)]
        trp = [es.enter_context(nc.psum_tensor(f"trp{i}", [P, 512], F32)) for i in range(2)]

        ftab_d = nc.dram_tensor("ftab_d", (HEADS, P, P), F32, kind="Internal").ap()

        raw_loaded = [sem(f"raw_loaded{i}") for i in range(RAW)]
        hi_ready, lo_ready, panel_used = sem("hi_ready"), sem("lo_ready"), sem("panel_used")
        acc_ready = sem("acc_ready")
        acc_freed = [sem("acc_freed0"), sem("acc_freed1")]

        use, filled = {}, {}
        n_use = n_fill = 0

        def uses(name, count, gemm=None):
            nonlocal n_use, n_fill
            use[name] = n_use
            for j in range(count):
                if gemm:
                    filled[n_use] = (panel_used, gemms[gemm][j][-1] + 1)
                else:
                    n_fill += 1
                    filled[n_use] = (acc_ready, n_fill)
                n_use += 1

        def gemm_uses(name):
            uses(name, len(gemms[name]), name)

        uses("cols", 1)
        uses("CT", 2)
        uses("ftab", 1)
        gemm_uses("ssm_in")
        uses("pT", 1)
        uses("BT", 2)
        uses("bu", 16)
        uses("K0", 1)
        for f in range(8):
            if f < 7:
                uses(f"K{f + 1}", 1)
            uses(f"y{f}", 1)
        gemm_uses("glu")
        gemm_uses("up0"), gemm_uses("down0")
        gemm_uses("kv"), gemm_uses("q")
        uses("z", 8), uses("rem", 8), uses("oT", 2)
        gemm_uses("o")
        gemm_uses("up1"), gemm_uses("down1")
        for i in range(DEPTH):
            gemm_uses(f"up{2 + 2 * i}"), gemm_uses(f"down{2 + 2 * i}")
            gemm_uses(f"win{i}")
            uses(f"bd{i}", 1)
            for n in range(8 + 2):
                if n < 8:
                    uses(f"s{i}_{n}", 1)
                if n >= 2:
                    uses(f"oa{i}_{n - 2}", 1)
            gemm_uses(f"brA{i}")
            uses(f"G{i}", 1), uses(f"Gr{i}", 2), uses(f"ss{i}", 4), uses(f"nat{i}", 4), uses(f"kk{i}", 2), uses(f"qk{i}", 2)
            for lv in range(LEVELS):
                uses(f"Y{i}_{lv}", 2)
                for t in range(TT):
                    uses(f"ZU{i}_{lv}_{t}", 1)
                    if lv < LEVELS - 1:
                        uses(f"ZT{i}_{lv}_{t}", 1)
            uses(f"dl{i}", 7)
            gemm_uses(f"brB{i}"), gemm_uses(f"wo{i}")
            gemm_uses(f"up{3 + 2 * i}"), gemm_uses(f"down{3 + 2 * i}")

        def wait_filled(eng, u):
            eng.wait_ge(*filled[u])

        def freed(u):
            return acc_freed[u % 2], 1

        tsplits = {}

        def tsplit_no(name):
            if name not in tsplits:
                tsplits[name] = len(tsplits)
            return tsplits[name]

        for name in ["mix0", "ffn0", "kv", "mix1", "ffn1", "final"]:
            tsplit_no(name)
        for i in range(DEPTH):
            for name in ["ln0", "delta", "mixed", "ln1"] + ["ln2"] * (i < DEPTH - 1):
                tsplit_no(f"{name}_{i}")
        norms = {n: i for i, n in enumerate(
            ["mix0", "ffn0", "kv", "ffn1", "final"] + [f"ln{j}_{i}" for i in range(DEPTH) for j in range(3)])}
        naturals = {n: i for i, n in enumerate(["final"] + [f"ln{j}_{i}" for i in range(DEPTH) for j in range(3)])}

        def gain_of(name):
            c0, c1 = cols[:, 0, :], cols[:, 1, :]
            if name.startswith("ln"):
                j, i = int(name[2]), int(name[4])
                at = (i * 3 + j) * 8
                return c0[:, 48 + at:48 + at + 8], c1[:, at:at + 8]
            at = {"mix0": 0, "mix1": 8, "ffn0": 16, "ffn1": 24, "kv": 32, "final": 96}[name]
            return c0[:, at:at + 8], None

        def A4(u, f=4):
            return acc[u % 2][:, :].rearrange("p (n t) -> p n t", n=f)

        def A2(u):
            return acc[u % 2][:, :].rearrange("p (t n) -> p t n", t=2)

        def A8(u):
            return acc[u % 2][:, :].rearrange("p (h m) -> p h m", h=8)

        def bc(ap, axis, n):
            a = ap.unsqueeze(axis)
            shape = list(a.shape)
            shape[axis] = n
            return a.to_broadcast(shape)

        class Steps:

            def __init__(self, eng, name):
                self.eng, self.sem, self.n = eng, sem(name), 0

            def __call__(self, ins):
                ins.then_inc(self.sem, 1)
                self.n += 1

            def settle(self):
                self.eng.wait_ge(self.sem, self.n)

        def wait_evacuated(eng, u):
            eng.wait_ge(acc_freed[u % 2], u // 2 + 1)

        def horner(eng, ops, step, tmp, odd):
            done = sem("chunks_odd" if odd else "chunks_even")
            for n in range(4):
                b = 2 * n + odd
                k = slice(4 * b, 4 * b + 4)
                eng.wait_ge(sem("bu_odd" if odd else "bu_even"), 4 * (n + 1))
                v = V[:, :, k, :]
                u = bu[:, odd].rearrange("p r k (c j) -> p r k c j", j=Q)
                t1, t2 = tmp[:, 0], tmp[:, 1]
                for j in range(1, Q):
                    src = u[:, :, :, :, 0] if j == 1 else v
                    step(ops.tensor_tensor(t1, src, bc(bc(pT[:, 0, k], 1, 2), 3, NC_), ALU.mult))
                    for r in range(2):
                        step(ops.tensor_tensor(t2[:, r], src[:, 1 - r], bc(pT[:, 1 + r, k], 2, NC_), ALU.mult))
                    step.settle()
                    step(ops.tensor_tensor(t1, t1, t2, ALU.add))
                    step.settle()
                    ins = ops.tensor_tensor(v, t1, u[:, :, :, :, j], ALU.add)
                    if j < Q - 1:
                        step(ins)
                        step.settle()
                    else:
                        ins.then_inc(done, 1)
            eng.wait_ge(done, 4)

        def s_(i):
            return pn[:, i, :]

        block = es.enter_context(nc.Block())

        @block.sync
        def _(sp):
            sp.dma_start(x[:, :, :], T["x"][0].rearrange("(t p) d -> p t d", p=P)).then_inc(sem("x_in"), 16)
            for p, (w, index, k0, kt, (c0, c1)) in enumerate(panels):
                if p >= n_panels:
                    break
                src = T[w]
                for i in index:
                    src = src[i]
                src = src[k0 * P:(k0 + kt) * P, :].rearrange("(k p) n -> p k n", p=P)
                if p >= RAW:
                    sp.wait_ge(lo_ready, p - RAW + 1)
                slot, half = raw[:, p % RAW, 0:kt, :], PN // 2
                if c1 == c0 + half:
                    sp.dma_start(slot, src[:, :, c0:c0 + PN]).then_inc(raw_loaded[p % RAW], 32)
                else:
                    sp.dma_start(slot[:, :, 0:half], src[:, :, c0:c0 + half]).then_inc(raw_loaded[p % RAW], 16)
                    sp.dma_start(slot[:, :, half:PN], src[:, :, c1:c1 + half]).then_inc(raw_loaded[p % RAW], 16)
            sp.wait_ge(sem("out_ready"), 1)
            sp.dma_start(out[0].rearrange("(t p) d -> p t d", p=P), x[:, :, :]).then_inc(sem("out_stored"), 16)
            sp.wait_ge(sem("out_stored"), 16)

        @block.gpsimd
        def _(pool):
            step = Steps(pool, "pool_steps")
            tt = nc.gpsimd.tensor_tensor
            ts = nc.gpsimd.tensor_scalar

            def s(i):
                return pn[:, i, :]

            def do(ins):
                step(ins)
                step.settle()

            step(nc.gpsimd.memset(Bm[:, :, :, :], 0.0))
            pool.wait_ge(sem("dt_ready"), 1)
            pool.wait_ge(sem("ssm_a_in"), 48)
            dt = bc(pn[:, 12, 2:4], 2, ST)

            def halves(i):
                return s(i).rearrange("k (a p) -> k a p", a=2)

            step(tt(halves(13), halves(9), dt, ALU.mult))
            do(tt(halves(14), halves(10), dt, ALU.mult))
            pool.wait_ge(step.sem, step.n)
            nc.gpsimd.tensor_copy(s(19), s(13)).then_inc(sem("mag_in"), 1)
            do(ts(s(15), s(14), 1 / TWO_PI, MAGIC, ALU.mult, ALU.add))
            do(ts(s(15), s(15), -MAGIC, None, ALU.add))
            for part in two_pi_parts():
                do(ts(s(16), s(15), -part, None, ALU.mult))
                do(tt(s(14), s(14), s(16), ALU.add))
            ts(s(14), s(14), 3.1415925, -3.1415925, ALU.min, ALU.max).then_inc(sem("angle_ready"), 1)
            pool.wait_ge(sem("trig_ready"), 3)
            do(tt(s(17), s(16), s(16), ALU.mult))
            do(ts(s(17), s(17), -2.0, 1.0, ALU.mult, ALU.add))
            step(tt(s(0), s(13), s(17), ALU.mult))
            do(tt(s(2), s(13), s(15), ALU.mult))
            step(ts(s(1), s(2), -1.0, None, ALU.mult))
            step(ts(s(3), s(2), -1.0, None, ALU.mult))
            step(tt(s(17), s(9), s(9), ALU.mult))
            do(tt(s(18), s(10), s(10), ALU.mult))
            tt(s(19), s(17), s(18), ALU.add).then_inc(sem("den_ready"), 1)
            pool.wait_ge(sem("den_ready"), 1)
            re, im = 0, 2
            for _ in range(int(math.log2(Q))):
                step(tt(s(17), s(re), s(re), ALU.mult))
                step(tt(s(18), s(im), s(im), ALU.mult))
                do(tt(s(16), s(re), s(im), ALU.mult))
                re, im = 4, 6
                step(tt(s(re), s(17), s(18), ALU.subtract))
                do(ts(s(im), s(16), 2.0, None, ALU.mult))
            step(ts(s(5), s(6), -1.0, None, ALU.mult))
            do(ts(s(16), s(0), -1.0, None, ALU.add))
            step(tt(s(13), s(16), s(9), ALU.mult))
            step(tt(s(14), s(2), s(10), ALU.mult))
            step(tt(s(17), s(2), s(9), ALU.mult))
            do(tt(s(18), s(16), s(10), ALU.mult))
            step(tt(s(13), s(13), s(14), ALU.add))
            do(tt(s(17), s(17), s(18), ALU.subtract))
            pool.wait_ge(sem("inv_ready"), 1)
            step(tt(s(7), s(13), s(19), ALU.mult))
            do(tt(s(8), s(17), s(19), ALU.mult))
            nc.gpsimd.tensor_copy(s(12), s(8)).then_inc(sem("powers_ready"), 1)

            pool.wait_ge(sem("pT_ready"), 1)
            horner(pool, nc.gpsimd, step, tmpp, 1)

            pool.wait_ge(sem("chunks_even"), 4)
            pool.wait_ge(sem("BT_ready"), 2)
            pool.wait_ge(sem("ftab_stored"), 16)
            step(nc.gpsimd.memset(CAm[:, :, :, :, :, :], 0.0))
            pool.wait_ge(sem("CT_ready"), 4)
            t1, t2 = (tmpv[:, i, :].rearrange("p (r k h) -> p r k h", r=2, h=GH) for i in range(2))
            for j in range(Q):
                prev = CA[:, j - 1] if j else CT[:, :, :, :]
                step(tt(t1, prev, bc(bc(pT[:, 0, :], 1, 2), 3, GH), ALU.mult))
                do(tt(t2, prev[:, ::-1], bc(pT[:, 2:4, :], 3, GH), ALU.mult))
                do(tt(CA[:, j], t1, t2, ALU.add))
            nc.gpsimd.tensor_copy(tmpv[:, 0, 0:1], CA[:, Q - 1, 0, 0, 0:1]).then_inc(sem("CA_ready"), 1)

            order = list(naturals)

            def load_gain(name):
                if name == "final":
                    pool.dma_start(gb[:, 0, :], T["norm_final"].partition_broadcast(P)).then_inc(sem("gain_in"), 32)
                else:
                    j, i = int(name[2]), int(name[4])
                    pool.dma_start(gb[:, 0, :], T["ln_g_2"][i, j].partition_broadcast(P)).then_inc(sem("gain_in"), 16)
                    pool.dma_start(gb[:, 1, :], T["ln_b_2"][i, j].partition_broadcast(P)).then_inc(sem("gain_in"), 16)

            def natural(name):
                n = naturals[name]
                pool.wait_ge(sem("gain_in"), 32 * (n + 1))
                pool.wait_ge(sem("xn_ready"), TT * (norms[name] + 1))
                for t in range(TT):
                    step(tt(x[:, t, :], xn[:, t, :], gb[:, 0, :], ALU.mult))
                step.settle()
                if name != "final":
                    for t in range(TT):
                        step(tt(x[:, t, :], x[:, t, :], gb[:, 1, :], ALU.add))
                    step.settle()
                pool.sem_inc(sem("xnat_ready"), 1)
                if n + 1 < len(order) :
                    load_gain(order[n + 1])

            pool.wait_ge(sem("scan_done"), 1)
            load_gain("final")
            natural("final")
            for i in range(DEPTH):
                natural(f"ln0_{i}")
                skew = bass.AP(ftab_d.tensor, P - 1, [[P - 1, P], [P * P, HEADS], [1, P]])
                pool.dma_start(biasL[:, :, :], skew).then_inc(sem("bias_in"), 16)
                pool.wait_ge(sem("bias_in"), 16 * (i + 1))
                do(tt(biasU[:, :, :], biasL[:, :, :], bc(const(C_NEGL), 1, HEADS), ALU.add))
                tt(biasL[:, :, :], biasL[:, :, :], bc(const(C_NEGU), 1, HEADS), ALU.add).then_inc(sem("bias_ready"), 1)
                pool.wait_ge(sem("z_gate"), 2 * (i + 1))
                szh = sz[:, :, :].rearrange("p t (h d) -> p (t h) d", d=DK)
                tt(szh, szh, bc(dng[:, i, :], 1, TT * DH), ALU.mult).then_inc(sem("sz_ready"), 1)
                for t in range(TT):
                    pool.wait_ge(sem("decay_exp"), 2 * (TT * i + t + 1))
                    tt(AT[:, t], AT[:, t], bc(const(C_LE), 1, DH), ALU.mult).then_inc(sem("decay_ready"), 1)
                    do(tt(L[:, t], L[:, t], bc(const(C_GT), 1, DH), ALU.mult))
                    tt(L[:, t], L[:, t], bc(sm[:, 0, t, :], 2, P), ALU.mult).then_inc(sem("decay_ready"), 1)
                for t in range(TT):
                    nc.gpsimd.tensor_copy(U[:, t], bc(ident, 1, DH)).then_inc(sem("inverse_init"), 1)
                    nc.gpsimd.tensor_copy(Ti[:, t], bc(ident, 1, DH)).then_inc(sem("inverse_init"), 1)
                for lv in range(LEVELS):
                    for t in range(TT):
                        if lv == 0:
                            wait_evacuated(pool, use[f"kk{i}"] + t)
                            wait_evacuated(pool, use[f"qk{i}"] + 1)
                        else:
                            wait_filled(pool, use[f"Y{i}_{lv - 1}"] + t)
                        tt(Xm[:, t], L[:, t], bc(const(C_LVL + lv * P), 1, DH), ALU.mult).then_inc(sem("Xm_ready"), 1)
                natural(f"ln1_{i}")
                natural(f"ln2_{i}")
            pool.sem_inc(sem("out_ready"), 1)

        @block.scalar
        def _(act):
            step = Steps(act, "act_steps")
            A = nc.scalar.activation

            act.dma_start(cst[:, :], T["const_masks"]).then_inc(sem("const_in"), 16)
            for i, parts in enumerate(COLUMN_TILES):
                at = 0
                for name, n, *first in parts:
                    src = T[name]
                    letters = "abcd"[:len(src.shape)]
                    src = src.rearrange(f"{' '.join(letters)} -> ({' '.join(letters)})").rearrange("(r c) -> r c", c=P)
                    first = first[0] if first else 0
                    act.dma_start(stage[at:at + n, i, :], src[first:first + n, :]).then_inc(sem("cols_in"), 16)
                    at += n
            act.dma_start(pn[:, 9, :], T["ssm_a_re"][0].rearrange("(k a) p -> k (a p)", a=2)).then_inc(sem("ssm_a_in"), 16)
            act.dma_start(pn[:, 10, :], T["ssm_a_im"][0].rearrange("(k a) p -> k (a p)", a=2)).then_inc(sem("ssm_a_in"), 16)
            act.dma_start(pn[:, 12, 0:2], T["ssm_log_dt"][0].rearrange("(k a) -> k a", a=2)).then_inc(sem("ssm_a_in"), 16)
            for r, name in enumerate(("ssm_c_re", "ssm_c_im")):
                for dup in range(2):
                    act.dma_start(c_n[:, r, :, dup, :], T[name][0].rearrange("(f q) h p -> (q h) f p", q=8)).then_inc(sem("ssm_c_in"), 16)
            for r, name in enumerate(("ssm_b_re", "ssm_b_im")):
                act.dma_start(b_n[:, r, :, :], T[name][0].rearrange("(k a) p h -> (a p) k h", a=2)).then_inc(sem("ssm_b_in"), 16)
            act.dma_start(bdw[:, :, :, :], T["w_in_2"][:, :, 4608:4624].rearrange("i (k p) n -> p i k n", p=P)).then_inc(sem("bdw_in"), 16)
            act.dma_start(relb[:, :], T["rel_bias_2"]).then_inc(sem("misc_in"), 16)
            act.dma_start(bsel[:, :], T["const_buckets"]).then_inc(sem("misc_in"), 16)
            act.dma_start(row[:, :, 0, :], T["a_log_2"].partition_broadcast(P)).then_inc(sem("misc_in"), 16)
            act.dma_start(row[:, :, 1, :], T["dt_bias_2"].partition_broadcast(P)).then_inc(sem("misc_in"), 16)
            act.dma_start(snk[:, :, :], T["sinks_2"].partition_broadcast(P)).then_inc(sem("misc_in"), 16)
            act.dma_start(dng[:, :, :], T["dn_norm_g_2"].partition_broadcast(P)).then_inc(sem("misc_in"), 16)

            def split_hi(p):
                if p >= n_panels:
                    return
                act.wait_ge(raw_loaded[p % RAW], 32 * (p // RAW + 1))
                if p >= SPL:
                    act.wait_ge(panel_used, p - SPL + 1)
                kt = panels[p][3]
                A(w_hi[:, p % SPL, 0:kt, :], raw[:, p % RAW, 0:kt, :], ACT.Copy).then_inc(hi_ready, 1)

            def gemm(name, evacuate, after=None):
                for j, ps in enumerate(gemms[name]):
                    for p in ps[:-1]:
                        split_hi(p + SPL)
                    evacuate(j, use[name] + j)
                    split_hi(ps[-1] + SPL)
                    if after:
                        after(j, use[name] + j)

            def root(name):
                act.wait_ge(sem("var_ready"), norms[name] + 1)
                A(nrm[:, 1, :], nrm[:, 0, :], ACT.Sqrt).then_inc(sem("std_ready"), 1)

            def tsplit(name, gain=None, bias=None):
                for g in range(4):
                    n = 4 * tsplits[name] + g
                    act.wait_ge(sem("turned"), n + 1)
                    tr = trp[n % 2][:, :].rearrange("p (k t) -> p k t", k=2)
                    if gain is None:
                        A(xT_hi[:, 2 * g:2 * g + 2, :], tr, ACT.Copy).then_inc(sem("xhi_ready"), 2)
                        continue
                    for k in range(2):
                        kk = 2 * g + k
                        if bias is None:
                            ins = A(xT_hi[:, kk, :], tr[:, k], ACT.Copy, scale=gain[:, kk:kk + 1])
                        else:
                            ins = A(xT_hi[:, kk, :], tr[:, k], ACT.Identity, scale=gain[:, kk:kk + 1], bias=bias[:, kk:kk + 1])
                        ins.then_inc(sem("xhi_ready"), 1)

            def ffn(f):
                def gate(j, u):
                    hn = f * 11 + j
                    if hn >= 2:
                        act.wait_ge(sem("hlo_ready"), hn - 1)
                    wait_filled(act, u)
                    h = hbuf[:, hn % 2]
                    if f < 2:
                        for n in range(2):
                            c = 2 * j + n
                            ins = A(h[:, n], A4(u)[:, n], ACT.Identity, scale=cols[:, 2 + f, 2 * FT + c:2 * FT + c + 1],
                                    bias=cols[:, 1, 48 + f * FT + c:48 + f * FT + c + 1])
                            ins.then_inc(sem("tap_ready"), 1)
                        act.wait_ge(sem("conv_ready"), 2 * hn + 2)
                        A(h, h, ACT.Silu).then_inc(sem("gate_ready"), 1)
                    else:
                        A(h, A4(u)[:, 0:2], ACT.Silu).then_inc(sem("gate_ready"), 1)

                def hidden(j, u):
                    wait_evacuated(act, u)
                    A(hT_hi[:, 2 * j:2 * j + 2, :], hbuf[:, (f * 11 + j) % 2], ACT.Copy).then_inc(sem("hhi_ready"), 1)

                gemm(f"up{f}", gate, hidden)
                gemm(f"down{f}", lambda j, u: None)

            for p in range(SPL):
                split_hi(p)
            u = use["cols"]
            wait_filled(act, u)
            for i, parts in enumerate(COLUMN_TILES):
                n = sum(q[1] for q in parts)
                ins = A(cols[:, i, 0:n], acc[u % 2][:, i * P:i * P + n], ACT.Copy)
                if i < 5:
                    step(ins)
            step.settle()
            ins.then_inc(*freed(u))
            wait_evacuated(act, u)
            root("mix0")
            tsplit("mix0", *gain_of("mix0"))
            for r in range(2):
                u = use["CT"] + r
                wait_filled(act, u)
                v = acc[u % 2][:, :].rearrange("p (f k a h) -> p f k a h", f=8, k=4, a=2)
                for a in range(2):
                    rows = slice(a * ST, a * ST + ST)
                    A(CT[rows, r].rearrange("p (f k) h -> p f k h", f=8), v[rows, :, :, a, :], ACT.Copy,
                      scale=-1.0 if r else 1.0).then_inc(sem("CT_ready"), 1)
                act.wait_ge(sem("CT_ready"), 2 * r + 2)
                A(tb[:, 0, 0:1], acc[u % 2][:, 0:1], ACT.Copy).then_inc(*freed(u))
            u = use["ftab"]
            wait_filled(act, u)
            A(ftab[:, :], acc[u % 2][0:HEADS, 0:P], ACT.Copy).then_inc(*freed(u))
            wait_evacuated(act, u)
            act.dma_start(ftab_d, bc(ftab[:, :], 1, P)).then_inc(sem("ftab_stored"), 16)
            act.wait_ge(sem("bdw_in"), 16)
            A(bdw_hi[:, :, :, :], bdw[:, :, :, :], ACT.Copy).then_inc(sem("bdw_hi_ready"), 1)

            act.wait_ge(sem("ssm_a_in"), 48)
            A(pn[:, 12, 2:4], pn[:, 12, 0:2], ACT.Exp).then_inc(sem("dt_ready"), 1)
            act.wait_ge(sem("mag_in"), 1)
            A(s_(13), s_(19), ACT.Exp).then_inc(sem("trig_ready"), 1)
            act.wait_ge(sem("angle_ready"), 1)
            A(s_(15), s_(14), ACT.Sin).then_inc(sem("trig_ready"), 1)
            A(s_(16), s_(14), ACT.Sin, scale=0.5).then_inc(sem("trig_ready"), 1)

            gemm("ssm_in", lambda j, u: (wait_filled(act, u), A(uT[:, 4 * j:4 * j + 4, :], A4(u), ACT.Copy).then_inc(*freed(u))))
            u = use["pT"]
            wait_filled(act, u)
            A(pT[:, :, :], acc[u % 2][:, 0:9 * PAIRS].rearrange("p (q k) -> p q k", q=9), ACT.Copy).then_inc(*freed(u))
            wait_evacuated(act, u)
            A(tb[:, 0, 0:1], pT[:, 0, 0:1], ACT.Copy).then_inc(sem("pT_ready"), 1)
            for j in range(2):
                u = use["BT"] + j
                wait_filled(act, u)
                A(BT[:, 4 * j:4 * j + 4].rearrange("p f r m -> p (f r m)"), acc[u % 2][:, :], ACT.Copy).then_inc(*freed(u))
                wait_evacuated(act, u)
                A(tb[:, 0, 0:1], BT[:, 4 * j, 0, 0:1], ACT.Copy).then_inc(sem("BT_ready"), 1)
            for r in range(16):
                b, u = r // 2, use["bu"] + r
                if r % 2 == 0 and b >= 2:
                    act.wait_ge(sem("chunks_odd" if b % 2 else "chunks_even"), b // 2)
                wait_filled(act, u)
                v = acc[u % 2][:, :].rearrange("p (k r t) -> p r k t", r=2, k=2)
                A(bu[:, b % 2, :, 2 * (r % 2):2 * (r % 2) + 2, :], v, ACT.Copy).then_inc(sem("bu_odd" if b % 2 else "bu_even"), 2)
                act.wait_ge(sem("bu_odd" if b % 2 else "bu_even"), 2 * (2 * (b // 2) + r % 2 + 1))
                A(tb[:, 0, 0:1], acc[u % 2][:, 0:1], ACT.Copy).then_inc(*freed(u))

            act.wait_ge(sem("CA_ready"), 1)

            def cam(f):
                if f >= 2:
                    wait_filled(act, use[f"y{f - 2}"])
                for a in range(2):
                    rows = slice(a * ST, a * ST + ST)
                    for r in range(2):
                        A(CAm[rows, f % 2, r, :, :, a * GH:a * GH + GH], CA[rows, :, r, 4 * f:4 * f + 4, :], ACT.Copy)\
                            .then_inc(sem("CAm_ready"), 1)

            cam(0)
            for f in range(8):
                if f < 7:
                    cam(f + 1)
                u = use[f"y{f}"]
                if f >= 2:
                    act.wait_ge(sem("ylo_ready"), f - 1)
                wait_filled(act, u)
                A(tb[:, f % 2, :], acc[u % 2][:, 0:SEQ], ACT.Gelu_apprx_tanh).then_inc(*freed(u))
                wait_evacuated(act, u)
                A(xT_hi[:, f, :], tb[:, f % 2, :], ACT.Copy).then_inc(sem("yhi_ready"), 1)

            def glu(j, u):
                if j >= 2:
                    act.wait_ge(sem("glu_added"), j - 1)
                wait_filled(act, u)
                A(hbuf[:, j % 2], A2(u)[:, :, PN // 2:PN], ACT.Sigmoid).then_inc(sem("glu_gate"), 1)

            gemm("glu", glu)
            root("ffn0")
            tsplit("ffn0", *gain_of("ffn0"))
            ffn(0)
            root("kv")
            tsplit("kv", *gain_of("kv"))

            def kv(j, u):
                wait_filled(act, u)
                if j < 2:
                    ins = A(kT[:, 4 * j:4 * j + 4, :], A4(u), ACT.Copy)
                else:
                    ins = A(vn_[:, :, (j - 2) * PN:(j - 1) * PN], A2(u), ACT.Copy)
                ins.then_inc(*freed(u))

            gemm("kv", kv)
            tsplit("mix1", *gain_of("mix1"))
            gemm("q", lambda j, u: (wait_filled(act, u), A(qT[:, 4 * j:4 * j + 4, :], A4(u), ACT.Copy, scale=HD ** -0.5).then_inc(*freed(u))))

            for i in range(8):
                u = use["z"] + i
                wait_filled(act, u)
                v = acc[u % 2][:, :].rearrange("p (h n) -> p h n", h=2)[:, :, 0:SW]
                A(zS[:, 2 * i:2 * i + 2, :], v, ACT.Copy).then_inc(sem("z_ready"), 1)
                A(spS[:, 2 * i:2 * i + 2, :], v, ACT.Abs).then_inc(*freed(u))
                wait_evacuated(act, u)
                act.wait_ge(sem("z_ready"), i + 1)
                step(A(spS[:, 2 * i:2 * i + 2, :], spS[:, 2 * i:2 * i + 2, :], ACT.Exp, scale=-1.0))
            step.settle()
            for i in range(4):
                A(spS[:, 4 * i:4 * i + 4, :], spS[:, 4 * i:4 * i + 4, :], ACT.Ln, bias=1.0).then_inc(sem("ln_ready"), 1)
            for i in range(8):
                act.wait_ge(sem("logw_ready"), i + 1)
                A(zS[:, 2 * i:2 * i + 2, :], zS[:, 2 * i:2 * i + 2, :], ACT.Exp).then_inc(sem("wexp_ready"), 1)
            for j in range(2):
                u = use["oT"] + j
                wait_filled(act, u)
                A(xT_hi[:, 4 * j:4 * j + 4, :], A4(u), ACT.Copy).then_inc(sem("ohi_ready"), 1)
            gemm("o", lambda j, u: None)
            root("ffn1")
            tsplit("ffn1", *gain_of("ffn1"))
            ffn(1)
            root("final")
            tsplit("final", *gain_of("final"))
            for i in range(DEPTH):
                ffn(2 + 2 * i)
                root(f"ln0_{i}")
                tsplit(f"ln0_{i}", *gain_of(f"ln0_{i}"))

                def win(j, u):
                    if j < 2:
                        wait_filled(act, u)
                        A(qaT[:, 4 * j:4 * j + 4, :], A4(u), ACT.Copy, scale=HD ** -0.5).then_inc(*freed(u))
                    elif j == 2:
                        wait_filled(act, u)
                        for src in range(2):
                            for dst in range(2):
                                step(A(kaT[dst * HD:dst * HD + HD, src::2, :], A4(u)[src * HD:src * HD + HD, 0:2], ACT.Copy))
                        step.settle()
                        A(va[:, :, :], acc[u % 2][:, 512:1024].rearrange("p (t n) -> p t n", t=TT), ACT.Copy).then_inc(*freed(u))
                    elif j < 9:
                        wait_filled(act, u)
                        for n in range(4):
                            c = 4 * (j - 3) + n
                            A(qkT[:, c, :], A4(u)[:, n], ACT.Copy, scale=cols[:, 4 + i, 3 * CONV_T + c:3 * CONV_T + c + 1]).then_inc(sem("tap4_ready"), 1)
                    elif j < 11:
                        wait_filled(act, u)
                        A(sz[:, :, (j - 9) * PN:(j - 8) * PN], A2(u), ACT.Silu).then_inc(*freed(u))
                        wait_evacuated(act, u)
                        act.sem_inc(sem("z_gate"), 1)
                    else:
                        wait_filled(act, u)
                        g, c = divmod(j - 11, 2)
                        A(gates[:, :, g, c * PN:(c + 1) * PN], A2(u), ACT.Sigmoid).then_inc(*freed(u))

                def conv_silu(j, u):
                    if 3 <= j < 9:
                        wait_evacuated(act, u)
                        c = slice(4 * (j - 3), 4 * (j - 3) + 4)
                        A(qkT[:, c, :], qkT[:, c, :], ACT.Silu).then_inc(sem("qkv_ready"), 1)

                gemm(f"win{i}", win, conv_silu)

                u = use[f"bd{i}"]
                wait_filled(act, u)
                b = acc[u % 2][:, 0:2 * TT * 8].rearrange("p (t n) -> p t n", t=TT)
                A(sm[:, 8], b[:, :, 0:8], ACT.Exp, scale=-1.0).then_inc(sem("beta_exp"), 1)
                act.wait_ge(sem("misc_in"), 96)
                step(A(sm[:, 9, 0, :], row[:, i, 0, :], ACT.Exp))
                act.wait_ge(sem("dt_raw"), i + 1)
                step(A(sm[:, 2], sm[:, 1], ACT.Abs))
                step.settle()
                step(A(sm[:, 2], sm[:, 2], ACT.Exp, scale=-1.0))
                step.settle()
                A(sm[:, 2], sm[:, 2], ACT.Ln, bias=1.0).then_inc(sem("dt_ln"), 1)

                def weights_exp(n):
                    act.wait_ge(sem("s_shifted"), 8 * i + n + 1)
                    A(zA[:, n % 2], zA[:, n % 2], ACT.Exp).then_inc(sem("s_exp"), 1)
                    A(red[:, 2, :], red[:, 2, :], ACT.Exp).then_inc(sem("s_exp"), 1)

                def attended_hi(n):
                    wait_filled(act, use[f"oa{i}_{n}"])
                    A(xT_hi[:, n, :], acc[use[f"oa{i}_{n}"] % 2][:, 0:SEQ], ACT.Copy).then_inc(sem("ahi_ready"), 1)

                for n in range(8 + 2):
                    if n < 8:
                        weights_exp(n)
                    if n >= 2:
                        attended_hi(n - 2)
                gemm(f"brA{i}", lambda j, u: None)

                act.wait_ge(sem("G_ready"), i + 1)
                step(A(sm[:, 5], sm[:, 4], ACT.Exp))
                A(sm[:, 7], sm[:, 7], ACT.Exp).then_inc(sem("G_exp"), 1)
                for t in range(TT):
                    act.wait_ge(sem("decay_log"), TT * i + t + 1)
                    A(AT[:, t], AT[:, t], ACT.Exp).then_inc(sem("decay_exp"), 1)
                    A(L[:, t], L[:, t], ACT.Exp, scale=-1.0).then_inc(sem("decay_exp"), 1)
                for g in range(4):
                    sq = (kbg, ktl)[g % 2][:, :, :].rearrange("p h d -> p (h d)")
                    u = use[f"ss{i}"] + g
                    act.wait_ge(sem("qkv_ready"), 6 * i + g + 1)
                    if g >= 2:
                        act.wait_ge(sem("qk_normed"), 4 * i + g - 1)
                    A(sq, qkT[:, 4 * g:4 * g + 4, :].rearrange("p c t -> p (c t)"), ACT.Square).then_inc(sem("squares"), 1)
                    wait_filled(act, u)
                    A(sq, acc[u % 2][:, :], ACT.Sqrt, bias=const(C_EPS, 1)).then_inc(*freed(u))
                for lv in range(LEVELS):
                    for t in range(TT):
                        u = use[f"Y{i}_{lv}"] + t
                        wait_filled(act, u)
                        A(Yp[:, t], A8(u), ACT.Copy).then_inc(*freed(u))
                for d, to in ((0, Ti[:, 0]), (2, Xm[:, 1]), (3, Ti[:, 1])):
                    u = use[f"dl{i}"] + d
                    wait_filled(act, u)
                    A(to, A8(u), ACT.Copy).then_inc(*freed(u))
                for t in range(TT):
                    act.wait_ge(sem("o_raw"), TT * i + t + 1)
                    A(Yp[:, t], L[:, t], ACT.Square).then_inc(sem("o_squares"), 1)
                for t in range(TT):
                    act.wait_ge(sem("o_var"), TT * i + t + 1)
                    A(sm[:, 9, t], sm[:, 8, t], ACT.Sqrt).then_inc(sem("o_std"), 1)
                tsplit(f"delta_{i}")
                gemm(f"brB{i}", lambda j, u: None)
                tsplit(f"mixed_{i}")
                gemm(f"wo{i}", lambda j, u: None)
                root(f"ln1_{i}")
                tsplit(f"ln1_{i}", *gain_of(f"ln1_{i}"))
                ffn(3 + 2 * i)
                root(f"ln2_{i}")
                if i < DEPTH - 1:
                    tsplit(f"ln2_{i}", *gain_of(f"ln2_{i}"))

        @block.vector
        def _(dve):
            step = Steps(dve, "dve_steps")
            V_ = nc.vector

            def do(ins):
                step(ins)
                step.settle()

            def split_lo(p):
                if p >= n_panels:
                    return
                dve.wait_ge(hi_ready, p + 1)
                kt = panels[p][3]
                V_.tensor_tensor(w_lo[:, p % SPL, 0:kt, :], raw[:, p % RAW, 0:kt, :], w_hi[:, p % SPL, 0:kt, :].bitcast(F32),
                                 ALU.subtract).then_inc(lo_ready, 1)

            def gemm(name, evacuate, after=None):
                for j, ps in enumerate(gemms[name]):
                    for p in ps[:-1]:
                        split_lo(p + SPL)
                    evacuate(j, use[name] + j)
                    split_lo(ps[-1] + SPL)
                    if after:
                        after(j, use[name] + j)

            def norm(name, eps, center=False):
                for t in range(TT):
                    for c in range(2):
                        step(V_.bn_stats(stat[:, t, c, :], x[:, t, c * 512:c * 512 + 512]))
                step.settle()
                for t in range(TT):
                    step(V_.bn_aggr(mv[:, t, :], stat[:, t].rearrange("p c s -> p (c s)")))
                step.settle()
                if center:
                    V_.tensor_scalar(nrm[:, 0, :], mv[:, :, 1], eps, None, ALU.add).then_inc(sem("var_ready"), 1)
                else:
                    do(V_.tensor_tensor(nrm[:, 2, :], mv[:, :, 0], mv[:, :, 0], ALU.mult))
                    V_.scalar_tensor_tensor(nrm[:, 0, :], nrm[:, 2, :], eps, mv[:, :, 1], ALU.add, ALU.add).then_inc(sem("var_ready"), 1)
                dve.wait_ge(sem("std_ready"), norms[name] + 1)
                do(V_.reciprocal(nrm[:, 3, :], nrm[:, 1, :]))
                for t in range(TT):
                    if center:
                        ins = V_.tensor_scalar(xn[:, t, :], x[:, t, :], mv[:, t, 0:1], nrm[:, 3, t:t + 1], ALU.subtract, ALU.mult)
                    else:
                        ins = V_.tensor_scalar(xn[:, t, :], x[:, t, :], nrm[:, 3, t:t + 1], None, ALU.mult)
                    ins.then_inc(sem("xn_ready"), 1)

            def tsplit(name, gain=None, bias=None):
                for g in range(4):
                    n = 4 * tsplits[name] + g
                    dve.wait_ge(sem("xhi_ready"), 2 * n + 2)
                    tr = trp[n % 2][:, :].rearrange("p (k t) -> p k t", k=2)
                    ks = slice(2 * g, 2 * g + 2)
                    if gain is None:
                        V_.tensor_tensor(xT_lo[:, ks, :], tr, xT_hi[:, ks, :].bitcast(F32), ALU.subtract).then_inc(sem("xlo_ready"), 2)
                        continue
                    if bias is not None:
                        dve.wait_ge(sem("xlo_ready"), 2 * n)
                        for k in range(2):
                            kk = 2 * g + k
                            step(V_.tensor_scalar(tb[:, k, :], tr[:, k], gain[:, kk:kk + 1], bias[:, kk:kk + 1], ALU.mult, ALU.add))
                        step.settle()
                        V_.tensor_tensor(xT_lo[:, ks, :], tb[:, :, :], xT_hi[:, ks, :].bitcast(F32), ALU.subtract).then_inc(sem("xlo_ready"), 2)
                        continue
                    for k in range(2):
                        kk = 2 * g + k
                        V_.scalar_tensor_tensor(xT_lo[:, kk, :], tr[:, k], gain[:, kk:kk + 1], xT_hi[:, kk, :].bitcast(F32),
                                                ALU.mult, ALU.subtract).then_inc(sem("xlo_ready"), 1)

            def add_to_x(scale=None, nat=None):
                def evacuate(j, u):
                    wait_filled(dve, u)
                    if nat is not None:
                        dve.wait_ge(sem("xnat_ready"), naturals[nat] + 1)
                    xs = x[:, :, j * PN:j * PN + PN]
                    if scale is None:
                        ins = V_.tensor_tensor(xs, xs, A2(u), ALU.add)
                    else:
                        ins = V_.scalar_tensor_tensor(xs, xs, scale, A2(u), ALU.mult, ALU.add)
                    ins.then_inc(*freed(u))
                    if j == 1:
                        wait_evacuated(dve, u - 1)
                        wait_evacuated(dve, u)
                return evacuate

            def ffn(f, scale=None, nat=None):
                def gate(j, u):
                    hn = f * 11 + j
                    h = hbuf[:, hn % 2]
                    if f < 2:
                        for n in range(2):
                            c = 2 * j + n
                            dve.wait_ge(sem("tap_ready"), 2 * hn + 2)
                            do(V_.scalar_tensor_tensor(h[:, n, 1:], A4(u)[:, n, 0:SEQ - 1], cols[:, 2 + f, FT + c:FT + c + 1], h[:, n, 1:], ALU.mult, ALU.add))
                            V_.scalar_tensor_tensor(h[:, n, 2:], A4(u)[:, n, 0:SEQ - 2], cols[:, 2 + f, c:c + 1], h[:, n, 2:], ALU.mult, ALU.add)\
                                .then_inc(sem("conv_ready"), 1)
                    dve.wait_ge(sem("gate_ready"), hn + 1)
                    V_.tensor_tensor(h, h, A4(u)[:, 2:4], ALU.mult).then_inc(*freed(u))

                def hidden(j, u):
                    hn = f * 11 + j
                    dve.wait_ge(sem("hhi_ready"), hn + 1)
                    ts_ = slice(2 * j, 2 * j + 2)
                    V_.tensor_tensor(hT_lo[:, ts_, :], hbuf[:, hn % 2], hT_hi[:, ts_, :].bitcast(F32), ALU.subtract).then_inc(sem("hlo_ready"), 1)

                gemm(f"up{f}", gate, hidden)
                gemm(f"down{f}", add_to_x(scale, nat))

            for p in range(SPL):
                split_lo(p)
            dve.wait_ge(sem("x_in"), 16)
            norm("mix0", EPS)
            tsplit("mix0", *gain_of("mix0"))
            dve.wait_ge(sem("bdw_hi_ready"), 1)
            V_.tensor_tensor(bdw_lo[:, :, :, :], bdw[:, :, :, :], bdw_hi[:, :, :, :].bitcast(F32), ALU.subtract).then_inc(sem("bdw_ready"), 1)
            dve.wait_ge(sem("den_ready"), 1)
            V_.reciprocal(s_(19), s_(19)).then_inc(sem("inv_ready"), 1)
            gemm("ssm_in", lambda j, u: None)

            dve.wait_ge(sem("pT_ready"), 1)
            dve.wait_ge(sem("ssm_b_in"), 32)
            t = [tmpv[:, i // 2, (i % 2) * 512:(i % 2) * 512 + 512].rearrange("p (k h) -> p k h", h=GH) for i in range(4)]
            for i, (r, f) in enumerate([(0, 7), (1, 8), (1, 7), (0, 8)]):
                step(V_.tensor_tensor(t[i], b_n[:, r], bc(pT[:, f, :], 2, GH), ALU.mult))
            step.settle()
            dve.wait_ge(sem("powers_ready"), 1)
            for a in range(2):
                rows = slice(a * ST, a * ST + ST)
                for r in range(2):
                    V_.tensor_tensor(Bm[rows, r, :, a * GH:a * GH + GH], t[2 * r][rows], t[2 * r + 1][rows],
                                     ALU.add if r else ALU.subtract).then_inc(sem("Bm_ready"), 1)
            dve.wait_ge(sem("Bm_ready"), 4)
            horner(dve, V_, step, tmpv[:, :, 0:256].rearrange("p i (r k c) -> p i r k c", r=2, c=NC_), 0)
            dve.wait_ge(sem("chunks_odd"), 4)
            step(V_.memset(E[:, :, :, 0], 0.0))
            do(V_.tensor_copy(E[:, :, :, 1], V[:, :, :, 0]))
            t1, t2 = (tmpp[:, i].rearrange("p r k c -> p r (k c)")[:, :, 0:PAIRS] for i in range(2))
            for c in range(2, NC_):
                e = E[:, :, :, c - 1]
                step(V_.tensor_tensor(t1, e, bc(pT[:, 4, :], 1, 2), ALU.mult))
                do(V_.tensor_tensor(t2, E[:, ::-1, :, c - 1], pT[:, 5:7, :], ALU.mult))
                do(V_.tensor_tensor(t1, t1, t2, ALU.add))
                ins = V_.tensor_tensor(E[:, :, :, c], t1, V[:, :, :, c - 1], ALU.add)
                if c < NC_ - 1:
                    do(ins)
                else:
                    ins.then_inc(sem("scan_done"), 1)

            def block_diagonal(f):
                u = use[f"K{f}"]
                if f >= 2:
                    wait_filled(dve, use[f"y{f - 2}"])
                wait_filled(dve, u)
                k = acc[u % 2][:, 0:P].rearrange("p (j h) -> p j h", j=Q)
                o = Kbd[:, f % 2].rearrange("p j (g h) -> p j g h", g=8)
                mask = bc(bc(const(C_PAIR, 8), 1, Q), 3, GH)
                V_.tensor_tensor(o, bc(k, 2, 8), mask, ALU.mult).then_inc(*freed(u))
                wait_evacuated(dve, u)
                V_.scalar_tensor_tensor(Kbd[:, f % 2, 0, :], ident, cols[:, 0, 40 + f:41 + f], Kbd[:, f % 2, 0, :], ALU.mult, ALU.add)\
                    .then_inc(sem("Kbd_ready"), 1)

            block_diagonal(0)
            for f in range(8):
                if f < 7:
                    block_diagonal(f + 1)
                dve.wait_ge(sem("yhi_ready"), f + 1)
                V_.tensor_tensor(xT_lo[:, f, :], tb[:, f % 2, :], xT_hi[:, f, :].bitcast(F32), ALU.subtract).then_inc(sem("ylo_ready"), 1)

            def glu(j, u):
                dve.wait_ge(sem("glu_gate"), j + 1)
                h = hbuf[:, j % 2]
                V_.tensor_tensor(h, h, A2(u)[:, :, 0:PN // 2], ALU.mult).then_inc(*freed(u))
                wait_evacuated(dve, u)
                xs = x[:, :, j * PN // 2:(j + 1) * PN // 2]
                V_.tensor_tensor(xs, xs, h, ALU.add).then_inc(sem("glu_added"), 1)

            gemm("glu", glu)
            dve.wait_ge(sem("glu_added"), 4)
            norm("ffn0", EPS)
            tsplit("ffn0", *gain_of("ffn0"))
            ffn(0)
            norm("kv", EPS)
            tsplit("kv", *gain_of("kv"))
            gemm("kv", lambda j, u: None)
            tsplit("mix1", *gain_of("mix1"))
            gemm("q", lambda j, u: None)

            def diagonal(t, hs):
                return t[:, hs, :].rearrange("p h (b q) -> p h b q", b=3)[:, :, 0::2, :]

            for i in range(4):
                hs = slice(4 * i, 4 * i + 4)
                dve.wait_ge(sem("ln_ready"), i + 1)
                dve.wait_ge(sem("z_ready"), 2 * i + 2)
                do(V_.scalar_tensor_tensor(spS[:, hs, :], zS[:, hs, :], 0.0, spS[:, hs, :], ALU.max, ALU.add))
                do(V_.tensor_tensor(zS[:, hs, :], zS[:, hs, :], spS[:, hs, :], ALU.subtract))
                V_.tensor_tensor(diagonal(spS, hs), diagonal(spS, hs), bc(bc(const(C_LT), 1, 2), 1, 4), ALU.mult).then_inc(sem("sp_ready"), 1)
            for i in range(8):
                u = use["rem"] + i
                hs = slice(2 * i, 2 * i + 2)
                wait_filled(dve, u)
                v = acc[u % 2][:, :].rearrange("p (h n) -> p h n", h=2)[:, :, 0:SW]
                V_.tensor_tensor(zS[:, hs, :], zS[:, hs, :], v, ALU.subtract).then_inc(*freed(u))
                wait_evacuated(dve, u)
                V_.tensor_copy(mv[:, 0, 0:1], zS[:, 2 * i, 0:1]).then_inc(sem("logw_ready"), 1)
            for i in range(8):
                hs = slice(2 * i, 2 * i + 2)
                dve.wait_ge(sem("wexp_ready"), i + 1)
                V_.tensor_tensor(diagonal(zS, hs), diagonal(zS, hs), bc(bc(const(C_LT), 1, 2), 1, 2), ALU.mult).then_inc(sem("w_ready"), 1)
            for j in range(2):
                u = use["oT"] + j
                dve.wait_ge(sem("ohi_ready"), j + 1)
                V_.tensor_tensor(xT_lo[:, 4 * j:4 * j + 4, :], A4(u), xT_hi[:, 4 * j:4 * j + 4, :].bitcast(F32), ALU.subtract).then_inc(*freed(u))
            gemm("o", add_to_x())
            norm("ffn1", EPS)
            tsplit("ffn1", *gain_of("ffn1"))
            ffn(1)
            norm("final", EPS)
            tsplit("final", *gain_of("final"))
            for i in range(DEPTH):
                last = "final" if i == 0 else f"ln2_{i - 1}"
                ffn(2 + 2 * i, 2 * ALPHA, last)
                norm(f"ln0_{i}", 4 * LN_EPS, True)
                tsplit(f"ln0_{i}", *gain_of(f"ln0_{i}"))

                def short_conv(j, u):
                    if not 3 <= j < 9:
                        return
                    dve.wait_ge(sem("tap4_ready"), 4 * (6 * i + j - 2))
                    for back in (1, 2, 3):
                        for n in range(4):
                            c = 4 * (j - 3) + n
                            w = (3 - back) * CONV_T + c
                            ins = V_.scalar_tensor_tensor(qkT[:, c, back:], A4(u)[:, n, 0:SEQ - back], cols[:, 4 + i, w:w + 1],
                                                          qkT[:, c, back:], ALU.mult, ALU.add)
                            if back < 3 or n < 3:
                                step(ins)
                        if back < 3:
                            step.settle()
                    step.settle()
                    ins.then_inc(*freed(u))

                gemm(f"win{i}", short_conv)

                u = use[f"bd{i}"]
                b = acc[u % 2][:, 0:2 * TT * 8].rearrange("p (t n) -> p t n", t=TT)
                dve.wait_ge(sem("beta_exp"), i + 1)
                dve.wait_ge(sem("misc_in"), 96)
                V_.tensor_tensor(sm[:, 1], b[:, :, 8:16], bc(row[:, i, 1, :], 1, TT), ALU.add).then_inc(*freed(u))
                wait_evacuated(dve, u)
                dve.sem_inc(sem("dt_raw"), 1)
                do(V_.tensor_scalar(sm[:, 8], sm[:, 8], 1.0, None, ALU.add))
                step(V_.reciprocal(sm[:, 0], sm[:, 8]))
                dve.wait_ge(sem("dt_ln"), i + 1)
                do(V_.scalar_tensor_tensor(sm[:, 3], sm[:, 1], 0.0, sm[:, 2], ALU.max, ALU.add))
                V_.scalar_tensor_tensor(sm[:, 3], sm[:, 3], -1.0, bc(sm[:, 9, 0, :], 1, TT), ALU.mult, ALU.mult).then_inc(sem("g_ready"), 1)

                def scores(n):
                    u = use[f"s{i}_{n}"]
                    v = acc[u % 2][:, :].rearrange("p (h b k) -> p h b k", h=2, b=4)
                    hs = slice(2 * n, 2 * n + 2)
                    z, zp = zA[:, n % 2], zB[:, n % 2]
                    if n >= 2:
                        dve.wait_ge(sem("s_turned"), 8 * i + n - 1)
                    wait_filled(dve, u)
                    step(V_.tensor_tensor(z, v[:, :, 0:3:2, :], bc(biasL[:, hs, :], 2, 2), ALU.add))
                    step.settle()
                    V_.tensor_tensor(zp, v[:, :, 1, :], biasU[:, hs, :], ALU.add).then_inc(*freed(u))
                    wait_evacuated(dve, u)
                    do(V_.tensor_tensor(z[:, :, 1, :], z[:, :, 1, :], zp, ALU.max))
                    do(V_.tensor_reduce(red[:, 0, :].rearrange("p (h b) -> p h b", h=2), z, AX_X, ALU.max))
                    r = [red[:, q, :].rearrange("p (h b) -> p h b", h=2) for q in range(4)]
                    sink = bc(snk[:, i, hs], 2, 2)
                    do(V_.tensor_tensor(r[1], r[0], sink, ALU.max))
                    do(V_.tensor_tensor(r[2], sink, r[1], ALU.subtract))
                    V_.tensor_tensor(z, z, bc(r[1], 3, P), ALU.subtract).then_inc(sem("s_shifted"), 1)

                def normalize(n):
                    z = zA[:, n % 2]
                    r = [red[:, q, :].rearrange("p (h b) -> p h b", h=2) for q in range(4)]
                    dve.wait_ge(sem("s_exp"), 2 * (8 * i + n + 1))
                    do(V_.tensor_reduce(r[0], z, AX_X, ALU.add))
                    do(V_.tensor_tensor(r[0], r[0], r[2], ALU.add))
                    do(V_.reciprocal(r[3], r[0]))
                    V_.tensor_tensor(z, z, bc(r[3], 3, P), ALU.mult).then_inc(sem("s_normed"), 1)

                def mask_turned(n):
                    tr = trp[n % 2][:, :].rearrange("p (h b q) -> p h b q", h=2, b=2)
                    dve.wait_ge(sem("s_turned"), 8 * i + n + 1)
                    if n >= 1:
                        wait_filled(dve, use[f"oa{i}_{n - 1}"])
                    step(V_.tensor_tensor(pT3[:, :, 0::2, :], tr, bc(bc(const(C_LE), 1, 2), 1, 2), ALU.mult))
                    step.settle()
                    V_.tensor_tensor(pT3[:, :, 1, :], tr[:, :, 1, :], bc(const(C_GT), 1, 2), ALU.mult).then_inc(sem("pT3_ready"), 1)

                def attended_lo(n):
                    u = use[f"oa{i}_{n}"]
                    dve.wait_ge(sem("ahi_ready"), 8 * i + n + 1)
                    V_.tensor_tensor(xT_lo[:, n, :], acc[u % 2][:, 0:SEQ], xT_hi[:, n, :].bitcast(F32), ALU.subtract).then_inc(*freed(u))

                dve.wait_ge(sem("bias_ready"), i + 1)
                for n in range(8 + 3):
                    if 1 <= n < 9:
                        normalize(n - 1)
                    if n < 8:
                        scores(n)
                    if 2 <= n < 10:
                        mask_turned(n - 2)
                    if n >= 3:
                        attended_lo(n - 3)

                def gate_a(j, u):
                    wait_filled(dve, u)
                    g = gates[:, :, 0, j * PN:(j + 1) * PN]
                    V_.tensor_tensor(g, g, A2(u), ALU.mult).then_inc(*freed(u))

                gemm(f"brA{i}", gate_a)

                u = use[f"G{i}"]
                wait_filled(dve, u)
                v = acc[u % 2][:, 0:32].rearrange("p (q t h) -> p q t h", q=2, t=TT)
                do(V_.tensor_copy(sm[:, 4], v[:, 0]))
                V_.tensor_tensor(sm[:, 7], v[:, 1], sm[:, 4], ALU.subtract).then_inc(*freed(u))
                wait_evacuated(dve, u)
                dve.sem_inc(sem("G_ready"), 1)
                for t in range(TT):
                    u = use[f"Gr{i}"] + t
                    wait_filled(dve, u)
                    V_.tensor_tensor(L[:, t], A8(u), bc(sm[:, 4, t, :], 2, P), ALU.subtract).then_inc(*freed(u))
                    wait_evacuated(dve, u)
                    do(V_.tensor_scalar(AT[:, t], L[:, t], 0.0, None, ALU.min))
                    V_.tensor_scalar(L[:, t], L[:, t], 0.0, None, ALU.max).then_inc(sem("decay_log"), 1)
                dve.wait_ge(sem("G_exp"), i + 1)
                do(V_.scalar_tensor_tensor(sm[:, 6], sm[:, 0], -1.0, sm[:, 5], ALU.mult, ALU.mult))
                for g in range(4):
                    sq = (kbg, ktl)[g % 2][:, :, :].rearrange("p h d -> p (h d)")
                    qk = qkT[:, 4 * g:4 * g + 4, :].rearrange("p c t -> p (c t)")
                    wait_evacuated(dve, use[f"ss{i}"] + g)
                    do(V_.reciprocal(sq, sq))
                    V_.scalar_tensor_tensor(qk, qk, DK ** -0.5 if g < 2 else 1.0, sq, ALU.mult, ALU.mult).then_inc(sem("qk_normed"), 1)
                for n, (to, by) in enumerate([(vb[:, 0], sm[:, 0, 0]), (vb[:, 1], sm[:, 0, 1]), (ktl[:, :, :], sm[:, 7, 0]), (kbg[:, :, :], sm[:, 6, 1])]):
                    u = use[f"nat{i}"] + n
                    if n == 0:
                        dve.wait_ge(sem("xnat_ready"), naturals[f"ln0_{i}"] + 1)
                    wait_filled(dve, u)
                    V_.tensor_tensor(to, A8(u), bc(by, 2, P), ALU.mult).then_inc(*freed(u))
                for n, m in (("kk", L), ("qk", AT)):
                    for t in range(TT):
                        u = use[f"{n}{i}"] + t
                        wait_filled(dve, u)
                        dve.wait_ge(sem("decay_ready"), 2 * (TT * i + TT))
                        V_.tensor_tensor(m[:, t], A8(u), m[:, t], ALU.mult).then_inc(*freed(u))
                for lv in range(LEVELS):
                    for t in range(TT):
                        for name, m in (("ZU", U), ("ZT", Ti)):
                            if f"{name}{i}_{lv}_{t}" in use:
                                u = use[f"{name}{i}_{lv}_{t}"]
                                wait_filled(dve, u)
                                if lv == 0:
                                    dve.wait_ge(sem("inverse_init"), 4 * (i + 1))
                                else:
                                    wait_evacuated(dve, use[f"{name}{i}_{lv - 1}_{t}"])
                                V_.tensor_tensor(m[:, t], m[:, t], A8(u), ALU.subtract).then_inc(*freed(u))
                u = use[f"dl{i}"] + 1
                wait_filled(dve, u)
                V_.tensor_copy(Xm[:, 0], A8(u)).then_inc(*freed(u))
                u = use[f"dl{i}"] + 4
                wait_filled(dve, u)
                V_.tensor_copy(L[:, 0], A8(u)).then_inc(*freed(u))
                wait_evacuated(dve, u)
                dve.sem_inc(sem("o_raw"), 1)
                wait_filled(dve, u + 1)
                V_.tensor_tensor(L[:, 1], A8(u + 1), bc(sm[:, 5, 1], 2, P), ALU.mult).then_inc(*freed(u + 1))
                wait_evacuated(dve, u + 1)
                wait_filled(dve, u + 2)
                V_.tensor_tensor(L[:, 1], L[:, 1], A8(u + 2), ALU.add).then_inc(*freed(u + 2))
                wait_evacuated(dve, u + 2)
                dve.sem_inc(sem("o_raw"), 1)
                for t in range(TT):
                    dve.wait_ge(sem("o_squares"), TT * i + t + 1)
                    do(V_.tensor_reduce(sm[:, 10, t], Yp[:, t], AX_X, ALU.add))
                    V_.tensor_scalar(sm[:, 8, t], sm[:, 10, t], 1 / DK, NORM_EPS, ALU.mult, ALU.add).then_inc(sem("o_var"), 1)
                dve.wait_ge(sem("sz_ready"), i + 1)
                for t in range(TT):
                    dve.wait_ge(sem("o_std"), TT * i + t + 1)
                    do(V_.reciprocal(sm[:, 11, t], sm[:, 9, t]))
                    do(V_.tensor_tensor(L[:, t], L[:, t], bc(sm[:, 11, t], 2, P), ALU.mult))
                    V_.tensor_tensor(L[:, t], L[:, t], sz[:, t].rearrange("p (h d) -> p h d", d=DK), ALU.mult).then_inc(sem("o_ready"), 1)
                tsplit(f"delta_{i}")

                def gate_b(j, u):
                    wait_filled(dve, u)
                    g = gates[:, :, 1, j * PN:(j + 1) * PN]
                    V_.tensor_tensor(g, g, A2(u), ALU.mult).then_inc(*freed(u))
                    wait_evacuated(dve, u)
                    wait_evacuated(dve, use[f"brA{i}"] + j)
                    ga = gates[:, :, 0, j * PN:(j + 1) * PN]
                    V_.tensor_tensor(ga, ga, g, ALU.add).then_inc(sem("mix_ready"), 1)

                gemm(f"brB{i}", gate_b)
                tsplit(f"mixed_{i}")
                gemm(f"wo{i}", add_to_x(ALPHA, f"ln0_{i}"))
                norm(f"ln1_{i}", LN_EPS, True)
                tsplit(f"ln1_{i}", *gain_of(f"ln1_{i}"))
                ffn(3 + 2 * i, 2 * ALPHA, f"ln1_{i}")
                norm(f"ln2_{i}", 4 * LN_EPS, True)
                if i < DEPTH - 1:
                    tsplit(f"ln2_{i}", *gain_of(f"ln2_{i}"))

        @block.tensor
        def _(pe):
            mm = nc.tensor.matmul

            def claim(u):
                if u >= 2:
                    pe.wait_ge(acc_freed[u % 2], u // 2)
                return acc[u % 2]

            def product(out, pairs, first, last):
                (ah, al), (bh, bl) = pairs
                mm(out, ah, bh, start=first, stop=False, skip_group_check=True)
                mm(out, ah, bl, start=False, stop=False, skip_group_check=True)
                return mm(out, al, bh, start=False, stop=last, skip_group_check=True)

            def features(name, j, u, src, n0=0, n1=4):
                out = A4(u)
                claim(u)
                for i, p in enumerate(gemms[name][j]):
                    pe.wait_ge(lo_ready, p + 1)
                    _, _, k0, kt, _ = panels[p]
                    for n in range(n0, n1):
                        for k in range(kt):
                            c = slice(n * P, n * P + P)
                            w = (w_hi[:, p % SPL, k, c], w_lo[:, p % SPL, k, c])
                            a = (src[0][:, k0 + k, :], src[1][:, k0 + k, :])
                            ins = product(out[:, n], (w, a), i == 0 and k == 0 and n % 2 == 0, i == len(gemms[name][j]) - 1 and k == kt - 1)
                    if n1 == 4:
                        ins.then_inc(panel_used, 1)
                    else:
                        values(name, j, u, src, p, i)

            def values(name, j, u, src, p, i):
                out = acc[u % 2][:, 512:1024].rearrange("p (t n) -> p t n", t=TT)
                _, _, k0, kt, _ = panels[p]
                for t in range(TT):
                    for k in range(kt):
                        tok = slice(t * P, t * P + P)
                        a = (src[0][:, k0 + k, tok], src[1][:, k0 + k, tok])
                        w = (w_hi[:, p % SPL, k, 256:512], w_lo[:, p % SPL, k, 256:512])
                        ins = product(out[:, t], (a, w), i == 0 and k == 0 and t == 0, i == len(gemms[name][j]) - 1 and k == kt - 1)
                ins.then_inc(panel_used, 1)

            def tokens(name, j, u, src, ready=None):
                out = A2(u)
                claim(u)
                for i, p in enumerate(gemms[name][j]):
                    pe.wait_ge(lo_ready, p + 1)
                    _, _, k0, kt, _ = panels[p]
                    if ready and j == 0:
                        ready(k0, kt)
                    for k in range(kt):
                        for t in range(TT):
                            tok = slice(t * P, t * P + P)
                            a = (src[0][:, k0 + k, tok], src[1][:, k0 + k, tok])
                            w = (w_hi[:, p % SPL, k, :], w_lo[:, p % SPL, k, :])
                            ins = product(out[:, t], (a, w), i == 0 and k == 0, i == len(gemms[name][j]) - 1 and k == kt - 1)
                    ins.then_inc(panel_used, 1)

            xT, hT = (xT_hi, xT_lo), (hT_hi, hT_lo)

            def xT_ready(name):
                pe.wait_ge(sem("xlo_ready"), 8 * (tsplits[name] + 1))

            def turn(name, src, ready, value):
                pe.wait_ge(sem(ready), value)
                for g in range(4):
                    n = 4 * tsplits[name] + g
                    if n >= 2:
                        pe.wait_ge(sem("xlo_ready"), 2 * (n - 1))
                    for k in range(2):
                        for t in range(TT):
                            ins = nc.tensor.transpose(trp[n % 2][:, (2 * k + t) * P:(2 * k + t + 1) * P],
                                                      src[:, t, (2 * g + k) * P:(2 * g + k + 1) * P], ident)
                    ins.then_inc(sem("turned"), 1)

            def turn_norm(norm_name, name=None):
                turn(name or norm_name, xn, "xn_ready", TT * (norms[norm_name] + 1))

            def ffn(f, xname):
                xT_ready(xname)
                for j in range(11):
                    features(f"up{f}", j, use[f"up{f}"] + j, xT)
                for j in range(2):
                    tokens(f"down{f}", j, use[f"down{f}"] + j, hT,
                           lambda k0, kt: pe.wait_ge(sem("hlo_ready"), f * 11 + (k0 + kt) // 2))

            pe.wait_ge(sem("const_in"), 16)
            pe.wait_ge(sem("cols_in"), 16 * sum(len(t) for t in COLUMN_TILES))
            a = claim(use["cols"])
            for i, parts in enumerate(COLUMN_TILES):
                n = sum(q[1] for q in parts)
                ins = nc.tensor.transpose(a[:, i * P:i * P + n], stage[0:n, i, :], cst[0:n, C_ID:C_ID + n])
            ins.then_inc(acc_ready, 1)
            turn_norm("mix0")
            pe.wait_ge(sem("ssm_c_in"), 64)
            for r in range(2):
                a = claim(use["CT"] + r)
                for f in range(8):
                    ins = nc.tensor.transpose(a[:, f * P:f * P + P], c_n[:, r, f].rearrange("p a b -> p (a b)"), ident)
                ins.then_inc(acc_ready, 1)
            pe.wait_ge(sem("misc_in"), 96)
            a = claim(use["ftab"])
            mm(a[0:HEADS, 0:P], relb[:, :], bsel[:, :], start=True, stop=True).then_inc(acc_ready, 1)
            xT_ready("mix0")
            for j in range(2):
                features("ssm_in", j, use["ssm_in"] + j, xT)

            pe.wait_ge(sem("powers_ready"), 1)
            a = claim(use["pT"])
            for q in range(9):
                ins = nc.tensor.transpose(a[:, q * PAIRS:(q + 1) * PAIRS], pn[:, q, :], cst[0:PAIRS, C_ID:C_ID + PAIRS])
            ins.then_inc(acc_ready, 1)
            pe.wait_ge(sem("Bm_ready"), 4)
            for j in range(2):
                a = claim(use["BT"] + j)
                for f in range(4):
                    for r in range(2):
                        ins = nc.tensor.transpose(a[:, (2 * f + r) * P:(2 * f + r + 1) * P],
                                                  Bm[:, r, 16 * j + 4 * f:16 * j + 4 * f + 4, :].rearrange("p k c -> p (k c)"), ident)
                ins.then_inc(acc_ready, 1)
            wait_evacuated(pe, use["ssm_in"] + 1)
            wait_evacuated(pe, use["ssm_in"])
            pe.wait_ge(sem("BT_ready"), 2)
            for r in range(16):
                u = use["bu"] + r
                claim(u)
                a = acc[u % 2][:, :].rearrange("p (k r t) -> p r k t", r=2, k=2)
                for k in range(2):
                    pair = 2 * r + k
                    rows = slice(32 * (pair % 4), 32 * (pair % 4) + 32)
                    for c in range(2):
                        ins = mm(a[:, c, k], BT[rows, pair // 4, c, :], uT[rows, pair // 4, :], start=True, stop=True, skip_group_check=True)
                ins.then_inc(acc_ready, 1)

            def response(f):
                a = claim(use[f"K{f}"])
                for k in range(4):
                    pair = 4 * f + k
                    o = a[32 * k:32 * k + 32, 0:P].rearrange("p (j h) -> p j h", j=Q)
                    for r in range(2):
                        mm(o[:, 0], Bm[:, r, pair, :], CT[:, r, pair, :], start=r == 0, stop=r == 1, skip_group_check=True)
                        ins = mm(o[:, 1:Q], Bm[:, r, pair, :], CA[:, 0:Q - 1, r, pair, :], start=False, stop=r == 1, skip_group_check=True)
                ins.then_inc(acc_ready, 1)

            pe.wait_ge(sem("CA_ready"), 1)
            response(0)
            for f in range(8):
                if f < 7:
                    response(f + 1)
                u = use[f"y{f}"]
                claim(u)
                y = acc[u % 2][:, 0:SEQ].rearrange("p (c j) -> p c j", j=Q)
                uc = uT[:, f, :].rearrange("p (c j) -> p c j", j=Q)
                pe.wait_ge(sem("Kbd_ready"), f + 1)
                for j in range(Q):
                    mm(y[:, :, j:Q], Kbd[:, f % 2, j, :], uc[:, :, 0:Q - j], start=j == 0, stop=False, skip_group_check=True)
                pe.wait_ge(sem("CAm_ready"), 4 * (f + 1))
                pe.wait_ge(sem("scan_done"), 1)
                for k in range(4):
                    for j in range(Q):
                        for r in range(2):
                            ins = mm(y[32 * k:32 * k + 32, :, j], CAm[:, f % 2, r, j, k, :], E[:, r, 4 * f + k, :], start=False,
                                     stop=r == 1, skip_group_check=True)
                ins.then_inc(acc_ready, 1)
            pe.wait_ge(sem("ylo_ready"), 8)
            for j in range(4):
                tokens("glu", j, use["glu"] + j, xT)
            turn_norm("ffn0")
            ffn(0, "ffn0")
            turn_norm("kv")
            xT_ready("kv")
            for j in range(2):
                features("kv", j, use["kv"] + j, xT)
            for j in range(2, 4):
                tokens("kv", j, use["kv"] + j, xT)
            turn_norm("kv", "mix1")
            xT_ready("mix1")
            for j in range(2):
                features("q", j, use["q"] + j, xT)

            wait_evacuated(pe, use["q"])
            wait_evacuated(pe, use["q"] + 1)
            for i in range(8):
                u = use["z"] + i
                a = claim(u)
                for h in range(2):
                    rows = slice(HD * h, HD * h + HD)
                    mm(a[:, h * 512:h * 512 + SEQ], kT[rows, i, 0:P], qT[rows, i, :], start=True, stop=True, skip_group_check=True)
                    ins = mm(a[:, h * 512 + SEQ:h * 512 + SW], kT[rows, i, P:SEQ], qT[rows, i, P:SEQ], start=True, stop=True, skip_group_check=True)
                ins.then_inc(acc_ready, 1)
            for i in range(8):
                u = use["rem"] + i
                a = claim(u)
                pe.wait_ge(sem("sp_ready"), i // 2 + 1)
                for h in range(2):
                    s0 = spS[:, 2 * i + h, :]
                    mm(a[:, h * 512:h * 512 + SEQ], const(C_GT), s0[:, 0:SEQ], start=True, stop=False, skip_group_check=True)
                    mm(a[:, h * 512 + P:h * 512 + SEQ], const(C_ONE), s0[:, SEQ:SW], start=False, stop=True, skip_group_check=True)
                    ins = mm(a[:, h * 512 + SEQ:h * 512 + SW], const(C_GT), s0[:, SEQ:SW], start=True, stop=True, skip_group_check=True)
                ins.then_inc(acc_ready, 1)
            for j in range(2):
                u = use["oT"] + j
                a = claim(u)
                for i in range(4 * j, 4 * j + 4):
                    pe.wait_ge(sem("w_ready"), i + 1)
                    for h in range(2):
                        head = 2 * i + h
                        o = a[HD * h:HD * h + HD, (i % 4) * SEQ:(i % 4 + 1) * SEQ]
                        d = slice(head * HD, head * HD + HD)
                        mm(o, vn_[:, 0, d], zS[:, head, 0:SEQ], start=True, stop=False, skip_group_check=True)
                        ins = mm(o[:, P:SEQ], vn_[:, 1, d], zS[:, head, SEQ:SW], start=False, stop=True, skip_group_check=True)
                ins.then_inc(acc_ready, 1)
            wait_evacuated(pe, use["oT"])
            wait_evacuated(pe, use["oT"] + 1)
            for j in range(2):
                tokens("o", j, use["o"] + j, xT)
            turn_norm("ffn1")
            ffn(1, "ffn1")
            turn_norm("final")
            for i in range(DEPTH):
                ffn(2 + 2 * i, "final" if i == 0 else f"ln2_{i - 1}")
                turn_norm(f"ln0_{i}")
                xT_ready(f"ln0_{i}")
                for j in range(15):
                    u = use[f"win{i}"] + j
                    if j == 2:
                        features(f"win{i}", j, u, xT, 0, 2)
                    elif j < 9:
                        features(f"win{i}", j, u, xT)
                    else:
                        tokens(f"win{i}", j, u, xT)
                pe.wait_ge(sem("bdw_ready"), 1)
                a = claim(use[f"bd{i}"])
                for t in range(TT):
                    for k in range(KT):
                        tok = slice(t * P, t * P + P)
                        ins = product(a[:, 16 * t:16 * t + 16], ((xT_hi[:, k, tok], xT_lo[:, k, tok]), (bdw_hi[:, i, k, :], bdw_lo[:, i, k, :])),
                                      t == 0 and k == 0, k == KT - 1)
                ins.then_inc(acc_ready, 1)

                def scores(n):
                    u = use[f"s{i}_{n}"]
                    a = claim(u)
                    for h in range(2):
                        rows = slice(HD * h, HD * h + HD)
                        mm(a[:, h * 512:h * 512 + P], qaT[rows, n, 0:P], kaT[rows, n // 2, 0:P], start=True, stop=True, skip_group_check=True)
                        ins = mm(a[:, h * 512 + P:h * 512 + 3 * P], qaT[rows, n, P:SEQ], kaT[rows, n // 2, :], start=True, stop=True, skip_group_check=True)
                    ins.then_inc(acc_ready, 1)

                def turn_weights(n):
                    pe.wait_ge(sem("s_normed"), 8 * i + n + 1)
                    if n >= 2:
                        pe.wait_ge(sem("pT3_ready"), 8 * i + n - 1)
                    for h in range(2):
                        for b in range(2):
                            ins = nc.tensor.transpose(trp[n % 2][:, (2 * h + b) * P:(2 * h + b + 1) * P], zA[:, n % 2, h, b, :], ident)
                    ins.then_inc(sem("s_turned"), 1)

                def attend(n):
                    a = claim(use[f"oa{i}_{n}"])
                    pe.wait_ge(sem("pT3_ready"), 8 * i + n + 1)
                    d = slice((n // 2) * HD, (n // 2) * HD + HD)
                    for h in range(2):
                        rows = slice(HD * h, HD * h + HD)
                        mm(a[rows, 0:P], va[:, 0, d], pT3[:, h, 0, :], start=True, stop=True, skip_group_check=True)
                        mm(a[rows, P:SEQ], va[:, 0, d], pT3[:, h, 1, :], start=True, stop=False, skip_group_check=True)
                        ins = mm(a[rows, P:SEQ], va[:, 1, d], pT3[:, h, 2, :], start=False, stop=True, skip_group_check=True)
                    ins.then_inc(acc_ready, 1)

                for j in range(3):
                    wait_evacuated(pe, use[f"win{i}"] + j)
                for n in range(8 + 2):
                    if n < 8:
                        scores(n)
                    if 1 <= n < 9:
                        turn_weights(n - 1)
                    if n >= 2:
                        attend(n - 2)
                for n in range(8):
                    wait_evacuated(pe, use[f"oa{i}_{n}"])
                for j in range(2):
                    tokens(f"brA{i}", j, use[f"brA{i}"] + j, xT)

                a = claim(use[f"G{i}"])
                pe.wait_ge(sem("g_ready"), i + 1)
                mm(a[:, 0:16], const(C_LE), sm[:, 3].rearrange("p t h -> p (t h)"), start=True, stop=True, skip_group_check=True)
                mm(a[:, 16:32], const(C_ONE), sm[:, 3].rearrange("p t h -> p (t h)"), start=True, stop=True, skip_group_check=True).then_inc(acc_ready, 1)
                for t in range(TT):
                    a = claim(use[f"Gr{i}"] + t)
                    for h in range(DH):
                        ins = mm(a[:, h * P:h * P + P], sm[:, 3, t, h:h + 1].to_broadcast([P, P]), const(C_LE), start=True, stop=True, skip_group_check=True)
                    ins.then_inc(acc_ready, 1)
                for g in range(4):
                    sq = (kbg, ktl)[g % 2][:, :, :].rearrange("p h d -> p (h d)")
                    a = claim(use[f"ss{i}"] + g)
                    pe.wait_ge(sem("squares"), 4 * i + g + 1)
                    for c in range(2):
                        ins = mm(a[:, c * 512:c * 512 + 512], const(C_ONE), sq[:, c * 512:c * 512 + 512], start=True, stop=True, skip_group_check=True)
                    ins.then_inc(acc_ready, 1)
                pe.wait_ge(sem("qkv_ready"), 6 * (i + 1))
                for n in range(4):
                    a = claim(use[f"nat{i}"] + n)
                    if n == 2:
                        pe.wait_ge(sem("qk_normed"), 4 * (i + 1))
                    src, t = (vh, n) if n < 2 else (kh, n - 2)
                    for h in range(DH):
                        ins = nc.tensor.transpose(a[:, h * P:h * P + P], src[:, h, t * P:t * P + P], ident)
                    ins.then_inc(acc_ready, 1)
                for name, right in (("kk", kh), ("qk", qh)):
                    for t in range(TT):
                        a = claim(use[f"{name}{i}"] + t)
                        tok = slice(t * P, t * P + P)
                        for h in range(DH):
                            ins = mm(a[:, h * P:h * P + P], kh[:, h, tok], right[:, h, tok], start=True, stop=True, skip_group_check=True)
                        ins.then_inc(acc_ready, 1)

                def heads(u, *terms):
                    a = claim(u)
                    for h in range(DH):
                        for n, (left, right) in enumerate(terms):
                            ins = mm(a[:, h * P:h * P + P], left[:, h, :], right[:, h, :], start=n == 0, stop=n == len(terms) - 1, skip_group_check=True)
                    ins.then_inc(acc_ready, 1)

                pe.wait_ge(sem("inverse_init"), 4 * (i + 1))
                for lv in range(LEVELS):
                    for t in range(TT):
                        pe.wait_ge(sem("Xm_ready"), TT * (LEVELS * i + lv) + t + 1)
                        if lv:
                            wait_evacuated(pe, use[f"ZU{i}_{lv - 1}_{t}"])
                        heads(use[f"Y{i}_{lv}"] + t, (Xm[:, t], U[:, t]))
                    for t in range(TT):
                        wait_evacuated(pe, use[f"Y{i}_{lv}"] + t)
                        if lv:
                            wait_evacuated(pe, use[f"ZT{i}_{lv - 1}_{t}"])
                        heads(use[f"ZU{i}_{lv}_{t}"], (Ti[:, t], Yp[:, t]))
                        if lv < LEVELS - 1:
                            heads(use[f"ZT{i}_{lv}_{t}"], (Yp[:, t], Ti[:, t]))
                for t in range(TT):
                    wait_evacuated(pe, use[f"ZU{i}_{LEVELS - 1}_{t}"])
                d = use[f"dl{i}"]
                heads(d, (U[:, 0], vb[:, 0]))
                heads(d + 1, (kbg, U[:, 1]))
                wait_evacuated(pe, d)
                heads(d + 2, (ktl, Ti[:, 0]))
                wait_evacuated(pe, d + 1)
                wait_evacuated(pe, d + 2)
                heads(d + 3, (U[:, 1], vb[:, 1]), (Xm[:, 0], Xm[:, 1]))
                heads(d + 4, (AT[:, 0], Ti[:, 0]))
                heads(d + 5, (qh[:, :, P:SEQ], Xm[:, 1]))
                wait_evacuated(pe, d + 3)
                heads(d + 6, (AT[:, 1], Ti[:, 1]))
                turn(f"delta_{i}", L[:, :, :, :].rearrange("p t h d -> p t (h d)"), "o_ready", TT * (i + 1))
                xT_ready(f"delta_{i}")
                for j in range(2):
                    tokens(f"brB{i}", j, use[f"brB{i}"] + j, xT)
                turn(f"mixed_{i}", gates[:, :, 0, :], "mix_ready", 2 * (i + 1))
                xT_ready(f"mixed_{i}")
                for j in range(2):
                    tokens(f"wo{i}", j, use[f"wo{i}"] + j, xT)
                turn_norm(f"ln1_{i}")
                ffn(3 + 2 * i, f"ln1_{i}")
                if i < DEPTH - 1:
                    turn_norm(f"ln2_{i}")


INPUTS = """x norm_mix norm_ffn norm_kv norm_final ssm_w_in ssm_a_re ssm_a_im ssm_log_dt ssm_b_re ssm_b_im ssm_c_re
ssm_c_im ssm_d ssm_w_glu kv_w attn_w_q attn_w_o ffn_w_up ffn_conv_w ffn_conv_b ffn_w_down rel_bias_2 ln_g_2 ln_b_2
ffn_w13_2 ffn_w2_2 w_in_2 conv_w_2 a_log_2 dt_bias_2 dn_norm_g_2 sinks_2 w_branch_a_2 w_branch_b_2 w_out_2""".split()


def kernel(**inputs):
    import concourse.bacc as _bacc
    from concourse.bass_utils import run_bass_kernel_spmd as _run

    nc = _bacc.Bacc("TRN2", target_bir_lowering=False, num_devices=1)
    arrays = {name: np.ascontiguousarray(inputs[name]) for name in INPUTS}
    arrays["const_masks"] = constants()
    arrays["const_buckets"] = bucket_pattern()
    tensors = {name: nc.dram_tensor(f"in_{name}", a.shape, F32, kind="ExternalInput").ap() for name, a in arrays.items()}
    out = nc.dram_tensor("out_x", (1, SEQ, D), F32, kind="ExternalOutput").ap()
    build(nc, tensors, out)
    result = _run(nc, [{f"in_{name}": a for name, a in arrays.items()}], core_ids=[0])
    return result.results[0]["out_x"]
```

```python
import math
from contextlib import ExitStack

import numpy as np

import concourse.bass as bass
from concourse import mybir

F32 = mybir.dt.float32
F32R = mybir.dt.float32r
ALU = mybir.AluOpType
ACT = mybir.ActivationFunctionType
AX_X = mybir.AxisListType.X

P = 128
SEQ = 256
D = 1024
KT = D // P
TT = SEQ // P
D_FF = 2816
FT = D_FF // P
DEPTH = 2
EPS = 1e-6
LN_EPS = 1e-5
NORM_EPS = 1e-6
ALPHA = (2 * DEPTH) ** 0.25
NEG_INF = -1e30
GROUPS, GH, ST = 64, 16, 64
PAIRS = GROUPS // 2
Q = 8
NC_ = SEQ // Q
HEADS, HD = 16, 64
KV_HEADS = 4
DH, DK = 8, 128
CONV_T = 3 * DH
LEVELS = 7
N_IN = 7696
BUCKETS = 32

PK, PN = 4, 512
RAW, SPL = 2, 3
TRP = 4

TWO_PI = 2 * math.pi
MAGIC = 1.5 * 2 ** 23


def two_pi_parts():
    c1 = float(np.float32(6.28125))
    c2 = float(np.float32(round((TWO_PI - c1) * 2 ** 22) / 2 ** 22))
    return c1, c2, TWO_PI - c1 - c2


SIDE = 9
SIDE_STEPS = [2, 2, 1, 1, 1, 1, 1, 1, 1, 1]

C_ID, C_LE, C_LT, C_GT, C_ONE = (i * P for i in range(5))
C_LVL = 5 * P
C_PAIR = C_LVL + LEVELS * P
C_NEGU = C_PAIR + 8
C_NEGL = C_NEGU + P
C_EPS = C_NEGL + P
N_CONST = C_EPS + 1


def constants():
    i, j = np.arange(P)[:, None], np.arange(P)[None, :]
    c = np.zeros((P, N_CONST), np.float32)
    c[:, C_ID:C_ID + P] = i == j
    c[:, C_LE:C_LE + P] = i <= j
    c[:, C_LT:C_LT + P] = i < j
    c[:, C_GT:C_GT + P] = i > j
    c[:, C_ONE:C_ONE + P] = 1
    for lv in range(LEVELS):
        b = 1 << lv
        c[:, C_LVL + lv * P:C_LVL + (lv + 1) * P] = (i // (2 * b) == j // (2 * b)) & (i // b % 2 == 1) & (j // b % 2 == 0)
    c[:, C_PAIR:C_PAIR + 8] = i // GH == np.arange(8)[None, :]
    c[:, C_NEGU:C_NEGU + P] = np.where(j > i, NEG_INF, 0)
    c[:, C_NEGL:C_NEGL + P] = np.where(j <= i, NEG_INF, 0)
    c[:, C_EPS] = NORM_EPS
    return c


def bucket_pattern():
    n = np.arange(P)
    exact = BUCKETS // 2
    nf = np.maximum(n, 1).astype(np.float32)
    large = exact + (np.log(nf / np.float32(exact)) / np.float32(math.log(P / exact)) * np.float32(BUCKETS - exact)).astype(np.int32)
    b = np.where(n < exact, n, np.minimum(large, BUCKETS - 1))
    return (np.arange(BUCKETS)[:, None] == b[::-1][None, :]).astype(np.float32)


def plan():
    panels, gemms = [], {}

    def add(name, w, index, ktiles, columns):
        cols = []
        for c0, c1 in columns:
            ps = []
            for k0 in range(0, ktiles, PK):
                ps.append(len(panels))
                panels.append((w, index, k0, min(PK, ktiles - k0), (c0, c1)))
            cols.append(ps)
        gemms[name] = cols

    def straight(n, start=0):
        return [(c, c + PN // 2) for c in range(start, start + n, PN)]

    def paired(n):
        return [(c, n + c) for c in range(0, n, PN // 2)]

    def ffn(f, up, down, index):
        add(f"up{f}", up, index, KT, paired(D_FF))
        add(f"down{f}", down, index, FT, straight(D))

    for j in range(2):
        add(f"ssm_in{j}", "ssm_w_in", (0,), KT, straight(PN, j * PN))
    add("glu", "ssm_w_glu", (0,), KT, paired(D))
    ffn(0, "ffn_w_up", "ffn_w_down", (0,))
    add("kv", "kv_w", (), KT, straight(2 * D))
    add("q", "attn_w_q", (0,), KT, straight(D))
    add("o", "attn_w_o", (0,), KT, straight(D))
    ffn(1, "ffn_w_up", "ffn_w_down", (1,))
    for i in range(DEPTH):
        ffn(2 + 2 * i, "ffn_w13_2", "ffn_w2_2", (i, 0))
        add(f"win{i}", "w_in_2", (i,), KT, straight(1536 + 3072) + straight(3072, 4624))
        for j in range(2):
            add(f"brA{i}_{j}", "w_branch_a_2", (i,), KT, straight(PN, j * PN))
        add(f"brB{i}", "w_branch_b_2", (i,), KT, straight(D))
        add(f"wo{i}", "w_out_2", (i,), KT, straight(D))
        ffn(3 + 2 * i, "ffn_w13_2", "ffn_w2_2", (i, 1))
    return panels, gemms


COLUMN_TILES = [
    [("norm_mix", 16), ("norm_ffn", 16), ("norm_kv", 8), ("ssm_d", 8), ("ln_g_2", 48), ("norm_final", 8)],
    [("ln_b_2", 48), ("ffn_conv_b", 44)],
    [("ffn_conv_w", 66, 0)],
    [("ffn_conv_w", 66, 66)],
    [("conv_w_2", 96, 0)],
    [("conv_w_2", 96, 96)],
]

def build(nc, T, out):
    panels, gemms = plan()
    n_panels = len(panels)

    es = ExitStack()
    with es:
        def sb(name, shape, dt=F32, stack=es):
            return stack.enter_context(nc.sbuf_tensor(name, shape, dt))

        sems = {}

        def sem(name):
            if name not in sems:
                sems[name] = es.enter_context(nc.semaphore(name))
            return sems[name]

        raw = sb("raw", [P, RAW, PK, PN])
        w_hi = sb("w_hi", [P, SPL, PK, PN], F32R)
        w_lo = sb("w_lo", [P, SPL, PK, PN], F32R)
        xT_hi = sb("xT_hi", [P, KT, SEQ], F32R)
        xT_lo = sb("xT_lo", [P, KT, SEQ], F32R)
        x = sb("x", [P, TT, D])
        xn = sb("xn", [P, TT, D])
        cst = sb("cst", [P, N_CONST])
        cols = sb("cols", [P, 6, 104])
        bdw_hi = sb("bdw_hi", [P, DEPTH, KT, 16], F32R)
        bdw_lo = sb("bdw_lo", [P, DEPTH, KT, 16], F32R)
        stat = sb("stat", [P, TT, 2, 6])
        mv = sb("mv", [P, TT, 2])
        nrm = sb("nrm", [P, 4, TT])
        row = sb("row", [P, DEPTH, 2, 8])
        snk = sb("snk", [P, DEPTH, HEADS])
        dng = sb("dng", [P, DEPTH, DK])

        def const(at, n=P):
            return cst[:, at:at + n]

        ident = const(C_ID)

        gb = sb("gb", [P, 2, D])
        tb = sb("tb", [P, 2, SEQ])

        s1 = ExitStack()
        uT = sb("uT", [P, KT, SEQ], F32, s1)
        Bm = sb("Bm", [P, 2, PAIRS, 32], F32, s1)
        pT = sb("pT", [P, 12, PAIRS], F32, s1)
        tmpv = sb("tmpv", [P, 2, 1024], F32, s1)
        CT = sb("CT", [P, 2, PAIRS, GH], F32, s1)
        tmpp = sb("tmpp", [P, 2, 2, 4, NC_], F32, s1)
        bsel = sb("bsel", [BUCKETS, P], F32, s1)
        relb = sb("relb", [BUCKETS, HEADS], F32, s1)
        ftab = sb("ftab", [HEADS, P], F32, s1)
        s1c = ExitStack()
        bdw = sb("bdw", [P, DEPTH, KT, 16], F32, s1c)
        b_n = sb("b_n", [P, 2, PAIRS, GH], F32, s1c)
        pn = sb("pn", [PAIRS, 23, P], F32, s1c)
        s1c.close()
        CA = sb("CA", [P, Q, 2, PAIRS, GH], F32, s1)
        s1a = ExitStack()
        BT = sb("BT", [P, 2, 8, 2, P], F32, s1a)
        bu = sb("bu", [P, 2, 2, 4, SEQ // 2], F32, s1a)
        s1a.close()
        s1b = ExitStack()
        CAm = sb("CAm", [P, 2, 2, Q, 4, 32], F32, s1b)
        Kbd = sb("Kbd", [P, 2, Q, P], F32, s1b)
        s1b.close()
        s1.close()
        stage = uT[:, 0:3, :].rearrange("p a (b c) -> p (a b) c", c=P)
        c_n = gb[:, :, :].rearrange("p r (f d s) -> p r f d s", f=8, d=2)
        BAm = gb[:, :, :].rearrange("p r (k c) -> p r k c", c=32)
        E = xn[:, :, :].rearrange("p t (k c) -> p t k c", c=NC_)
        V = gb[:, :, :].rearrange("p t (k c) -> p t k c", c=NC_)

        s2 = ExitStack()
        hT_hi = sb("hT_hi", [P, FT, SEQ], F32R, s2)
        hT_lo = sb("hT_lo", [P, FT, SEQ], F32R, s2)
        hbuf = sb("hbuf", [P, 2, 2, SEQ], F32, s2)
        s2.close()

        s3 = ExitStack()
        kT = sb("kT", [P, KT, SEQ], F32, s3)
        qT = sb("qT", [P, KT, SEQ], F32, s3)
        vn_ = sb("vnat", [P, TT, D], F32, s3)
        SW = 3 * P
        zS = sb("zS", [P, HEADS, SW], F32, s3)
        spS = sb("spS", [P, HEADS, SW], F32, s3)
        s3.close()

        s4 = ExitStack()
        qkT = sb("qkT", [P, CONV_T, SEQ], F32, s4)
        sz = sb("sz", [P, TT, D], F32, s4)
        gates = sb("gates", [P, TT, 2, D], F32, s4)
        sm = sb("sm", [P, 12, TT, 8], F32, s4)
        s4a = ExitStack()
        qaT = sb("qaT", [P, KT, SEQ], F32, s4a)
        kaT = sb("kaT", [P, KV_HEADS, SEQ], F32, s4a)
        va = sb("va", [P, TT, 256], F32, s4a)
        biasL = sb("biasL", [P, HEADS, P], F32, s4a)
        biasU = sb("biasU", [P, HEADS, P], F32, s4a)
        zA = sb("zA", [P, 2, 2, 2, P], F32, s4a)
        zB = sb("zB", [P, 2, 2, P], F32, s4a)
        pT3 = sb("pT3", [P, 2, 3, P], F32, s4a)
        red = sb("red", [P, 4, 4], F32, s4a)
        s4a.close()
        s4b = ExitStack()
        L = sb("L", [P, TT, 8, P], F32, s4b)
        AT = sb("AT", [P, TT, 8, P], F32, s4b)
        Ti = sb("Ti", [P, TT, 8, P], F32, s4b)
        U = sb("U", [P, TT, 8, P], F32, s4b)
        kbg = sb("kbg", [P, 8, P], F32, s4b)
        ktl = sb("ktl", [P, 8, P], F32, s4b)
        s4b.close()
        s4.close()
        vb = xn[:, :, :].rearrange("p t (h d) -> p t h d", d=DK)
        qh, kh, vh = qkT[:, 0:8], qkT[:, 8:16], qkT[:, 16:24]
        Xm = kh.rearrange("p a b -> p (a b)").rearrange("p (t h m) -> p t h m", t=TT, h=8)
        Yp = vh.rearrange("p a b -> p (a b)").rearrange("p (t h m) -> p t h m", t=TT, h=8)

        acc = [es.enter_context(nc.psum_tensor(f"acc{i}", [P, 1024], F32)) for i in range(2)]
        trp = [es.enter_context(nc.psum_tensor(f"trp{i}", [P, 512], F32)) for i in range(TRP)]

        ftab_d = nc.dram_tensor("ftab_d", (HEADS, P, P), F32, kind="Internal").ap()

        raw_loaded = [sem(f"raw_loaded{i}") for i in range(RAW)]
        hi_ready, lo_ready, panel_used = sem("hi_ready"), sem("lo_ready"), sem("panel_used")
        acc_ready = sem("acc_ready")
        acc_freed = [sem("acc_freed0"), sem("acc_freed1")]

        use, filled = {}, {}
        n_use = n_fill = 0

        def uses(name, count, gemm=None):
            nonlocal n_use, n_fill
            use[name] = n_use
            for j in range(count):
                if gemm:
                    filled[n_use] = (panel_used, gemms[gemm][j][-1] + 1)
                else:
                    n_fill += 1
                    filled[n_use] = (acc_ready, n_fill)
                n_use += 1

        def gemm_uses(name):
            uses(name, len(gemms[name]), name)

        uses("cols", 1)
        uses("CT", 2)
        uses("ftab", 1)
        gemm_uses("ssm_in0")
        uses("pT", 1)
        gemm_uses("ssm_in1")
        uses("BT", 4)
        uses("bu", 16)
        uses("K0", 1)
        for f in range(8):
            if f < 7:
                uses(f"K{f + 1}", 1)
            uses(f"y{f}", 1)
        gemm_uses("glu")
        gemm_uses("up0"), gemm_uses("down0")
        gemm_uses("kv"), gemm_uses("q")
        uses("z", 8), uses("rem", 8), uses("oT", 2)
        gemm_uses("o")
        gemm_uses("up1"), gemm_uses("down1")
        for i in range(DEPTH):
            gemm_uses(f"up{2 + 2 * i}"), gemm_uses(f"down{2 + 2 * i}")
            uses(f"win{i}", SIDE, f"win{i}")
            uses(f"bd{i}", 1)
            for n in range(8 + 2):
                if n < 8:
                    uses(f"s{i}_{n}", 1)
                if n >= 2:
                    uses(f"oa{i}_{n - 2}", 1)
            uses(f"G{i}", 1)
            gemm_uses(f"brA{i}_0")
            uses(f"Gr{i}", 2), uses(f"ss{i}a", 2)
            gemm_uses(f"brA{i}_1")
            uses(f"ss{i}b", 2), uses(f"nat{i}", 4), uses(f"kk{i}", 2), uses(f"qk{i}", 2)
            for lv in range(LEVELS):
                uses(f"Y{i}_{lv}", 2)
                for t in range(TT):
                    if lv:
                        uses(f"ZU{i}_{lv}_{t}", 1)
                    if 0 < lv < LEVELS - 1:
                        uses(f"ZT{i}_{lv}_{t}", 1)
            uses(f"dl{i}", 7)
            gemm_uses(f"brB{i}"), gemm_uses(f"wo{i}")
            gemm_uses(f"up{3 + 2 * i}"), gemm_uses(f"down{3 + 2 * i}")

        def side_panels(i, n):
            every = [(j, p == ps[-1], p) for j, ps in enumerate(gemms[f"win{i}"]) if j >= SIDE for p in ps]
            first = sum(SIDE_STEPS[:n])
            return every[first:first + SIDE_STEPS[n]]

        def wait_filled(eng, u):
            eng.wait_ge(*filled[u])

        def freed(u):
            return acc_freed[u % 2], 1

        tsplits = {}

        def tsplit_no(name):
            if name not in tsplits:
                tsplits[name] = len(tsplits)
            return tsplits[name]

        for name in ["mix0", "ffn0", "kv", "mix1", "ffn1", "final"]:
            tsplit_no(name)
        for i in range(DEPTH):
            for name in ["ln0", "delta", "mixed", "ln1"] + ["ln2"] * (i < DEPTH - 1):
                tsplit_no(f"{name}_{i}")
        norms = {n: i for i, n in enumerate(
            ["mix0", "ffn0", "kv", "ffn1", "final"] + [f"ln{j}_{i}" for i in range(DEPTH) for j in range(3)])}
        naturals = {n: i for i, n in enumerate(["final"] + [f"ln{j}_{i}" for i in range(DEPTH) for j in range(3)])}

        def gain_of(name):
            c0, c1 = cols[:, 0, :], cols[:, 1, :]
            if name.startswith("ln"):
                j, i = int(name[2]), int(name[4])
                at = (i * 3 + j) * 8
                return c0[:, 48 + at:48 + at + 8], c1[:, at:at + 8]
            at = {"mix0": 0, "mix1": 8, "ffn0": 16, "ffn1": 24, "kv": 32, "final": 96}[name]
            return c0[:, at:at + 8], None

        def A4(u, f=4):
            return acc[u % 2][:, :].rearrange("p (n t) -> p n t", n=f)

        def A2(u):
            return acc[u % 2][:, :].rearrange("p (t n) -> p t n", t=2)

        def A8(u):
            return acc[u % 2][:, :].rearrange("p (h m) -> p h m", h=8)

        def doubled(i, lv, t, name):
            return use[f"{name}{i}_{lv}_{t}"] if lv else use[f"Y{i}_0"] + t

        def blocks(ap, lv, side):
            return ap.rearrange("p (m s b) -> p m s b", s=2, b=1 << lv)[:, :, side, :]

        def bc(ap, axis, n):
            a = ap.unsqueeze(axis)
            shape = list(a.shape)
            shape[axis] = n
            return a.to_broadcast(shape)

        class Steps:

            def __init__(self, eng, name):
                self.eng, self.sem, self.n = eng, sem(name), 0

            def __call__(self, ins):
                ins.then_inc(self.sem, 1)
                self.n += 1

            def settle(self, but=0):
                self.eng.wait_ge(self.sem, self.n - but)

        def wait_evacuated(eng, u):
            eng.wait_ge(acc_freed[u % 2], u // 2 + 1)

        def rows_of(name):
            src = T[name]
            letters = " ".join("abcd"[:len(src.shape)])
            return src.rearrange(f"{letters} -> ({letters})").rearrange("(r c) -> r c", c=P)

        def s_(i):
            return pn[:, i, :]

        block = es.enter_context(nc.Block())

        @block.sync
        def _(sp):
            sp.dma_start(pn[:, 9, :], T["ssm_a_re"][0].rearrange("(k a) p -> k (a p)", a=2)).then_inc(sem("ssm_a_in"), 16)
            sp.dma_start(pn[:, 10, :], T["ssm_a_im"][0].rearrange("(k a) p -> k (a p)", a=2)).then_inc(sem("ssm_a_in"), 16)
            sp.dma_start(pn[:, 12, 0:2], T["ssm_log_dt"][0].rearrange("(k a) -> k a", a=2)).then_inc(sem("ssm_a_in"), 16)
            sp.dma_start(x[:, :, :], T["x"][0].rearrange("(t p) d -> p t d", p=P)).then_inc(sem("x_in"), 16)

            for r, name in enumerate(("ssm_c_re", "ssm_c_im")):
                for dup in range(2):
                    sp.dma_start(c_n[:, r, :, dup, :], T[name][0].rearrange("(f q) h p -> (q h) f p", q=8)).then_inc(sem("ssm_c_in"), 16)
            for r, name in enumerate(("ssm_b_re", "ssm_b_im")):
                sp.dma_start(b_n[:, r, :, :], T[name][0].rearrange("(k a) p h -> (a p) k h", a=2)).then_inc(sem("ssm_b_in"), 16)

            def parameters():
                sp.dma_start(bdw[:, :, :, :], T["w_in_2"][:, :, 4608:4624].rearrange("i (k p) n -> p i k n", p=P)).then_inc(sem("bdw_in"), 16)
                sp.dma_start(relb[:, :], T["rel_bias_2"]).then_inc(sem("misc_in"), 16)
                sp.dma_start(bsel[:, :], T["const_buckets"]).then_inc(sem("misc_in"), 16)
                sp.dma_start(row[:, :, 0, :], T["a_log_2"].partition_broadcast(P)).then_inc(sem("misc_in"), 16)
                sp.dma_start(row[:, :, 1, :], T["dt_bias_2"].partition_broadcast(P)).then_inc(sem("misc_in"), 16)
                sp.dma_start(snk[:, :, :], T["sinks_2"].partition_broadcast(P)).then_inc(sem("misc_in"), 16)
                sp.dma_start(dng[:, :, :], T["dn_norm_g_2"].partition_broadcast(P)).then_inc(sem("misc_in"), 16)

            for p, (w, index, k0, kt, (c0, c1)) in enumerate(panels):
                if p >= n_panels:
                    break
                src = T[w]
                for i in index:
                    src = src[i]
                src = src[k0 * P:(k0 + kt) * P, :].rearrange("(k p) n -> p k n", p=P)
                if p == RAW:
                    parameters()
                if p >= RAW:
                    sp.wait_ge(lo_ready, p - RAW + 1)
                slot, half = raw[:, p % RAW, 0:kt, :], PN // 2
                if c1 == c0 + half:
                    sp.dma_start(slot, src[:, :, c0:c0 + PN]).then_inc(raw_loaded[p % RAW], 32)
                else:
                    sp.dma_start(slot[:, :, 0:half], src[:, :, c0:c0 + half]).then_inc(raw_loaded[p % RAW], 16)
                    sp.dma_start(slot[:, :, half:PN], src[:, :, c1:c1 + half]).then_inc(raw_loaded[p % RAW], 16)
            sp.wait_ge(sem("out_ready"), 1)
            sp.dma_start(out[0].rearrange("(t p) d -> p t d", p=P), x[:, :, :]).then_inc(sem("out_stored"), 16)
            sp.wait_ge(sem("out_stored"), 16)

        @block.gpsimd
        def _(pool):
            step = Steps(pool, "pool_steps")
            tt = nc.gpsimd.tensor_tensor
            ts = nc.gpsimd.tensor_scalar

            def s(i):
                return pn[:, i, :]

            def do(ins):
                step(ins)
                step.settle()

            for i, ((name, n, first),) in enumerate(COLUMN_TILES[2:], 2):
                pool.dma_start(stage[0:n, i, :], rows_of(name)[first:first + n, :]).then_inc(sem("conv_cols_in"), 16)
            step(nc.gpsimd.memset(Bm[:, :, :, :], 0.0))
            pool.wait_ge(sem("dt_ready"), 1)
            pool.wait_ge(sem("ssm_a_in"), 48)
            dt = bc(pn[:, 12, 2:4], 2, ST)

            def halves(i):
                return s(i).rearrange("k (a p) -> k a p", a=2)

            step(tt(halves(13), halves(9), dt, ALU.mult))
            do(tt(halves(14), halves(10), dt, ALU.mult))
            pool.wait_ge(step.sem, step.n)
            nc.gpsimd.tensor_copy(s(19), s(13)).then_inc(sem("mag_in"), 1)
            do(ts(s(15), s(14), 1 / TWO_PI, MAGIC, ALU.mult, ALU.add))
            do(ts(s(15), s(15), -MAGIC, None, ALU.add))
            for part in two_pi_parts():
                do(ts(s(16), s(15), -part, None, ALU.mult))
                do(tt(s(14), s(14), s(16), ALU.add))
            ts(s(14), s(14), 3.1415925, -3.1415925, ALU.min, ALU.max).then_inc(sem("angle_ready"), 1)
            pool.wait_ge(sem("trig_ready"), 3)
            do(tt(s(17), s(16), s(16), ALU.mult))
            do(ts(s(17), s(17), -2.0, 1.0, ALU.mult, ALU.add))
            step(tt(s(0), s(13), s(17), ALU.mult))
            do(tt(s(2), s(13), s(15), ALU.mult))
            step(ts(s(1), s(2), -1.0, None, ALU.mult))
            step(ts(s(3), s(2), -1.0, None, ALU.mult))
            step(tt(s(17), s(9), s(9), ALU.mult))
            do(tt(s(18), s(10), s(10), ALU.mult))
            tt(s(19), s(17), s(18), ALU.add).then_inc(sem("den_ready"), 1)
            pool.wait_ge(sem("den_ready"), 1)
            re, im = 0, 2
            for n in range(int(math.log2(Q))):
                step(tt(s(17), s(re), s(re), ALU.mult))
                step(tt(s(18), s(im), s(im), ALU.mult))
                do(tt(s(16), s(re), s(im), ALU.mult))
                re, im = 4, 6
                step(tt(s(re), s(17), s(18), ALU.subtract))
                do(ts(s(im), s(16), 2.0, None, ALU.mult))
                if n == 0:
                    step(nc.gpsimd.tensor_copy(s(20), s(re)))
                    step(ts(s(21), s(im), -1.0, None, ALU.mult))
                    do(nc.gpsimd.tensor_copy(s(22), s(im)))
            step(ts(s(5), s(6), -1.0, None, ALU.mult))
            do(ts(s(16), s(0), -1.0, None, ALU.add))
            step(tt(s(13), s(16), s(9), ALU.mult))
            step(tt(s(14), s(2), s(10), ALU.mult))
            step(tt(s(17), s(2), s(9), ALU.mult))
            do(tt(s(18), s(16), s(10), ALU.mult))
            step(tt(s(13), s(13), s(14), ALU.add))
            do(tt(s(17), s(17), s(18), ALU.subtract))
            pool.wait_ge(sem("inv_ready"), 1)
            step(tt(s(7), s(13), s(19), ALU.mult))
            do(tt(s(8), s(17), s(19), ALU.mult))
            nc.gpsimd.tensor_copy(s(12), s(8)).then_inc(sem("powers_ready"), 1)

            pool.wait_ge(sem("pT_ready"), 1)
            pool.wait_ge(sem("CT_ready"), 4)
            pool.wait_ge(sem("BAm_ready"), 1)
            t1, t2 = (tmpv[:, i, :].rearrange("p (r k h) -> p r k h", r=2, h=GH) for i in range(2))
            for j in range(Q):
                prev = CA[:, j - 1] if j else CT[:, :, :, :]
                step(tt(t1, prev, bc(bc(pT[:, 0, :], 1, 2), 3, GH), ALU.mult))
                do(tt(t2, prev[:, ::-1], bc(pT[:, 2:4, :], 3, GH), ALU.mult))
                do(tt(CA[:, j], t1, t2, ALU.add))
            pool.sem_inc(sem("CA_ready"), 1)
            pool.wait_ge(sem("chunks_done"), 8)
            pool.wait_ge(sem("ftab_stored"), 16)
            nc.gpsimd.memset(CAm[:, :, :, :, :, :], 0.0).then_inc(sem("CAm_cleared"), 1)

            order = list(naturals)

            def load_gain(name):
                if name == "final":
                    pool.dma_start(gb[:, 0, :], T["norm_final"].partition_broadcast(P)).then_inc(sem("gain_in"), 32)
                else:
                    j, i = int(name[2]), int(name[4])
                    pool.dma_start(gb[:, 0, :], T["ln_g_2"][i, j].partition_broadcast(P)).then_inc(sem("gain_in"), 16)
                    pool.dma_start(gb[:, 1, :], T["ln_b_2"][i, j].partition_broadcast(P)).then_inc(sem("gain_in"), 16)

            def natural(name):
                n = naturals[name]
                pool.wait_ge(sem("gain_in"), 32 * (n + 1))
                pool.wait_ge(sem("xn_ready"), TT * (norms[name] + 1))
                for t in range(TT):
                    step(tt(x[:, t, :], xn[:, t, :], gb[:, 0, :], ALU.mult))
                step.settle()
                if name != "final":
                    for t in range(TT):
                        step(tt(x[:, t, :], x[:, t, :], gb[:, 1, :], ALU.add))
                    step.settle()
                pool.sem_inc(sem("xnat_ready"), 1)
                if n + 1 < len(order) :
                    load_gain(order[n + 1])

            pool.wait_ge(sem("scan_done"), 1)
            load_gain("final")
            natural("final")
            for i in range(DEPTH):
                natural(f"ln0_{i}")
                skew = bass.AP(ftab_d.tensor, P - 1, [[P - 1, P], [P * P, HEADS], [1, P]])
                pool.dma_start(biasL[:, :, :], skew).then_inc(sem("bias_in"), 16)
                pool.wait_ge(sem("bias_in"), 16 * (i + 1))
                do(tt(biasU[:, :, :], biasL[:, :, :], bc(const(C_NEGL), 1, HEADS), ALU.add))
                tt(biasL[:, :, :], biasL[:, :, :], bc(const(C_NEGU), 1, HEADS), ALU.add).then_inc(sem("bias_ready"), 1)
                pool.wait_ge(sem("gate_columns"), 12 * i + 4)
                szh = sz[:, :, :].rearrange("p t (h d) -> p (t h) d", d=DK)
                tt(szh, szh, bc(dng[:, i, :], 1, TT * DH), ALU.mult).then_inc(sem("sz_ready"), 1)
                for t in range(TT):
                    pool.wait_ge(sem("decay_exp"), 2 * (TT * i + t + 1))
                    tt(AT[:, t], AT[:, t], bc(const(C_LE), 1, DH), ALU.mult).then_inc(sem("decay_ready"), 1)
                    do(tt(L[:, t], L[:, t], bc(const(C_GT), 1, DH), ALU.mult))
                    tt(L[:, t], L[:, t], bc(sm[:, 0, t, :], 2, P), ALU.mult).then_inc(sem("decay_ready"), 1)
                for t in range(TT):
                    nc.gpsimd.tensor_copy(U[:, t], bc(ident, 1, DH)).then_inc(sem("inverse_init"), 1)
                    nc.gpsimd.tensor_copy(Ti[:, t], bc(ident, 1, DH)).then_inc(sem("inverse_init"), 1)
                for lv in range(LEVELS):
                    for t in range(TT):
                        if lv == 0:
                            wait_evacuated(pool, use[f"kk{i}"] + t)
                            wait_evacuated(pool, use[f"qk{i}"] + 1)
                        else:
                            wait_filled(pool, use[f"Y{i}_{lv - 1}"] + t)
                        if lv == 1:
                            pool.wait_ge(sem("Ti_pairs"), TT * i + t + 1)
                        tt(Xm[:, t], L[:, t], bc(const(C_LVL + lv * P), 1, DH), ALU.mult).then_inc(sem("Xm_ready"), 1)
                        if lv == 0:
                            pool.wait_ge(sem("Xm_ready"), TT * LEVELS * i + t + 1)
                            pool.wait_ge(sem("inverse_init"), 4 * i + 2 * t + 2)
                            tt(Ti[:, t], Ti[:, t], Xm[:, t], ALU.subtract).then_inc(sem("Ti_pairs"), 1)
                natural(f"ln1_{i}")
                natural(f"ln2_{i}")
            pool.sem_inc(sem("out_ready"), 1)

        @block.scalar
        def _(act):
            step = Steps(act, "act_steps")
            A = nc.scalar.activation

            act.dma_start(cst[:, :], T["const_masks"]).then_inc(sem("const_in"), 16)
            for i, parts in enumerate(COLUMN_TILES[:2]):
                at = 0
                for name, n in parts:
                    act.dma_start(stage[at:at + n, i, :], rows_of(name)[:n, :]).then_inc(sem("cols_in"), 16)
                    at += n
            def split_hi(p):
                if p >= n_panels:
                    return
                act.wait_ge(raw_loaded[p % RAW], 32 * (p // RAW + 1))
                if p >= SPL:
                    act.wait_ge(panel_used, p - SPL + 1)
                kt = panels[p][3]
                A(w_hi[:, p % SPL, 0:kt, :], raw[:, p % RAW, 0:kt, :], ACT.Copy).then_inc(hi_ready, 1)

            def gemm(name, evacuate, after=None, columns=None):
                for j, ps in enumerate(gemms[name][:columns]):
                    for p in ps[:-1]:
                        split_hi(p + SPL)
                    evacuate(j, use[name] + j)
                    split_hi(ps[-1] + SPL)
                    if after:
                        after(j, use[name] + j)

            def root(name):
                act.wait_ge(sem("var_ready"), norms[name] + 1)
                A(nrm[:, 1, :], nrm[:, 0, :], ACT.Sqrt).then_inc(sem("std_ready"), 1)

            def tsplit(name, gain=None, bias=None):
                for g in range(4):
                    n = 4 * tsplits[name] + g
                    act.wait_ge(sem("turned"), n + 1)
                    tr = trp[n % TRP][:, :].rearrange("p (k t) -> p k t", k=2)
                    if gain is None:
                        A(xT_hi[:, 2 * g:2 * g + 2, :], tr, ACT.Copy).then_inc(sem("xhi_ready"), 2)
                        continue
                    for k in range(2):
                        kk = 2 * g + k
                        if bias is None:
                            ins = A(xT_hi[:, kk, :], tr[:, k], ACT.Copy, scale=gain[:, kk:kk + 1])
                        else:
                            ins = A(xT_hi[:, kk, :], tr[:, k], ACT.Identity, scale=gain[:, kk:kk + 1], bias=bias[:, kk:kk + 1])
                        ins.then_inc(sem("xhi_ready"), 1)

            def ffn(f):
                def gate(j, u):
                    hn = f * 11 + j
                    if hn >= 2:
                        act.wait_ge(sem("hlo_ready"), hn - 1)
                    wait_filled(act, u)
                    h = hbuf[:, hn % 2]
                    if f < 2:
                        for n in range(2):
                            c = 2 * j + n
                            ins = A(h[:, n], A4(u)[:, n], ACT.Identity, scale=cols[:, 2 + f, 2 * FT + c:2 * FT + c + 1],
                                    bias=cols[:, 1, 48 + f * FT + c:48 + f * FT + c + 1])
                            ins.then_inc(sem("tap_ready"), 1)
                        act.wait_ge(sem("conv_ready"), 2 * hn + 2)
                        A(h, h, ACT.Silu).then_inc(sem("gate_ready"), 1)
                    else:
                        A(h, A4(u)[:, 0:2], ACT.Silu).then_inc(sem("gate_ready"), 1)

                def hidden(j, u):
                    wait_evacuated(act, u)
                    A(hT_hi[:, 2 * j:2 * j + 2, :], hbuf[:, (f * 11 + j) % 2], ACT.Copy).then_inc(sem("hhi_ready"), 1)

                gemm(f"up{f}", gate, hidden)
                gemm(f"down{f}", lambda j, u: None)

            act.wait_ge(sem("ssm_a_in"), 48)
            A(pn[:, 12, 2:4], pn[:, 12, 0:2], ACT.Exp).then_inc(sem("dt_ready"), 1)
            act.wait_ge(sem("mag_in"), 1)
            A(s_(13), s_(19), ACT.Exp).then_inc(sem("trig_ready"), 1)
            split_hi(0)
            u = use["cols"]
            wait_filled(act, u)
            for i, parts in enumerate(COLUMN_TILES):
                n = sum(q[1] for q in parts)
                ins = A(cols[:, i, 0:n], acc[u % 2][:, i * P:i * P + n], ACT.Copy)
                if i < 5:
                    step(ins)
            step.settle()
            ins.then_inc(*freed(u))
            wait_evacuated(act, u)
            root("mix0")
            act.wait_ge(sem("angle_ready"), 1)
            A(s_(15), s_(14), ACT.Sin).then_inc(sem("trig_ready"), 1)
            A(s_(16), s_(14), ACT.Sin, scale=0.5).then_inc(sem("trig_ready"), 1)
            tsplit("mix0", *gain_of("mix0"))
            for p in range(1, SPL):
                split_hi(p)
            for r in range(2):
                u = use["CT"] + r
                wait_filled(act, u)
                v = acc[u % 2][:, :].rearrange("p (f k a h) -> p f k a h", f=8, k=4, a=2)
                for a in range(2):
                    rows = slice(a * ST, a * ST + ST)
                    A(CT[rows, r].rearrange("p (f k) h -> p f k h", f=8), v[rows, :, :, a, :], ACT.Copy,
                      scale=-1.0 if r else 1.0).then_inc(sem("CT_ready"), 1)
                act.wait_ge(sem("CT_ready"), 2 * r + 2)
                A(tb[:, 0, 0:1], acc[u % 2][:, 0:1], ACT.Copy).then_inc(*freed(u))
            u = use["ftab"]
            wait_filled(act, u)
            A(ftab[:, :], acc[u % 2][0:HEADS, 0:P], ACT.Copy).then_inc(*freed(u))
            wait_evacuated(act, u)
            act.dma_start(ftab_d, bc(ftab[:, :], 1, P)).then_inc(sem("ftab_stored"), 16)
            act.wait_ge(sem("bdw_in"), 16)
            A(bdw_hi[:, :, :, :], bdw[:, :, :, :], ACT.Copy).then_inc(sem("bdw_hi_ready"), 1)

            def ssm_in(j):
                def evacuate(_, u):
                    wait_filled(act, u)
                    A(uT[:, 4 * j:4 * j + 4, :], A4(u), ACT.Copy).then_inc(*freed(u))
                return evacuate

            gemm("ssm_in0", ssm_in(0))
            u = use["pT"]
            wait_filled(act, u)
            A(pT[:, :, :], acc[u % 2][:, 0:12 * PAIRS].rearrange("p (q k) -> p q k", q=12), ACT.Copy).then_inc(*freed(u))
            wait_evacuated(act, u)
            act.sem_inc(sem("pT_ready"), 1)
            gemm("ssm_in1", ssm_in(1))
            for j in range(4):
                u = use["BT"] + j
                wait_filled(act, u)
                A(BT[:, j // 2, 4 * (j % 2):4 * (j % 2) + 4].rearrange("p f r m -> p (f r m)"), acc[u % 2][:, :], ACT.Copy).then_inc(*freed(u))
                wait_evacuated(act, u)
                act.sem_inc(sem("BT_ready"), 1)
            for r in range(16):
                b, u = r // 2, use["bu"] + r
                if r % 2 == 0 and b >= 2:
                    act.wait_ge(sem("chunks_done"), b - 1)
                wait_filled(act, u)
                v = acc[u % 2][:, :].rearrange("p (k r t) -> p r k t", r=4, k=2)[:, 0:2, :, 0:SEQ // 2]
                A(bu[:, b % 2, :, 2 * (r % 2):2 * (r % 2) + 2, :], v, ACT.Copy).then_inc(*freed(u))
                wait_evacuated(act, u)
                act.sem_inc(sem("bu_ready"), 1)

            act.wait_ge(sem("CAm_cleared"), 1)
            act.wait_ge(sem("CA_ready"), 1)

            def cam(f):
                if f >= 2:
                    wait_filled(act, use[f"y{f - 2}"])
                for a in range(2):
                    rows = slice(a * ST, a * ST + ST)
                    for r in range(2):
                        A(CAm[rows, f % 2, r, :, :, a * GH:a * GH + GH], CA[rows, :, r, 4 * f:4 * f + 4, :], ACT.Copy)\
                            .then_inc(sem("CAm_ready"), 1)

            cam(0)
            for f in range(8):
                if f < 7:
                    cam(f + 1)
                u = use[f"y{f}"]
                if f >= 2:
                    act.wait_ge(sem("ylo_ready"), f - 1)
                wait_filled(act, u)
                A(tb[:, f % 2, :], acc[u % 2][:, 0:SEQ], ACT.Gelu_apprx_tanh).then_inc(*freed(u))
                wait_evacuated(act, u)
                A(xT_hi[:, f, :], tb[:, f % 2, :], ACT.Copy).then_inc(sem("yhi_ready"), 1)

            def glu(j, u):
                if j >= 2:
                    act.wait_ge(sem("glu_added"), j - 1)
                wait_filled(act, u)
                A(hbuf[:, j % 2], A2(u)[:, :, PN // 2:PN], ACT.Sigmoid).then_inc(sem("glu_gate"), 1)

            gemm("glu", glu)
            root("ffn0")
            tsplit("ffn0", *gain_of("ffn0"))
            ffn(0)
            root("kv")
            tsplit("kv", *gain_of("kv"))

            def kv(j, u):
                wait_filled(act, u)
                if j < 2:
                    ins = A(kT[:, 4 * j:4 * j + 4, :], A4(u), ACT.Copy)
                else:
                    ins = A(vn_[:, :, (j - 2) * PN:(j - 1) * PN], A2(u), ACT.Copy)
                ins.then_inc(*freed(u))

            gemm("kv", kv)
            tsplit("mix1", *gain_of("mix1"))
            gemm("q", lambda j, u: (wait_filled(act, u), A(qT[:, 4 * j:4 * j + 4, :], A4(u), ACT.Copy, scale=HD ** -0.5).then_inc(*freed(u))))

            for i in range(8):
                u = use["z"] + i
                wait_filled(act, u)
                v = acc[u % 2][:, :].rearrange("p (h n) -> p h n", h=2)[:, :, 0:SW]
                A(zS[:, 2 * i:2 * i + 2, :], v, ACT.Copy).then_inc(sem("z_ready"), 1)
                A(spS[:, 2 * i:2 * i + 2, :], v, ACT.Abs).then_inc(*freed(u))
                wait_evacuated(act, u)
                act.wait_ge(sem("z_ready"), i + 1)
                step(A(spS[:, 2 * i:2 * i + 2, :], spS[:, 2 * i:2 * i + 2, :], ACT.Exp, scale=-1.0))
            step.settle()
            for i in range(4):
                A(spS[:, 4 * i:4 * i + 4, :], spS[:, 4 * i:4 * i + 4, :], ACT.Ln, bias=1.0).then_inc(sem("ln_ready"), 1)
            for i in range(8):
                act.wait_ge(sem("logw_ready"), i + 1)
                A(zS[:, 2 * i:2 * i + 2, :], zS[:, 2 * i:2 * i + 2, :], ACT.Exp).then_inc(sem("wexp_ready"), 1)
            for j in range(2):
                u = use["oT"] + j
                wait_filled(act, u)
                A(xT_hi[:, 4 * j:4 * j + 4, :], A4(u), ACT.Copy).then_inc(sem("ohi_ready"), 1)
            gemm("o", lambda j, u: None)
            root("ffn1")
            tsplit("ffn1", *gain_of("ffn1"))
            ffn(1)
            root("final")
            tsplit("final", *gain_of("final"))
            for i in range(DEPTH):
                ffn(2 + 2 * i)
                root(f"ln0_{i}")
                tsplit(f"ln0_{i}", *gain_of(f"ln0_{i}"))

                def win(j, u):
                    if j < 2:
                        wait_filled(act, u)
                        A(qaT[:, 4 * j:4 * j + 4, :], A4(u), ACT.Copy, scale=HD ** -0.5).then_inc(*freed(u))
                    elif j == 2:
                        wait_filled(act, u)
                        for src in range(2):
                            for dst in range(2):
                                step(A(kaT[dst * HD:dst * HD + HD, src::2, :], A4(u)[src * HD:src * HD + HD, 0:2], ACT.Copy))
                        step.settle()
                        A(va[:, :, :], acc[u % 2][:, 512:1024].rearrange("p (t n) -> p t n", t=TT), ACT.Copy).then_inc(*freed(u))
                    else:
                        wait_filled(act, u)
                        for n in range(4):
                            c = 4 * (j - 3) + n
                            A(qkT[:, c, :], A4(u)[:, n], ACT.Copy, scale=cols[:, 4 + i, 3 * CONV_T + c:3 * CONV_T + c + 1]).then_inc(sem("tap4_ready"), 1)

                def conv_silu(j, u):
                    if 3 <= j < 9:
                        wait_evacuated(act, u)
                        c = slice(4 * (j - 3), 4 * (j - 3) + 4)
                        A(qkT[:, c, :], qkT[:, c, :], ACT.Silu).then_inc(sem("qkv_ready"), 1)

                gemm(f"win{i}", win, conv_silu, columns=SIDE)

                u = use[f"bd{i}"]
                wait_filled(act, u)
                b = acc[u % 2][:, 0:2 * TT * 8].rearrange("p (t n) -> p t n", t=TT)
                A(sm[:, 8], b[:, :, 0:8], ACT.Exp, scale=-1.0).then_inc(sem("beta_exp"), 1)
                act.wait_ge(sem("misc_in"), 96)
                step(A(sm[:, 9, 0, :], row[:, i, 0, :], ACT.Exp))
                act.wait_ge(sem("dt_raw"), i + 1)
                step(A(sm[:, 2], sm[:, 1], ACT.Abs))
                step.settle()
                step(A(sm[:, 2], sm[:, 2], ACT.Exp, scale=-1.0))
                step.settle()
                A(sm[:, 2], sm[:, 2], ACT.Ln, bias=1.0).then_inc(sem("dt_ln"), 1)

                def weights_exp(n):
                    act.wait_ge(sem("s_shifted"), 8 * i + n + 1)
                    A(zA[:, n % 2], zA[:, n % 2], ACT.Exp).then_inc(sem("s_exp"), 1)
                    A(red[:, 2, :], red[:, 2, :], ACT.Exp).then_inc(sem("s_exp"), 1)

                def attended(n):
                    u = use[f"oa{i}_{n}"]
                    wait_filled(act, u)
                    A(qaT[:, n, :], acc[u % 2][:, 0:SEQ], ACT.Copy).then_inc(*freed(u))

                def gate_columns(j):
                    for t in range(TT):
                        if j < 11:
                            to = sz[:, t, (j - 9) * PN:(j - 8) * PN]
                        else:
                            g, c = divmod(j - 11, 2)
                            to = gates[:, t, g, c * PN:(c + 1) * PN]
                        A(to, trp[2 + t][:, :], ACT.Silu if j < 11 else ACT.Sigmoid).then_inc(sem("gate_columns"), 1)

                for n in range(8 + 2):
                    if n < 8:
                        weights_exp(n)
                    if n >= 2:
                        attended(n - 2)
                    for j, last, p in side_panels(i, n):
                        act.wait_ge(panel_used, p + 1)
                        if last:
                            gate_columns(j)
                        split_hi(p + SPL)
                for h in range(2):
                    for n in range(2):
                        wait_evacuated(act, use[f"oa{i}_{4 * h + 2 + n}"])
                    A(xT_hi[:, 4 * h:4 * h + 4, :], qaT[:, 4 * h:4 * h + 4, :], ACT.Copy).then_inc(sem("ahi_ready"), 1)

                def squares(g):
                    sq = (kbg, ktl)[g % 2][:, :, :].rearrange("p h d -> p (h d)")
                    if g >= 2:
                        act.wait_ge(sem("qk_normed"), 4 * i + g - 1)
                    A(sq, qkT[:, 4 * g:4 * g + 4, :].rearrange("p c t -> p (c t)"), ACT.Square).then_inc(sem("squares"), 1)

                def inverse_norms(g):
                    sq = (kbg, ktl)[g % 2][:, :, :].rearrange("p h d -> p (h d)")
                    u = use[f"ss{i}{'ab'[g // 2]}"] + g % 2
                    wait_filled(act, u)
                    A(sq, acc[u % 2][:, :], ACT.Ln, bias=const(C_EPS, 1)).then_inc(*freed(u))
                    wait_evacuated(act, u)
                    A(sq, sq, ACT.Exp, scale=-0.5).then_inc(sem("inverse_norms"), 1)

                act.wait_ge(sem("qkv_ready"), 6 * (i + 1))
                squares(0)
                squares(1)
                act.wait_ge(sem("G_ready"), i + 1)
                step(A(sm[:, 5], sm[:, 4], ACT.Exp))
                A(sm[:, 7], sm[:, 7], ACT.Exp).then_inc(sem("G_exp"), 1)
                gemm(f"brA{i}_0", lambda j, u: None)
                for t in range(TT):
                    act.wait_ge(sem("decay_log"), TT * i + t + 1)
                    A(AT[:, t], AT[:, t], ACT.Exp).then_inc(sem("decay_exp"), 1)
                    A(L[:, t], L[:, t], ACT.Exp, scale=-1.0).then_inc(sem("decay_exp"), 1)
                inverse_norms(0)
                inverse_norms(1)
                squares(2)
                squares(3)
                gemm(f"brA{i}_1", lambda j, u: None)
                inverse_norms(2)
                inverse_norms(3)
                for lv in range(1, LEVELS):
                    for t in range(TT):
                        u = use[f"Y{i}_{lv}"] + t
                        wait_filled(act, u)
                        A(Yp[:, t], A8(u), ACT.Copy).then_inc(*freed(u))
                for d, to in ((0, Ti[:, 0]), (2, Xm[:, 1]), (3, Ti[:, 1])):
                    u = use[f"dl{i}"] + d
                    wait_filled(act, u)
                    A(to, A8(u), ACT.Copy).then_inc(*freed(u))
                for t in range(TT):
                    act.wait_ge(sem("o_raw"), TT * i + t + 1)
                    A(Yp[:, t], L[:, t], ACT.Square).then_inc(sem("o_squares"), 1)
                for t in range(TT):
                    act.wait_ge(sem("o_var"), TT * i + t + 1)
                    A(sm[:, 9, t], sm[:, 8, t], ACT.Sqrt).then_inc(sem("o_std"), 1)
                tsplit(f"delta_{i}")
                gemm(f"brB{i}", lambda j, u: None)
                tsplit(f"mixed_{i}")
                gemm(f"wo{i}", lambda j, u: None)
                root(f"ln1_{i}")
                tsplit(f"ln1_{i}", *gain_of(f"ln1_{i}"))
                ffn(3 + 2 * i)
                root(f"ln2_{i}")
                if i < DEPTH - 1:
                    tsplit(f"ln2_{i}", *gain_of(f"ln2_{i}"))

        @block.vector
        def _(dve):
            step = Steps(dve, "dve_steps")
            V_ = nc.vector

            def do(ins):
                step(ins)
                step.settle()

            def split_lo(p):
                if p >= n_panels:
                    return
                dve.wait_ge(hi_ready, p + 1)
                kt = panels[p][3]
                V_.tensor_tensor(w_lo[:, p % SPL, 0:kt, :], raw[:, p % RAW, 0:kt, :], w_hi[:, p % SPL, 0:kt, :].bitcast(F32),
                                 ALU.subtract).then_inc(lo_ready, 1)

            late = []

            def gemm(name, evacuate, after=None, hold=0, columns=None):
                last = gemms[name][:columns][-1][-1]
                for j, ps in enumerate(gemms[name][:columns]):
                    for p in ps[:-1]:
                        if p <= last - hold:
                            split_lo(p + SPL)
                    evacuate(j, use[name] + j)
                    if ps[-1] <= last - hold:
                        split_lo(ps[-1] + SPL)
                    if after:
                        after(j, use[name] + j)
                late.extend(range(last - hold + 1 + SPL, last + 1 + SPL))

            def late_splits():
                for p in late:
                    split_lo(p)
                late.clear()

            def statistics(c):
                for t in range(TT):
                    step(V_.bn_stats(stat[:, t, c, :], x[:, t, c * PN:c * PN + PN]))

            def norm(name, eps, center=False):
                step.settle()
                for t in range(TT):
                    step(V_.bn_aggr(mv[:, t, :], stat[:, t].rearrange("p c s -> p (c s)")))
                step.settle()
                if center:
                    V_.tensor_scalar(nrm[:, 0, :], mv[:, :, 1], eps, None, ALU.add).then_inc(sem("var_ready"), 1)
                else:
                    do(V_.tensor_tensor(nrm[:, 2, :], mv[:, :, 0], mv[:, :, 0], ALU.mult))
                    V_.scalar_tensor_tensor(nrm[:, 0, :], nrm[:, 2, :], eps, mv[:, :, 1], ALU.add, ALU.add).then_inc(sem("var_ready"), 1)
                dve.wait_ge(sem("std_ready"), norms[name] + 1)
                do(V_.reciprocal(nrm[:, 3, :], nrm[:, 1, :]))
                for t in range(TT):
                    if center:
                        ins = V_.tensor_scalar(xn[:, t, :], x[:, t, :], mv[:, t, 0:1], nrm[:, 3, t:t + 1], ALU.subtract, ALU.mult)
                    else:
                        ins = V_.tensor_scalar(xn[:, t, :], x[:, t, :], nrm[:, 3, t:t + 1], None, ALU.mult)
                    ins.then_inc(sem("xn_ready"), 1)

            def tsplit(name, gain=None, bias=None):
                for g in range(4):
                    n = 4 * tsplits[name] + g
                    dve.wait_ge(sem("xhi_ready"), 2 * n + 2)
                    tr = trp[n % TRP][:, :].rearrange("p (k t) -> p k t", k=2)
                    ks = slice(2 * g, 2 * g + 2)
                    if gain is None:
                        V_.tensor_tensor(xT_lo[:, ks, :], tr, xT_hi[:, ks, :].bitcast(F32), ALU.subtract).then_inc(sem("xlo_ready"), 2)
                        continue
                    if bias is not None:
                        dve.wait_ge(sem("xlo_ready"), 2 * n)
                        for k in range(2):
                            kk = 2 * g + k
                            step(V_.tensor_scalar(tb[:, k, :], tr[:, k], gain[:, kk:kk + 1], bias[:, kk:kk + 1], ALU.mult, ALU.add))
                        step.settle()
                        V_.tensor_tensor(xT_lo[:, ks, :], tb[:, :, :], xT_hi[:, ks, :].bitcast(F32), ALU.subtract).then_inc(sem("xlo_ready"), 2)
                        continue
                    for k in range(2):
                        kk = 2 * g + k
                        V_.scalar_tensor_tensor(xT_lo[:, kk, :], tr[:, k], gain[:, kk:kk + 1], xT_hi[:, kk, :].bitcast(F32),
                                                ALU.mult, ALU.subtract).then_inc(sem("xlo_ready"), 1)

            def add_to_x(scale=None, nat=None):
                def evacuate(j, u):
                    wait_filled(dve, u)
                    if nat is not None:
                        dve.wait_ge(sem("xnat_ready"), naturals[nat] + 1)
                    xs = x[:, :, j * PN:j * PN + PN]
                    if scale is None:
                        ins = V_.tensor_tensor(xs, xs, A2(u), ALU.add)
                    else:
                        ins = V_.scalar_tensor_tensor(xs, xs, scale, A2(u), ALU.mult, ALU.add)
                    ins.then_inc(*freed(u))
                    wait_evacuated(dve, u)
                    statistics(j)
                return evacuate

            def ffn(f, scale=None, nat=None):
                def gate(j, u):
                    hn = f * 11 + j
                    h = hbuf[:, hn % 2]
                    if f < 2:
                        for n in range(2):
                            c = 2 * j + n
                            dve.wait_ge(sem("tap_ready"), 2 * hn + 2)
                            do(V_.scalar_tensor_tensor(h[:, n, 1:], A4(u)[:, n, 0:SEQ - 1], cols[:, 2 + f, FT + c:FT + c + 1], h[:, n, 1:], ALU.mult, ALU.add))
                            V_.scalar_tensor_tensor(h[:, n, 2:], A4(u)[:, n, 0:SEQ - 2], cols[:, 2 + f, c:c + 1], h[:, n, 2:], ALU.mult, ALU.add)\
                                .then_inc(sem("conv_ready"), 1)
                    dve.wait_ge(sem("gate_ready"), hn + 1)
                    V_.tensor_tensor(h, h, A4(u)[:, 2:4], ALU.mult).then_inc(*freed(u))

                def hidden(j, u):
                    hn = f * 11 + j
                    dve.wait_ge(sem("hhi_ready"), hn + 1)
                    ts_ = slice(2 * j, 2 * j + 2)
                    V_.tensor_tensor(hT_lo[:, ts_, :], hbuf[:, hn % 2], hT_hi[:, ts_, :].bitcast(F32), ALU.subtract).then_inc(sem("hlo_ready"), 1)

                gemm(f"up{f}", gate, hidden)
                gemm(f"down{f}", add_to_x(scale, nat), hold=2)

            dve.wait_ge(sem("x_in"), 16)
            statistics(0)
            statistics(1)
            norm("mix0", EPS)
            split_lo(0)
            tsplit("mix0", *gain_of("mix0"))
            for p in range(1, SPL):
                split_lo(p)
            dve.wait_ge(sem("den_ready"), 1)
            V_.reciprocal(s_(19), s_(19)).then_inc(sem("inv_ready"), 1)
            dve.wait_ge(sem("bdw_hi_ready"), 1)
            V_.tensor_tensor(bdw_lo[:, :, :, :], bdw[:, :, :, :], bdw_hi[:, :, :, :].bitcast(F32), ALU.subtract).then_inc(sem("bdw_ready"), 1)
            gemm("ssm_in0", lambda j, u: None)

            dve.wait_ge(sem("pT_ready"), 1)
            dve.wait_ge(sem("ssm_b_in"), 32)
            t = [tmpv[:, i // 2, (i % 2) * 512:(i % 2) * 512 + 512].rearrange("p (k h) -> p k h", h=GH) for i in range(4)]
            for i, (r, f) in enumerate([(0, 7), (1, 8), (1, 7), (0, 8)]):
                step(V_.tensor_tensor(t[i], b_n[:, r], bc(pT[:, f, :], 2, GH), ALU.mult))
            step.settle()
            dve.wait_ge(sem("powers_ready"), 1)
            for a in range(2):
                rows = slice(a * ST, a * ST + ST)
                for r in range(2):
                    V_.tensor_tensor(Bm[rows, r, :, a * GH:a * GH + GH], t[2 * r][rows], t[2 * r + 1][rows],
                                     ALU.add if r else ALU.subtract).then_inc(sem("Bm_ready"), 1)
            dve.wait_ge(sem("Bm_ready"), 4)
            wait_filled(dve, use["CT"] + 1)
            for r in range(2):
                t = [tmpv[:, i, :].rearrange("p (k c) -> p k c", c=32) for i in range(2)]
                step(V_.tensor_tensor(t[0], Bm[:, r], bc(pT[:, 0, :], 2, 32), ALU.mult))
                do(V_.tensor_tensor(t[1], Bm[:, 1 - r], bc(pT[:, 1 + r, :], 2, 32), ALU.mult))
                ins = V_.tensor_tensor(BAm[:, r], t[0], t[1], ALU.add)
                if r == 0:
                    do(ins)
                else:
                    ins.then_inc(sem("BAm_ready"), 1)
            gemm("ssm_in1", lambda j, u: None)
            t1, t2 = tmpp[:, 0], tmpp[:, 1]
            for b in range(8):
                k = slice(4 * b, 4 * b + 4)
                dve.wait_ge(sem("bu_ready"), 2 * (b + 1))
                v = V[:, :, k, :]
                added = bu[:, b % 2].rearrange("p r k (c j) -> p r k c j", j=Q // 2)
                for j in range(1, Q // 2):
                    src = added[:, :, :, :, 0] if j == 1 else v
                    step(V_.tensor_tensor(t1, src, bc(bc(pT[:, 9, k], 1, 2), 3, NC_), ALU.mult))
                    for r in range(2):
                        step(V_.tensor_tensor(t2[:, r], src[:, 1 - r], bc(pT[:, 10 + r, k], 2, NC_), ALU.mult))
                    step.settle(2)
                    step(V_.tensor_tensor(t1, t1, added[:, :, :, :, j], ALU.add))
                    step.settle()
                    ins = V_.tensor_tensor(v, t1, t2, ALU.add)
                    if j < Q // 2 - 1:
                        do(ins)
                    else:
                        ins.then_inc(sem("chunks_done"), 1)
                dve.wait_ge(sem("chunks_done"), b + 1)
            step(V_.memset(E[:, :, :, 0], 0.0))
            do(V_.tensor_copy(E[:, :, :, 1], V[:, :, :, 0]))
            t1, t2 = (tmpp[:, i].rearrange("p r k c -> p r (k c)")[:, :, 0:PAIRS] for i in range(2))
            for c in range(2, NC_):
                e = E[:, :, :, c - 1]
                step(V_.tensor_tensor(t1, e, bc(pT[:, 4, :], 1, 2), ALU.mult))
                step(V_.tensor_tensor(t2, E[:, ::-1, :, c - 1], pT[:, 5:7, :], ALU.mult))
                step.settle(1)
                do(V_.tensor_tensor(t1, t1, V[:, :, :, c - 1], ALU.add))
                ins = V_.tensor_tensor(E[:, :, :, c], t1, t2, ALU.add)
                if c < NC_ - 1:
                    do(ins)
                else:
                    ins.then_inc(sem("scan_done"), 1)

            def block_diagonal(f):
                u = use[f"K{f}"]
                if f >= 2:
                    wait_filled(dve, use[f"y{f - 2}"])
                wait_filled(dve, u)
                k = acc[u % 2][:, 0:P].rearrange("p (j h) -> p j h", j=Q)
                o = Kbd[:, f % 2].rearrange("p j (g h) -> p j g h", g=8)
                mask = bc(bc(const(C_PAIR, 8), 1, Q), 3, GH)
                V_.tensor_tensor(o, bc(k, 2, 8), mask, ALU.mult).then_inc(*freed(u))
                wait_evacuated(dve, u)
                V_.scalar_tensor_tensor(Kbd[:, f % 2, 0, :], ident, cols[:, 0, 40 + f:41 + f], Kbd[:, f % 2, 0, :], ALU.mult, ALU.add)\
                    .then_inc(sem("Kbd_ready"), 1)

            block_diagonal(0)
            for f in range(8):
                if f < 7:
                    block_diagonal(f + 1)
                dve.wait_ge(sem("yhi_ready"), f + 1)
                V_.tensor_tensor(xT_lo[:, f, :], tb[:, f % 2, :], xT_hi[:, f, :].bitcast(F32), ALU.subtract).then_inc(sem("ylo_ready"), 1)

            def glu(j, u):
                dve.wait_ge(sem("glu_gate"), j + 1)
                h = hbuf[:, j % 2]
                V_.tensor_tensor(h, h, A2(u)[:, :, 0:PN // 2], ALU.mult).then_inc(*freed(u))
                wait_evacuated(dve, u)
                xs = x[:, :, j * PN // 2:(j + 1) * PN // 2]
                V_.tensor_tensor(xs, xs, h, ALU.add).then_inc(sem("glu_added"), 1)
                if j % 2:
                    dve.wait_ge(sem("glu_added"), j + 1)
                    statistics(j // 2)

            gemm("glu", glu, hold=2)
            norm("ffn0", EPS)
            tsplit("ffn0", *gain_of("ffn0"))
            late_splits()
            ffn(0)
            norm("kv", EPS)
            tsplit("kv", *gain_of("kv"))
            late_splits()
            gemm("kv", lambda j, u: None)
            tsplit("mix1", *gain_of("mix1"))
            gemm("q", lambda j, u: None)

            def diagonal(t, hs):
                return t[:, hs, :].rearrange("p h (b q) -> p h b q", b=3)[:, :, 0::2, :]

            for i in range(4):
                hs = slice(4 * i, 4 * i + 4)
                dve.wait_ge(sem("ln_ready"), i + 1)
                dve.wait_ge(sem("z_ready"), 2 * i + 2)
                do(V_.scalar_tensor_tensor(spS[:, hs, :], zS[:, hs, :], 0.0, spS[:, hs, :], ALU.max, ALU.add))
                do(V_.tensor_tensor(zS[:, hs, :], zS[:, hs, :], spS[:, hs, :], ALU.subtract))
                V_.tensor_tensor(diagonal(spS, hs), diagonal(spS, hs), bc(bc(const(C_LT), 1, 2), 1, 4), ALU.mult).then_inc(sem("sp_ready"), 1)
            for i in range(8):
                u = use["rem"] + i
                hs = slice(2 * i, 2 * i + 2)
                wait_filled(dve, u)
                v = acc[u % 2][:, :].rearrange("p (h n) -> p h n", h=2)[:, :, 0:SW]
                V_.tensor_tensor(zS[:, hs, :], zS[:, hs, :], v, ALU.subtract).then_inc(*freed(u))
                wait_evacuated(dve, u)
                V_.tensor_copy(mv[:, 0, 0:1], zS[:, 2 * i, 0:1]).then_inc(sem("logw_ready"), 1)
            for i in range(8):
                hs = slice(2 * i, 2 * i + 2)
                dve.wait_ge(sem("wexp_ready"), i + 1)
                V_.tensor_tensor(diagonal(zS, hs), diagonal(zS, hs), bc(bc(const(C_LT), 1, 2), 1, 2), ALU.mult).then_inc(sem("w_ready"), 1)
            for j in range(2):
                u = use["oT"] + j
                dve.wait_ge(sem("ohi_ready"), j + 1)
                V_.tensor_tensor(xT_lo[:, 4 * j:4 * j + 4, :], A4(u), xT_hi[:, 4 * j:4 * j + 4, :].bitcast(F32), ALU.subtract).then_inc(*freed(u))
            gemm("o", add_to_x(), hold=2)
            norm("ffn1", EPS)
            tsplit("ffn1", *gain_of("ffn1"))
            late_splits()
            ffn(1)
            norm("final", EPS)
            tsplit("final", *gain_of("final"))
            late_splits()
            for i in range(DEPTH):
                last = "final" if i == 0 else f"ln2_{i - 1}"
                ffn(2 + 2 * i, 2 * ALPHA, last)
                norm(f"ln0_{i}", 4 * LN_EPS, True)
                tsplit(f"ln0_{i}", *gain_of(f"ln0_{i}"))
                late_splits()

                def short_conv(j, u):
                    if not 3 <= j < 9:
                        return
                    dve.wait_ge(sem("tap4_ready"), 4 * (6 * i + j - 2))
                    for back in (1, 2, 3):
                        for n in range(4):
                            c = 4 * (j - 3) + n
                            w = (3 - back) * CONV_T + c
                            ins = V_.scalar_tensor_tensor(qkT[:, c, back:], A4(u)[:, n, 0:SEQ - back], cols[:, 4 + i, w:w + 1],
                                                          qkT[:, c, back:], ALU.mult, ALU.add)
                            if back < 3 or n < 3:
                                step(ins)
                        if back < 3:
                            step.settle()
                    step.settle()
                    ins.then_inc(*freed(u))

                gemm(f"win{i}", short_conv, columns=SIDE)

                u = use[f"bd{i}"]
                b = acc[u % 2][:, 0:2 * TT * 8].rearrange("p (t n) -> p t n", t=TT)
                dve.wait_ge(sem("beta_exp"), i + 1)
                dve.wait_ge(sem("misc_in"), 96)
                V_.tensor_tensor(sm[:, 1], b[:, :, 8:16], bc(row[:, i, 1, :], 1, TT), ALU.add).then_inc(*freed(u))
                wait_evacuated(dve, u)
                dve.sem_inc(sem("dt_raw"), 1)
                do(V_.tensor_scalar(sm[:, 8], sm[:, 8], 1.0, None, ALU.add))
                step(V_.reciprocal(sm[:, 0], sm[:, 8]))
                dve.wait_ge(sem("dt_ln"), i + 1)
                do(V_.scalar_tensor_tensor(sm[:, 3], sm[:, 1], 0.0, sm[:, 2], ALU.max, ALU.add))
                V_.scalar_tensor_tensor(sm[:, 3], sm[:, 3], -1.0, bc(sm[:, 9, 0, :], 1, TT), ALU.mult, ALU.mult).then_inc(sem("g_ready"), 1)

                def scores(n):
                    u = use[f"s{i}_{n}"]
                    v = acc[u % 2][:, :].rearrange("p (h b k) -> p h b k", h=2, b=4)
                    hs = slice(2 * n, 2 * n + 2)
                    z, zp = zA[:, n % 2], zB[:, n % 2]
                    if n >= 2:
                        dve.wait_ge(sem("s_turned"), 8 * i + n - 1)
                    wait_filled(dve, u)
                    step(V_.tensor_tensor(z, v[:, :, 0:3:2, :], bc(biasL[:, hs, :], 2, 2), ALU.add))
                    step.settle()
                    V_.tensor_tensor(zp, v[:, :, 1, :], biasU[:, hs, :], ALU.add).then_inc(*freed(u))
                    wait_evacuated(dve, u)
                    do(V_.tensor_tensor(z[:, :, 1, :], z[:, :, 1, :], zp, ALU.max))
                    do(V_.tensor_reduce(red[:, 0, :].rearrange("p (h b) -> p h b", h=2), z, AX_X, ALU.max))
                    r = [red[:, q, :].rearrange("p (h b) -> p h b", h=2) for q in range(4)]
                    sink = bc(snk[:, i, hs], 2, 2)
                    do(V_.tensor_tensor(r[1], r[0], sink, ALU.max))
                    do(V_.tensor_tensor(r[2], sink, r[1], ALU.subtract))
                    V_.tensor_tensor(z, z, bc(r[1], 3, P), ALU.subtract).then_inc(sem("s_shifted"), 1)

                def normalize(n):
                    z = zA[:, n % 2]
                    r = [red[:, q, :].rearrange("p (h b) -> p h b", h=2) for q in range(4)]
                    dve.wait_ge(sem("s_exp"), 2 * (8 * i + n + 1))
                    do(V_.tensor_reduce(r[0], z, AX_X, ALU.add))
                    do(V_.tensor_tensor(r[0], r[0], r[2], ALU.add))
                    do(V_.reciprocal(r[3], r[0]))
                    V_.tensor_tensor(z, z, bc(r[3], 3, P), ALU.mult).then_inc(sem("s_normed"), 1)

                def mask_turned(n):
                    tr = trp[n % 2][:, :].rearrange("p (h b q) -> p h b q", h=2, b=2)
                    dve.wait_ge(sem("s_turned"), 8 * i + n + 1)
                    if n >= 1:
                        wait_filled(dve, use[f"oa{i}_{n - 1}"])
                    step(V_.tensor_tensor(pT3[:, :, 0::2, :], tr, bc(bc(const(C_LE), 1, 2), 1, 2), ALU.mult))
                    step.settle()
                    V_.tensor_tensor(pT3[:, :, 1, :], tr[:, :, 1, :], bc(const(C_GT), 1, 2), ALU.mult).then_inc(sem("pT3_ready"), 1)

                dve.wait_ge(sem("bias_ready"), i + 1)
                for n in range(8 + 2):
                    if n < 8:
                        scores(n)
                    if 1 <= n < 9:
                        mask_turned(n - 1)
                    if n < 8:
                        normalize(n)
                    for j, last, p in side_panels(i, n):
                        split_lo(p + SPL)
                for h in range(2):
                    dve.wait_ge(sem("ahi_ready"), 2 * i + h + 1)
                    hs = slice(4 * h, 4 * h + 4)
                    V_.tensor_tensor(xT_lo[:, hs, :], qaT[:, hs, :], xT_hi[:, hs, :].bitcast(F32), ALU.subtract).then_inc(sem("alo_ready"), 1)

                def gate_a(j):
                    def evacuate(_, u):
                        wait_filled(dve, u)
                        g = gates[:, :, 0, j * PN:(j + 1) * PN]
                        dve.wait_ge(sem("gate_columns"), 12 * (i + 1))
                        V_.tensor_tensor(g, g, A2(u), ALU.mult).then_inc(*freed(u))
                    return evacuate

                u = use[f"G{i}"]
                wait_filled(dve, u)
                v = acc[u % 2][:, 0:32].rearrange("p (q t h) -> p q t h", q=2, t=TT)
                do(V_.tensor_copy(sm[:, 4], v[:, 0]))
                V_.tensor_tensor(sm[:, 7], v[:, 1], sm[:, 4], ALU.subtract).then_inc(*freed(u))
                wait_evacuated(dve, u)
                dve.sem_inc(sem("G_ready"), 1)
                gemm(f"brA{i}_0", gate_a(0))
                for t in range(TT):
                    u = use[f"Gr{i}"] + t
                    wait_filled(dve, u)
                    V_.tensor_tensor(L[:, t], A8(u), bc(sm[:, 4, t, :], 2, P), ALU.subtract).then_inc(*freed(u))
                    wait_evacuated(dve, u)
                    do(V_.tensor_scalar(AT[:, t], L[:, t], 0.0, None, ALU.min))
                    V_.tensor_scalar(L[:, t], L[:, t], 0.0, None, ALU.max).then_inc(sem("decay_log"), 1)
                dve.wait_ge(sem("G_exp"), i + 1)
                do(V_.scalar_tensor_tensor(sm[:, 6], sm[:, 0], -1.0, sm[:, 5], ALU.mult, ALU.mult))
                def unit(g):
                    sq = (kbg, ktl)[g % 2][:, :, :].rearrange("p h d -> p (h d)")
                    qk = qkT[:, 4 * g:4 * g + 4, :].rearrange("p c t -> p (c t)")
                    dve.wait_ge(sem("inverse_norms"), 4 * i + g + 1)
                    V_.scalar_tensor_tensor(qk, qk, DK ** -0.5 if g < 2 else 1.0, sq, ALU.mult, ALU.mult).then_inc(sem("qk_normed"), 1)

                unit(0)
                unit(1)
                gemm(f"brA{i}_1", gate_a(1))
                unit(2)
                unit(3)
                for n, (to, by) in enumerate([(vb[:, 0], sm[:, 0, 0]), (vb[:, 1], sm[:, 0, 1]), (ktl[:, :, :], sm[:, 7, 0]), (kbg[:, :, :], sm[:, 6, 1])]):
                    u = use[f"nat{i}"] + n
                    if n == 0:
                        dve.wait_ge(sem("xnat_ready"), naturals[f"ln0_{i}"] + 1)
                    wait_filled(dve, u)
                    V_.tensor_tensor(to, A8(u), bc(by, 2, P), ALU.mult).then_inc(*freed(u))
                for n, m in (("kk", L), ("qk", AT)):
                    for t in range(TT):
                        u = use[f"{n}{i}"] + t
                        wait_filled(dve, u)
                        dve.wait_ge(sem("decay_ready"), 2 * (TT * i + TT))
                        V_.tensor_tensor(m[:, t], A8(u), m[:, t], ALU.mult).then_inc(*freed(u))
                dve.wait_ge(sem("inverse_init"), 4 * (i + 1))
                for t in range(TT):
                    u = use[f"Y{i}_0"] + t
                    wait_filled(dve, u)
                    V_.tensor_tensor(U[:, t], U[:, t], A8(u), ALU.subtract).then_inc(*freed(u))
                dve.wait_ge(sem("Ti_pairs"), TT * (i + 1))
                for lv in range(1, LEVELS):
                    for t in range(TT):
                        for name, m, side in (("ZU", U, 1), ("ZT", Ti, 0)):
                            if f"{name}{i}_{lv}_{t}" in use:
                                u = use[f"{name}{i}_{lv}_{t}"]
                                wait_filled(dve, u)
                                wait_evacuated(dve, doubled(i, lv - 1, t, name))
                                part = blocks(m[:, t].rearrange("p h c -> p (h c)"), lv, side)
                                v = acc[u % 2][:, 0:512].rearrange("p (m b) -> p m b", b=1 << lv)
                                V_.tensor_tensor(part, part, v, ALU.subtract).then_inc(*freed(u))
                u = use[f"dl{i}"] + 1
                wait_filled(dve, u)
                V_.tensor_copy(Xm[:, 0], A8(u)).then_inc(*freed(u))
                u = use[f"dl{i}"] + 4
                wait_filled(dve, u)
                V_.tensor_copy(L[:, 0], A8(u)).then_inc(*freed(u))
                wait_evacuated(dve, u)
                dve.sem_inc(sem("o_raw"), 1)
                wait_filled(dve, u + 1)
                V_.tensor_tensor(L[:, 1], A8(u + 1), bc(sm[:, 5, 1], 2, P), ALU.mult).then_inc(*freed(u + 1))
                wait_evacuated(dve, u + 1)
                wait_filled(dve, u + 2)
                V_.tensor_tensor(L[:, 1], L[:, 1], A8(u + 2), ALU.add).then_inc(*freed(u + 2))
                wait_evacuated(dve, u + 2)
                dve.sem_inc(sem("o_raw"), 1)
                for t in range(TT):
                    dve.wait_ge(sem("o_squares"), TT * i + t + 1)
                    do(V_.tensor_reduce(sm[:, 10, t], Yp[:, t], AX_X, ALU.add))
                    V_.tensor_scalar(sm[:, 8, t], sm[:, 10, t], 1 / DK, NORM_EPS, ALU.mult, ALU.add).then_inc(sem("o_var"), 1)
                dve.wait_ge(sem("sz_ready"), i + 1)
                for t in range(TT):
                    dve.wait_ge(sem("o_std"), TT * i + t + 1)
                    do(V_.reciprocal(sm[:, 11, t], sm[:, 9, t]))
                    do(V_.tensor_tensor(L[:, t], L[:, t], bc(sm[:, 11, t], 2, P), ALU.mult))
                    V_.tensor_tensor(L[:, t], L[:, t], sz[:, t].rearrange("p (h d) -> p h d", d=DK), ALU.mult).then_inc(sem("o_ready"), 1)
                tsplit(f"delta_{i}")

                def gate_b(j, u):
                    wait_filled(dve, u)
                    g = gates[:, :, 1, j * PN:(j + 1) * PN]
                    V_.tensor_tensor(g, g, A2(u), ALU.mult).then_inc(*freed(u))
                    wait_evacuated(dve, u)
                    wait_evacuated(dve, use[f"brA{i}_{j}"])
                    ga = gates[:, :, 0, j * PN:(j + 1) * PN]
                    V_.tensor_tensor(ga, ga, g, ALU.add).then_inc(sem("mix_ready"), 1)

                gemm(f"brB{i}", gate_b)
                tsplit(f"mixed_{i}")
                gemm(f"wo{i}", add_to_x(ALPHA, f"ln0_{i}"), hold=2)
                norm(f"ln1_{i}", LN_EPS, True)
                tsplit(f"ln1_{i}", *gain_of(f"ln1_{i}"))
                late_splits()
                ffn(3 + 2 * i, 2 * ALPHA, f"ln1_{i}")
                norm(f"ln2_{i}", 4 * LN_EPS, True)
                if i < DEPTH - 1:
                    tsplit(f"ln2_{i}", *gain_of(f"ln2_{i}"))
                    late_splits()

        @block.tensor
        def _(pe):
            mm = nc.tensor.matmul

            def claim(u):
                if u >= 2:
                    pe.wait_ge(acc_freed[u % 2], u // 2)
                return acc[u % 2]

            def product(out, pairs, first, last):
                (ah, al), (bh, bl) = pairs
                mm(out, ah, bh, start=first, stop=False, skip_group_check=True)
                mm(out, ah, bl, start=False, stop=False, skip_group_check=True)
                return mm(out, al, bh, start=False, stop=last, skip_group_check=True)

            def features(name, j, u, src, n0=0, n1=4, ready=None):
                out = A4(u)
                claim(u)
                for i, p in enumerate(gemms[name][j]):
                    pe.wait_ge(lo_ready, p + 1)
                    _, _, k0, kt, _ = panels[p]
                    if ready and j == 0:
                        ready(k0, kt)
                    for n in range(n0, n1):
                        for k in range(kt):
                            c = slice(n * P, n * P + P)
                            w = (w_hi[:, p % SPL, k, c], w_lo[:, p % SPL, k, c])
                            a = (src[0][:, k0 + k, :], src[1][:, k0 + k, :])
                            ins = product(out[:, n], (w, a), i == 0 and k == 0 and n % 2 == 0, i == len(gemms[name][j]) - 1 and k == kt - 1)
                    if n1 == 4:
                        ins.then_inc(panel_used, 1)
                    else:
                        values(name, j, u, src, p, i)

            def values(name, j, u, src, p, i):
                out = acc[u % 2][:, 512:1024].rearrange("p (t n) -> p t n", t=TT)
                _, _, k0, kt, _ = panels[p]
                for t in range(TT):
                    for k in range(kt):
                        tok = slice(t * P, t * P + P)
                        a = (src[0][:, k0 + k, tok], src[1][:, k0 + k, tok])
                        w = (w_hi[:, p % SPL, k, 256:512], w_lo[:, p % SPL, k, 256:512])
                        ins = product(out[:, t], (a, w), i == 0 and k == 0 and t == 0, i == len(gemms[name][j]) - 1 and k == kt - 1)
                ins.then_inc(panel_used, 1)

            def tokens(name, j, u, src, ready=None):
                out = A2(u)
                claim(u)
                for i, p in enumerate(gemms[name][j]):
                    pe.wait_ge(lo_ready, p + 1)
                    _, _, k0, kt, _ = panels[p]
                    if ready and j == 0:
                        ready(k0, kt)
                    for k in range(kt):
                        for t in range(TT):
                            tok = slice(t * P, t * P + P)
                            a = (src[0][:, k0 + k, tok], src[1][:, k0 + k, tok])
                            w = (w_hi[:, p % SPL, k, :], w_lo[:, p % SPL, k, :])
                            ins = product(out[:, t], (a, w), i == 0 and k == 0, i == len(gemms[name][j]) - 1 and k == kt - 1)
                    ins.then_inc(panel_used, 1)

            xT, hT = (xT_hi, xT_lo), (hT_hi, hT_lo)

            def xT_ready(name):
                return lambda k0, kt: pe.wait_ge(sem("xlo_ready"), 8 * tsplits[name] + k0 + kt)

            def turn(name, src, ready, value):
                pe.wait_ge(sem(ready), value)
                for g in range(4):
                    n = 4 * tsplits[name] + g
                    if n >= TRP:
                        pe.wait_ge(sem("xlo_ready"), 2 * (n - TRP + 1))
                    for k in range(2):
                        for t in range(TT):
                            ins = nc.tensor.transpose(trp[n % TRP][:, (2 * k + t) * P:(2 * k + t + 1) * P],
                                                      src[:, t, (2 * g + k) * P:(2 * g + k + 1) * P], ident)
                    ins.then_inc(sem("turned"), 1)

            def turn_norm(norm_name, name=None):
                turn(name or norm_name, xn, "xn_ready", TT * (norms[norm_name] + 1))

            def ffn(f, xname):
                for j in range(11):
                    features(f"up{f}", j, use[f"up{f}"] + j, xT, ready=xT_ready(xname))
                for j in range(2):
                    tokens(f"down{f}", j, use[f"down{f}"] + j, hT,
                           lambda k0, kt: pe.wait_ge(sem("hlo_ready"), f * 11 + (k0 + kt) // 2))

            pe.wait_ge(sem("const_in"), 16)
            pe.wait_ge(sem("cols_in"), 16 * sum(len(t) for t in COLUMN_TILES[:2]))
            pe.wait_ge(sem("conv_cols_in"), 16 * len(COLUMN_TILES[2:]))
            a = claim(use["cols"])
            for i, parts in enumerate(COLUMN_TILES):
                n = sum(q[1] for q in parts)
                ins = nc.tensor.transpose(a[:, i * P:i * P + n], stage[0:n, i, :], cst[0:n, C_ID:C_ID + n])
            ins.then_inc(acc_ready, 1)
            turn_norm("mix0")
            pe.wait_ge(sem("ssm_c_in"), 64)
            for r in range(2):
                a = claim(use["CT"] + r)
                for f in range(8):
                    ins = nc.tensor.transpose(a[:, f * P:f * P + P], c_n[:, r, f].rearrange("p a b -> p (a b)"), ident)
                ins.then_inc(acc_ready, 1)
            pe.wait_ge(sem("misc_in"), 96)
            a = claim(use["ftab"])
            mm(a[0:HEADS, 0:P], relb[:, :], bsel[:, :], start=True, stop=True).then_inc(acc_ready, 1)
            features("ssm_in0", 0, use["ssm_in0"], xT, ready=xT_ready("mix0"))
            pe.wait_ge(sem("powers_ready"), 1)
            a = claim(use["pT"])
            for at, q in enumerate([*range(9), 20, 21, 22]):
                ins = nc.tensor.transpose(a[:, at * PAIRS:(at + 1) * PAIRS], pn[:, q, :], cst[0:PAIRS, C_ID:C_ID + PAIRS])
            ins.then_inc(acc_ready, 1)
            features("ssm_in1", 0, use["ssm_in1"], xT)
            pe.wait_ge(sem("Bm_ready"), 4)
            for j in range(4):
                a = claim(use["BT"] + j)
                if j == 2:
                    pe.wait_ge(sem("BAm_ready"), 1)
                for f in range(4):
                    for r in range(2):
                        k = 16 * (j % 2) + 4 * f
                        ins = nc.tensor.transpose(a[:, (2 * f + r) * P:(2 * f + r + 1) * P],
                                                  (Bm, BAm)[j // 2][:, r, k:k + 4, :].rearrange("p k c -> p (k c)"), ident)
                ins.then_inc(acc_ready, 1)
            wait_evacuated(pe, use["ssm_in0"])
            wait_evacuated(pe, use["ssm_in1"])
            pe.wait_ge(sem("BT_ready"), 4)
            for r in range(16):
                u = use["bu"] + r
                claim(u)
                a = acc[u % 2][:, :].rearrange("p (k r t) -> p r k t", r=4, k=2)
                for k in range(2):
                    pair = 2 * r + k
                    rows = slice(32 * (pair % 4), 32 * (pair % 4) + 32)
                    for c in range(2):
                        for lag in (1, 0):
                            ins = mm(a[:, c, k], BT[rows, lag, pair // 4, c, :], uT[rows, pair // 4, 1 - lag::2],
                                     start=lag == 1, stop=lag == 0, skip_group_check=True)
                ins.then_inc(acc_ready, 1)

            def response(f):
                a = claim(use[f"K{f}"])
                for k in range(4):
                    pair = 4 * f + k
                    o = a[32 * k:32 * k + 32, 0:P].rearrange("p (j h) -> p j h", j=Q)
                    for r in range(2):
                        mm(o[:, 0], Bm[:, r, pair, :], CT[:, r, pair, :], start=r == 0, stop=r == 1, skip_group_check=True)
                        ins = mm(o[:, 1:Q], Bm[:, r, pair, :], CA[:, 0:Q - 1, r, pair, :], start=False, stop=r == 1, skip_group_check=True)
                ins.then_inc(acc_ready, 1)

            pe.wait_ge(sem("CA_ready"), 1)
            response(0)
            for f in range(8):
                if f < 7:
                    response(f + 1)
                u = use[f"y{f}"]
                claim(u)
                y = acc[u % 2][:, 0:SEQ].rearrange("p (c j) -> p c j", j=Q)
                uc = uT[:, f, :].rearrange("p (c j) -> p c j", j=Q)
                pe.wait_ge(sem("Kbd_ready"), f + 1)
                for j in range(Q):
                    mm(y[:, :, j:Q], Kbd[:, f % 2, j, :], uc[:, :, 0:Q - j], start=j == 0, stop=False, skip_group_check=True)
                pe.wait_ge(sem("CAm_ready"), 4 * (f + 1))
                pe.wait_ge(sem("scan_done"), 1)
                for k in range(4):
                    for j in range(Q):
                        for r in range(2):
                            ins = mm(y[32 * k:32 * k + 32, :, j], CAm[:, f % 2, r, j, k, :], E[:, r, 4 * f + k, :], start=False,
                                     stop=r == 1, skip_group_check=True)
                ins.then_inc(acc_ready, 1)
            pe.wait_ge(sem("ylo_ready"), 8)
            for j in range(4):
                tokens("glu", j, use["glu"] + j, xT)
            turn_norm("ffn0")
            ffn(0, "ffn0")
            turn_norm("kv")
            for j in range(2):
                features("kv", j, use["kv"] + j, xT, ready=xT_ready("kv"))
            for j in range(2, 4):
                tokens("kv", j, use["kv"] + j, xT)
            turn_norm("kv", "mix1")
            for j in range(2):
                features("q", j, use["q"] + j, xT, ready=xT_ready("mix1"))

            wait_evacuated(pe, use["q"])
            wait_evacuated(pe, use["q"] + 1)
            for i in range(8):
                u = use["z"] + i
                a = claim(u)
                for h in range(2):
                    rows = slice(HD * h, HD * h + HD)
                    mm(a[:, h * 512:h * 512 + SEQ], kT[rows, i, 0:P], qT[rows, i, :], start=True, stop=True, skip_group_check=True)
                    ins = mm(a[:, h * 512 + SEQ:h * 512 + SW], kT[rows, i, P:SEQ], qT[rows, i, P:SEQ], start=True, stop=True, skip_group_check=True)
                ins.then_inc(acc_ready, 1)
            for i in range(8):
                u = use["rem"] + i
                a = claim(u)
                pe.wait_ge(sem("sp_ready"), i // 2 + 1)
                for h in range(2):
                    s0 = spS[:, 2 * i + h, :]
                    mm(a[:, h * 512:h * 512 + SEQ], const(C_GT), s0[:, 0:SEQ], start=True, stop=False, skip_group_check=True)
                    mm(a[:, h * 512 + P:h * 512 + SEQ], const(C_ONE), s0[:, SEQ:SW], start=False, stop=True, skip_group_check=True)
                    ins = mm(a[:, h * 512 + SEQ:h * 512 + SW], const(C_GT), s0[:, SEQ:SW], start=True, stop=True, skip_group_check=True)
                ins.then_inc(acc_ready, 1)
            for j in range(2):
                u = use["oT"] + j
                a = claim(u)
                for i in range(4 * j, 4 * j + 4):
                    pe.wait_ge(sem("w_ready"), i + 1)
                    for h in range(2):
                        head = 2 * i + h
                        o = a[HD * h:HD * h + HD, (i % 4) * SEQ:(i % 4 + 1) * SEQ]
                        d = slice(head * HD, head * HD + HD)
                        mm(o, vn_[:, 0, d], zS[:, head, 0:SEQ], start=True, stop=False, skip_group_check=True)
                        ins = mm(o[:, P:SEQ], vn_[:, 1, d], zS[:, head, SEQ:SW], start=False, stop=True, skip_group_check=True)
                ins.then_inc(acc_ready, 1)
            wait_evacuated(pe, use["oT"])
            wait_evacuated(pe, use["oT"] + 1)
            for j in range(2):
                tokens("o", j, use["o"] + j, xT)
            turn_norm("ffn1")
            ffn(1, "ffn1")
            turn_norm("final")
            for i in range(DEPTH):
                ffn(2 + 2 * i, "final" if i == 0 else f"ln2_{i - 1}")
                turn_norm(f"ln0_{i}")
                for j in range(SIDE):
                    u = use[f"win{i}"] + j
                    if j == 2:
                        features(f"win{i}", j, u, xT, 0, 2)
                    else:
                        features(f"win{i}", j, u, xT, ready=xT_ready(f"ln0_{i}"))
                pe.wait_ge(sem("bdw_ready"), 1)
                a = claim(use[f"bd{i}"])
                for t in range(TT):
                    for k in range(KT):
                        tok = slice(t * P, t * P + P)
                        ins = product(a[:, 16 * t:16 * t + 16], ((xT_hi[:, k, tok], xT_lo[:, k, tok]), (bdw_hi[:, i, k, :], bdw_lo[:, i, k, :])),
                                      t == 0 and k == 0, k == KT - 1)
                ins.then_inc(acc_ready, 1)

                def scores(n):
                    u = use[f"s{i}_{n}"]
                    a = claim(u)
                    for h in range(2):
                        rows = slice(HD * h, HD * h + HD)
                        mm(a[:, h * 512:h * 512 + P], qaT[rows, n, 0:P], kaT[rows, n // 2, 0:P], start=True, stop=True, skip_group_check=True)
                        ins = mm(a[:, h * 512 + P:h * 512 + 3 * P], qaT[rows, n, P:SEQ], kaT[rows, n // 2, :], start=True, stop=True, skip_group_check=True)
                    ins.then_inc(acc_ready, 1)

                def turn_weights(n):
                    pe.wait_ge(sem("s_normed"), 8 * i + n + 1)
                    if n >= 2:
                        pe.wait_ge(sem("pT3_ready"), 8 * i + n - 1)
                    for h in range(2):
                        for b in range(2):
                            ins = nc.tensor.transpose(trp[n % 2][:, (2 * h + b) * P:(2 * h + b + 1) * P], zA[:, n % 2, h, b, :], ident)
                    ins.then_inc(sem("s_turned"), 1)

                def attend(n):
                    a = claim(use[f"oa{i}_{n}"])
                    pe.wait_ge(sem("pT3_ready"), 8 * i + n + 1)
                    d = slice((n // 2) * HD, (n // 2) * HD + HD)
                    for h in range(2):
                        rows = slice(HD * h, HD * h + HD)
                        mm(a[rows, 0:P], va[:, 0, d], pT3[:, h, 0, :], start=True, stop=True, skip_group_check=True)
                        mm(a[rows, P:SEQ], va[:, 0, d], pT3[:, h, 1, :], start=True, stop=False, skip_group_check=True)
                        ins = mm(a[rows, P:SEQ], va[:, 1, d], pT3[:, h, 2, :], start=False, stop=True, skip_group_check=True)
                    ins.then_inc(acc_ready, 1)

                for j in range(3):
                    wait_evacuated(pe, use[f"win{i}"] + j)
                def beside(n):
                    for j, last, p in side_panels(i, n):
                        pe.wait_ge(lo_ready, p + 1)
                        _, _, k0, kt, _ = panels[p]
                        if k0 == 0 and i + j > SIDE:
                            pe.wait_ge(sem("gate_columns"), 12 * i + 2 * (j - SIDE))
                        for k in range(kt):
                            for t in range(TT):
                                tok = slice(t * P, t * P + P)
                                a = (xT_hi[:, k0 + k, tok], xT_lo[:, k0 + k, tok])
                                w = (w_hi[:, p % SPL, k, :], w_lo[:, p % SPL, k, :])
                                ins = product(trp[2 + t][:, :], (a, w), k0 + k == 0, last and k == kt - 1)
                        ins.then_inc(panel_used, 1)

                for n in range(8 + 2):
                    if n < 8:
                        scores(n)
                    if 1 <= n < 9:
                        turn_weights(n - 1)
                    if n >= 2:
                        attend(n - 2)
                    beside(n)
                pe.wait_ge(sem("gate_columns"), 12 * (i + 1))

                a = claim(use[f"G{i}"])
                pe.wait_ge(sem("g_ready"), i + 1)
                mm(a[:, 0:16], const(C_LE), sm[:, 3].rearrange("p t h -> p (t h)"), start=True, stop=True, skip_group_check=True)
                mm(a[:, 16:32], const(C_ONE), sm[:, 3].rearrange("p t h -> p (t h)"), start=True, stop=True, skip_group_check=True).then_inc(acc_ready, 1)
                def branch_a(j):
                    tokens(f"brA{i}_{j}", 0, use[f"brA{i}_{j}"], xT, lambda k0, kt: pe.wait_ge(sem("alo_ready"), 2 * i + (k0 + kt) // 4))

                branch_a(0)
                for t in range(TT):
                    a = claim(use[f"Gr{i}"] + t)
                    for h in range(DH):
                        ins = mm(a[:, h * P:h * P + P], sm[:, 3, t, h:h + 1].to_broadcast([P, P]), const(C_LE), start=True, stop=True, skip_group_check=True)
                    ins.then_inc(acc_ready, 1)
                for g in range(4):
                    if g == 2:
                        branch_a(1)
                    sq = (kbg, ktl)[g % 2][:, :, :].rearrange("p h d -> p (h d)")
                    a = claim(use[f"ss{i}{'ab'[g // 2]}"] + g % 2)
                    pe.wait_ge(sem("squares"), 4 * i + g + 1)
                    for c in range(2):
                        ins = mm(a[:, c * 512:c * 512 + 512], const(C_ONE), sq[:, c * 512:c * 512 + 512], start=True, stop=True, skip_group_check=True)
                    ins.then_inc(acc_ready, 1)
                pe.wait_ge(sem("qkv_ready"), 6 * (i + 1))
                for n in range(4):
                    a = claim(use[f"nat{i}"] + n)
                    if n == 2:
                        pe.wait_ge(sem("qk_normed"), 4 * (i + 1))
                    src, t = (vh, n) if n < 2 else (kh, n - 2)
                    for h in range(DH):
                        ins = nc.tensor.transpose(a[:, h * P:h * P + P], src[:, h, t * P:t * P + P], ident)
                    ins.then_inc(acc_ready, 1)
                for name, right in (("kk", kh), ("qk", qh)):
                    for t in range(TT):
                        a = claim(use[f"{name}{i}"] + t)
                        tok = slice(t * P, t * P + P)
                        for h in range(DH):
                            ins = mm(a[:, h * P:h * P + P], kh[:, h, tok], right[:, h, tok], start=True, stop=True, skip_group_check=True)
                        ins.then_inc(acc_ready, 1)

                def heads_blocks(u, left, right, lv, side):
                    a = claim(u)
                    for h in range(DH):
                        o = a[:, h * HD:h * HD + HD].rearrange("p (m b) -> p m b", b=1 << lv)
                        ins = mm(o, left[:, h, :], blocks(right[:, h, :], lv, side), start=True, stop=True, skip_group_check=True)
                    ins.then_inc(acc_ready, 1)

                def heads(u, *terms):
                    a = claim(u)
                    for h in range(DH):
                        for n, (left, right) in enumerate(terms):
                            ins = mm(a[:, h * P:h * P + P], left[:, h, :], right[:, h, :], start=n == 0, stop=n == len(terms) - 1, skip_group_check=True)
                    ins.then_inc(acc_ready, 1)

                pe.wait_ge(sem("inverse_init"), 4 * (i + 1))
                for lv in range(LEVELS):
                    for t in range(TT):
                        pe.wait_ge(sem("Xm_ready"), TT * (LEVELS * i + lv) + t + 1)
                        if lv:
                            wait_evacuated(pe, doubled(i, lv - 1, t, "ZU"))
                        heads(use[f"Y{i}_{lv}"] + t, (Xm[:, t], U[:, t]))
                    if lv == 0:
                        continue
                    for t in range(TT):
                        wait_evacuated(pe, use[f"Y{i}_{lv}"] + t)
                        if lv == 1:
                            pe.wait_ge(sem("Ti_pairs"), TT * i + t + 1)
                        else:
                            wait_evacuated(pe, doubled(i, lv - 1, t, "ZT"))
                        heads_blocks(use[f"ZU{i}_{lv}_{t}"], Ti[:, t], Yp[:, t], lv, 1)
                        if lv < LEVELS - 1:
                            heads_blocks(use[f"ZT{i}_{lv}_{t}"], Yp[:, t], Ti[:, t], lv, 0)
                for t in range(TT):
                    wait_evacuated(pe, use[f"ZU{i}_{LEVELS - 1}_{t}"])
                d = use[f"dl{i}"]
                heads(d, (U[:, 0], vb[:, 0]))
                heads(d + 1, (kbg, U[:, 1]))
                wait_evacuated(pe, d)
                heads(d + 2, (ktl, Ti[:, 0]))
                wait_evacuated(pe, d + 1)
                wait_evacuated(pe, d + 2)
                heads(d + 3, (U[:, 1], vb[:, 1]), (Xm[:, 0], Xm[:, 1]))
                heads(d + 4, (AT[:, 0], Ti[:, 0]))
                heads(d + 5, (qh[:, :, P:SEQ], Xm[:, 1]))
                wait_evacuated(pe, d + 3)
                heads(d + 6, (AT[:, 1], Ti[:, 1]))
                turn(f"delta_{i}", L[:, :, :, :].rearrange("p t h d -> p t (h d)"), "o_ready", TT * (i + 1))
                for j in range(2):
                    tokens(f"brB{i}", j, use[f"brB{i}"] + j, xT, xT_ready(f"delta_{i}"))
                turn(f"mixed_{i}", gates[:, :, 0, :], "mix_ready", 2 * (i + 1))
                for j in range(2):
                    tokens(f"wo{i}", j, use[f"wo{i}"] + j, xT, xT_ready(f"mixed_{i}"))
                turn_norm(f"ln1_{i}")
                ffn(3 + 2 * i, f"ln1_{i}")
                if i < DEPTH - 1:
                    turn_norm(f"ln2_{i}")


INPUTS = """x norm_mix norm_ffn norm_kv norm_final ssm_w_in ssm_a_re ssm_a_im ssm_log_dt ssm_b_re ssm_b_im ssm_c_re
ssm_c_im ssm_d ssm_w_glu kv_w attn_w_q attn_w_o ffn_w_up ffn_conv_w ffn_conv_b ffn_w_down rel_bias_2 ln_g_2 ln_b_2
ffn_w13_2 ffn_w2_2 w_in_2 conv_w_2 a_log_2 dt_bias_2 dn_norm_g_2 sinks_2 w_branch_a_2 w_branch_b_2 w_out_2""".split()


def kernel(**inputs):
    import concourse.bacc as _bacc
    from concourse.bass_utils import run_bass_kernel_spmd as _run

    nc = _bacc.Bacc("TRN2", target_bir_lowering=False, num_devices=1)
    arrays = {name: np.ascontiguousarray(inputs[name]) for name in INPUTS}
    arrays["const_masks"] = constants()
    arrays["const_buckets"] = bucket_pattern()
    tensors = {name: nc.dram_tensor(f"in_{name}", a.shape, F32, kind="ExternalInput").ap() for name, a in arrays.items()}
    out = nc.dram_tensor("out_x", (1, SEQ, D), F32, kind="ExternalOutput").ap()
    build(nc, tensors, out)
    result = _run(nc, [{f"in_{name}": a for name, a in arrays.items()}], core_ids=[0])
    return result.results[0]["out_x"]
```

```python
import math
from contextlib import ExitStack

import numpy as np

import concourse.bass as bass
from concourse import mybir

F32 = mybir.dt.float32
F32R = mybir.dt.float32r
ALU = mybir.AluOpType
ACT = mybir.ActivationFunctionType
AX_X = mybir.AxisListType.X

P = 128
SEQ = 256
D = 1024
KT = D // P
TT = SEQ // P
D_FF = 2816
FT = D_FF // P
DEPTH = 2
EPS = 1e-6
LN_EPS = 1e-5
NORM_EPS = 1e-6
ALPHA = (2 * DEPTH) ** 0.25
NEG_INF = -1e30
GROUPS, GH, ST = 64, 16, 64
PAIRS = GROUPS // 2
Q = 8
NC_ = SEQ // Q
HEADS, HD = 16, 64
KV_HEADS = 4
DH, DK = 8, 128
CONV_T = 3 * DH
LEVELS = 7
N_IN = 7696
BUCKETS = 32

PK, PN = 4, 512
RAW, SPL = 2, 3
TRP = 4

TWO_PI = 2 * math.pi
MAGIC = 1.5 * 2 ** 23


def two_pi_parts():
    c1 = float(np.float32(6.28125))
    c2 = float(np.float32(round((TWO_PI - c1) * 2 ** 22) / 2 ** 22))
    return c1, c2, TWO_PI - c1 - c2


CONV_COLS = CONV_T // 4
SIDE = CONV_COLS + 3

C_ID, C_LE, C_LT, C_GT, C_ONE = (i * P for i in range(5))
C_LVL = 5 * P
C_PAIR = C_LVL + LEVELS * P
C_NEGU = C_PAIR + 8
C_NEGL = C_NEGU + P
C_EPS = C_NEGL + P
N_CONST = C_EPS + 1


def constants():
    i, j = np.arange(P)[:, None], np.arange(P)[None, :]
    c = np.zeros((P, N_CONST), np.float32)
    c[:, C_ID:C_ID + P] = i == j
    c[:, C_LE:C_LE + P] = i <= j
    c[:, C_LT:C_LT + P] = i < j
    c[:, C_GT:C_GT + P] = i > j
    c[:, C_ONE:C_ONE + P] = 1
    for lv in range(LEVELS):
        b = 1 << lv
        c[:, C_LVL + lv * P:C_LVL + (lv + 1) * P] = (i // (2 * b) == j // (2 * b)) & (i // b % 2 == 1) & (j // b % 2 == 0)
    c[:, C_PAIR:C_PAIR + 8] = i // GH == np.arange(8)[None, :]
    c[:, C_NEGU:C_NEGU + P] = np.where(j > i, NEG_INF, 0)
    c[:, C_NEGL:C_NEGL + P] = np.where(j <= i, NEG_INF, 0)
    c[:, C_EPS] = NORM_EPS
    return c


def bucket_pattern():
    n = np.arange(P)
    exact = BUCKETS // 2
    nf = np.maximum(n, 1).astype(np.float32)
    large = exact + (np.log(nf / np.float32(exact)) / np.float32(math.log(P / exact)) * np.float32(BUCKETS - exact)).astype(np.int32)
    b = np.where(n < exact, n, np.minimum(large, BUCKETS - 1))
    return (np.arange(BUCKETS)[:, None] == b[::-1][None, :]).astype(np.float32)


def plan():
    panels, gemms = [], {}

    def add(name, w, index, ktiles, columns):
        cols = []
        for c0, c1 in columns:
            ps = []
            for k0 in range(0, ktiles, PK):
                ps.append(len(panels))
                panels.append((w, index, k0, min(PK, ktiles - k0), (c0, c1)))
            cols.append(ps)
        gemms[name] = cols

    def straight(n, start=0):
        return [(c, c + PN // 2) for c in range(start, start + n, PN)]

    def paired(n):
        return [(c, n + c) for c in range(0, n, PN // 2)]

    def ffn(f, up, down, index):
        add(f"up{f}", up, index, KT, paired(D_FF))
        add(f"down{f}", down, index, FT, straight(D))

    for j in range(2):
        add(f"ssm_in{j}", "ssm_w_in", (0,), KT, straight(PN, j * PN))
    add("glu", "ssm_w_glu", (0,), KT, paired(D))
    ffn(0, "ffn_w_up", "ffn_w_down", (0,))
    add("kv", "kv_w", (), KT, straight(2 * D))
    for j in range(2):
        add(f"q{j}", "attn_w_q", (0,), KT, straight(PN, j * PN))
    add("o", "attn_w_o", (0,), KT, straight(D))
    ffn(1, "ffn_w_up", "ffn_w_down", (1,))
    for i in range(DEPTH):
        ffn(2 + 2 * i, "ffn_w13_2", "ffn_w2_2", (i, 0))
        add(f"win{i}", "w_in_2", (i,), KT, straight(3072, 1536) + straight(1536) + straight(3072, 4624))
        for j in range(2):
            add(f"brA{i}_{j}", "w_branch_a_2", (i,), KT, straight(PN, j * PN))
        add(f"brB{i}", "w_branch_b_2", (i,), KT, straight(D))
        add(f"wo{i}", "w_out_2", (i,), KT, straight(D))
        ffn(3 + 2 * i, "ffn_w13_2", "ffn_w2_2", (i, 1))
    return panels, gemms


COLUMN_TILES = [
    [("norm_mix", 16), ("norm_ffn", 16), ("norm_kv", 8), ("ssm_d", 8), ("ln_g_2", 48), ("norm_final", 8)],
    [("ln_b_2", 48), ("ffn_conv_b", 44)],
    [("ffn_conv_w", 66, 0)],
    [("ffn_conv_w", 66, 66)],
    [("conv_w_2", 96, 0)],
    [("conv_w_2", 96, 96)],
]

def build(nc, T, out):
    panels, gemms = plan()
    n_panels = len(panels)

    es = ExitStack()
    with es:
        def sb(name, shape, dt=F32, stack=es):
            return stack.enter_context(nc.sbuf_tensor(name, shape, dt))

        sems = {}

        def sem(name):
            if name not in sems:
                sems[name] = es.enter_context(nc.semaphore(name))
            return sems[name]

        raw = sb("raw", [P, RAW, PK, PN])
        w_hi = sb("w_hi", [P, SPL, PK, PN], F32R)
        w_lo = sb("w_lo", [P, SPL, PK, PN], F32R)
        xT_hi = sb("xT_hi", [P, KT, SEQ], F32R)
        xT_lo = sb("xT_lo", [P, KT, SEQ], F32R)
        x = sb("x", [P, TT, D])
        xn = sb("xn", [P, TT, D])
        cst = sb("cst", [P, N_CONST])
        cols = sb("cols", [P, 6, 104])
        bdw_hi = sb("bdw_hi", [P, DEPTH, KT, 16], F32R)
        bdw_lo = sb("bdw_lo", [P, DEPTH, KT, 16], F32R)
        stat = sb("stat", [P, TT, 2, 6])
        mv = sb("mv", [P, TT, 2])
        nrm = sb("nrm", [P, 4, TT])
        row = sb("row", [P, DEPTH, 2, 8])
        snk = sb("snk", [P, DEPTH, HEADS])
        dng = sb("dng", [P, DEPTH, DK])

        def const(at, n=P):
            return cst[:, at:at + n]

        ident = const(C_ID)

        gb = sb("gb", [P, 2, D])
        tb = sb("tb", [P, 2, SEQ])

        s1 = ExitStack()
        uT = sb("uT", [P, KT, SEQ], F32, s1)
        Bm = sb("Bm", [P, 2, PAIRS, 32], F32, s1)
        pT = sb("pT", [P, 12, PAIRS], F32, s1)
        tmpv = sb("tmpv", [P, 2, 1024], F32, s1)
        CT = sb("CT", [P, 2, PAIRS, GH], F32, s1)
        tmpp = sb("tmpp", [P, 2, 2, 4, NC_], F32, s1)
        bsel = sb("bsel", [BUCKETS, P], F32, s1)
        relb = sb("relb", [BUCKETS, HEADS], F32, s1)
        ftab = sb("ftab", [HEADS, P], F32, s1)
        s1c = ExitStack()
        bdw = sb("bdw", [P, DEPTH, KT, 16], F32, s1c)
        b_n = sb("b_n", [P, 2, PAIRS, GH], F32, s1c)
        pn = sb("pn", [PAIRS, 23, P], F32, s1c)
        s1c.close()
        CA = sb("CA", [P, Q, 2, PAIRS, GH], F32, s1)
        s1a = ExitStack()
        BT = sb("BT", [P, 2, 8, 2, P], F32, s1a)
        bu = sb("bu", [P, 2, 2, 4, SEQ // 2], F32, s1a)
        s1a.close()
        s1b = ExitStack()
        CAm = sb("CAm", [P, 2, 2, Q, 4, 32], F32, s1b)
        Kbd = sb("Kbd", [P, 2, Q, P], F32, s1b)
        s1b.close()
        s1.close()
        stage = uT[:, 0:3, :].rearrange("p a (b c) -> p (a b) c", c=P)
        c_n = gb[:, :, :].rearrange("p r (f d s) -> p r f d s", f=8, d=2)
        BAm = gb[:, :, :].rearrange("p r (k c) -> p r k c", c=32)
        lags = tmpv[:, 0, :].rearrange("p (f j h) -> p f j h", f=8, j=Q)
        skip = tmpv[:, 1, :].rearrange("p (f m) -> p f m", f=8)
        E = xn[:, :, :].rearrange("p t (k c) -> p t k c", c=NC_)
        V = gb[:, :, :].rearrange("p t (k c) -> p t k c", c=NC_)

        s2 = ExitStack()
        hT_hi = sb("hT_hi", [P, FT, SEQ], F32R, s2)
        hT_lo = sb("hT_lo", [P, FT, SEQ], F32R, s2)
        hbuf = sb("hbuf", [P, 2, 2, SEQ], F32, s2)
        s2.close()

        s3 = ExitStack()
        kT = sb("kT", [P, KT, SEQ], F32, s3)
        qT = sb("qT", [P, KT, SEQ], F32, s3)
        vn_ = sb("vnat", [P, TT, D], F32, s3)
        SW = 3 * P
        zS = sb("zS", [P, HEADS, SW], F32, s3)
        spS = sb("spS", [P, HEADS, SW], F32, s3)
        s3.close()

        s4 = ExitStack()
        qkT = sb("qkT", [P, CONV_T, SEQ], F32, s4)
        sz = sb("sz", [P, TT, D], F32, s4)
        gates = sb("gates", [P, TT, 2, D], F32, s4)
        sm = sb("sm", [P, 12, TT, 8], F32, s4)
        s4a = ExitStack()
        qaT = sb("qaT", [P, KT, SEQ], F32, s4a)
        kaT = sb("kaT", [P, KV_HEADS, SEQ], F32, s4a)
        va = sb("va", [P, TT, 256], F32, s4a)
        biasL = sb("biasL", [P, HEADS, P], F32, s4a)
        biasU = sb("biasU", [P, HEADS, P], F32, s4a)
        zA = sb("zA", [P, 2, 2, 2, P], F32, s4a)
        zB = sb("zB", [P, 2, 2, P], F32, s4a)
        pT3 = sb("pT3", [P, 2, 3, P], F32, s4a)
        red = sb("red", [P, 4, 4], F32, s4a)
        s4a.close()
        s4b = ExitStack()
        L = sb("L", [P, TT, 8, P], F32, s4b)
        AT = sb("AT", [P, TT, 8, P], F32, s4b)
        Ti = sb("Ti", [P, TT, 8, P], F32, s4b)
        U = sb("U", [P, TT, 8, P], F32, s4b)
        kbg = sb("kbg", [P, 8, P], F32, s4b)
        ktl = sb("ktl", [P, 8, P], F32, s4b)
        s4b.close()
        s4.close()
        vb = xn[:, :, :].rearrange("p t (h d) -> p t h d", d=DK)
        qh, kh, vh = qkT[:, 0:8], qkT[:, 8:16], qkT[:, 16:24]
        Xm = kh.rearrange("p a b -> p (a b)").rearrange("p (t h m) -> p t h m", t=TT, h=8)
        Yp = vh.rearrange("p a b -> p (a b)").rearrange("p (t h m) -> p t h m", t=TT, h=8)

        acc = [es.enter_context(nc.psum_tensor(f"acc{i}", [P, 1024], F32)) for i in range(2)]
        trp = [es.enter_context(nc.psum_tensor(f"trp{i}", [P, 512], F32)) for i in range(TRP)]

        ftab_d = nc.dram_tensor("ftab_d", (HEADS, P, P), F32, kind="Internal").ap()

        raw_loaded = [sem(f"raw_loaded{i}") for i in range(RAW)]
        hi_ready, lo_ready, panel_used = sem("hi_ready"), sem("lo_ready"), sem("panel_used")
        acc_ready = sem("acc_ready")
        acc_freed = [sem("acc_freed0"), sem("acc_freed1")]

        use, filled = {}, {}
        n_use = n_fill = 0

        def uses(name, count, gemm=None):
            nonlocal n_use, n_fill
            use[name] = n_use
            for j in range(count):
                if gemm:
                    filled[n_use] = (panel_used, gemms[gemm][j][-1] + 1)
                else:
                    n_fill += 1
                    filled[n_use] = (acc_ready, n_fill)
                n_use += 1

        def gemm_uses(name):
            uses(name, len(gemms[name]), name)

        uses("cols", 1)
        uses("CT", 2)
        uses("ftab", 1)
        gemm_uses("ssm_in0")
        uses("pT", 1)
        gemm_uses("ssm_in1")
        uses("BT", 4)
        uses("bu", 16)
        use["y"] = n_use
        n_use += 2
        gemm_uses("glu")
        gemm_uses("up0"), gemm_uses("down0")
        gemm_uses("kv")
        for half in range(2):
            gemm_uses(f"q{half}"), uses(f"z{half}", 4)
        uses("rem", 8), uses("oT", 2)
        gemm_uses("o")
        gemm_uses("up1"), gemm_uses("down1")
        for i in range(DEPTH):
            gemm_uses(f"up{2 + 2 * i}"), gemm_uses(f"down{2 + 2 * i}")
            uses(f"win{i}", SIDE, f"win{i}")
            uses(f"bd{i}", 1)
            for n in range(8 + 2):
                if n < 8:
                    uses(f"s{i}_{n}", 1)
                if n >= 2:
                    uses(f"oa{i}_{n - 2}", 1)
            uses(f"G{i}", 1), uses(f"Gr{i}", 2), uses(f"ss{i}", 4)
            gemm_uses(f"brA{i}_0")
            uses(f"nat{i}k", 2), uses(f"kk{i}", 2), uses(f"qk{i}", 2), uses(f"nat{i}v", 2)
            for lv in range(LEVELS):
                uses(f"Y{i}_{lv}", 2)
                for t in range(TT):
                    if lv:
                        uses(f"ZU{i}_{lv}_{t}", 1)
                    if 0 < lv < LEVELS - 1:
                        uses(f"ZT{i}_{lv}_{t}", 1)
            uses(f"dl{i}", 7)
            gemm_uses(f"brA{i}_1")
            gemm_uses(f"brB{i}"), gemm_uses(f"wo{i}")
            gemm_uses(f"up{3 + 2 * i}"), gemm_uses(f"down{3 + 2 * i}")

        def side_panel(i, n):
            j, k = SIDE + n // 2, n % 2
            ps = gemms[f"win{i}"][j]
            return j, k == len(ps) - 1, ps[k]

        def y_tiles(f, n=1):
            return A4(use["y"] + f // 4)[:, f % 4:f % 4 + n]

        def wait_filled(eng, u):
            eng.wait_ge(*filled[u])

        def freed(u):
            return acc_freed[u % 2], 1

        tsplits = {}

        def tsplit_no(name):
            if name not in tsplits:
                tsplits[name] = len(tsplits)
            return tsplits[name]

        for name in ["mix0", "ffn0", "kv", "mix1", "ffn1", "final"]:
            tsplit_no(name)
        for i in range(DEPTH):
            for name in ["ln0", "delta", "mixed", "ln1"] + ["ln2"] * (i < DEPTH - 1):
                tsplit_no(f"{name}_{i}")
        norms = {n: i for i, n in enumerate(
            ["mix0", "ffn0", "kv", "ffn1", "final"] + [f"ln{j}_{i}" for i in range(DEPTH) for j in range(3)])}
        naturals = {n: i for i, n in enumerate(["final"] + [f"ln{j}_{i}" for i in range(DEPTH) for j in range(3)])}

        residuals = {n: i for i, n in enumerate(
            ["down0", "o", "down1"] + [n for i in range(DEPTH) for n in (f"down{2 + 2 * i}", f"wo{i}", f"down{3 + 2 * i}")])}

        shifted = {f"ln{j}_{i}": 3 * i + j for i in range(DEPTH) for j in range(3)}

        def gain_of(name):
            c0, c1 = cols[:, 0, :], cols[:, 1, :]
            if name.startswith("ln"):
                j, i = int(name[2]), int(name[4])
                at = (i * 3 + j) * 8
                return c0[:, 48 + at:48 + at + 8], c1[:, at:at + 8]
            at = {"mix0": 0, "mix1": 8, "ffn0": 16, "ffn1": 24, "kv": 32, "final": 96}[name]
            return c0[:, at:at + 8], None

        def A4(u, f=4):
            return acc[u % 2][:, :].rearrange("p (n t) -> p n t", n=f)

        def A2(u):
            return acc[u % 2][:, :].rearrange("p (t n) -> p t n", t=2)

        def A8(u):
            return acc[u % 2][:, :].rearrange("p (h m) -> p h m", h=8)

        def doubled(i, lv, t, name):
            return use[f"{name}{i}_{lv}_{t}"] if lv else use[f"Y{i}_0"] + t

        def blocks(ap, lv, side):
            return ap.rearrange("p (m s b) -> p m s b", s=2, b=1 << lv)[:, :, side, :]

        def bc(ap, axis, n):
            a = ap.unsqueeze(axis)
            shape = list(a.shape)
            shape[axis] = n
            return a.to_broadcast(shape)

        class Steps:

            def __init__(self, eng, name):
                self.eng, self.sem, self.n = eng, sem(name), 0

            def __call__(self, ins):
                ins.then_inc(self.sem, 1)
                self.n += 1

            def settle(self, but=0):
                self.eng.wait_ge(self.sem, self.n - but)

        def wait_evacuated(eng, u):
            eng.wait_ge(acc_freed[u % 2], u // 2 + 1)

        def rows_of(name):
            src = T[name]
            letters = " ".join("abcd"[:len(src.shape)])
            return src.rearrange(f"{letters} -> ({letters})").rearrange("(r c) -> r c", c=P)

        def s_(i):
            return pn[:, i, :]

        block = es.enter_context(nc.Block())

        @block.sync
        def _(sp):
            sp.dma_start(pn[:, 9, :], T["ssm_a_re"][0].rearrange("(k a) p -> k (a p)", a=2)).then_inc(sem("ssm_a_in"), 16)
            sp.dma_start(pn[:, 10, :], T["ssm_a_im"][0].rearrange("(k a) p -> k (a p)", a=2)).then_inc(sem("ssm_a_in"), 16)
            sp.dma_start(pn[:, 12, 0:2], T["ssm_log_dt"][0].rearrange("(k a) -> k a", a=2)).then_inc(sem("ssm_a_in"), 16)
            sp.dma_start(x[:, :, :], T["x"][0].rearrange("(t p) d -> p t d", p=P)).then_inc(sem("x_in"), 16)

            def mixer_parameters():
                for r, name in enumerate(("ssm_c_re", "ssm_c_im")):
                    for dup in range(2):
                        sp.dma_start(c_n[:, r, :, dup, :], T[name][0].rearrange("(f q) h p -> (q h) f p", q=8)).then_inc(sem("ssm_c_in"), 16)
                for r, name in enumerate(("ssm_b_re", "ssm_b_im")):
                    sp.dma_start(b_n[:, r, :, :], T[name][0].rearrange("(k a) p h -> (a p) k h", a=2)).then_inc(sem("ssm_b_in"), 16)
                sp.dma_start(cst[:, C_ID + P:], T["const_masks"][:, C_ID + P:]).then_inc(sem("masks_in"), 16)

            def parameters():
                sp.dma_start(bdw[:, :, :, :], T["w_in_2"][:, :, 4608:4624].rearrange("i (k p) n -> p i k n", p=P)).then_inc(sem("bdw_in"), 16)
                sp.dma_start(row[:, :, 0, :], T["a_log_2"].partition_broadcast(P)).then_inc(sem("misc_in"), 16)
                sp.dma_start(row[:, :, 1, :], T["dt_bias_2"].partition_broadcast(P)).then_inc(sem("misc_in"), 16)
                sp.dma_start(snk[:, :, :], T["sinks_2"].partition_broadcast(P)).then_inc(sem("misc_in"), 16)
                sp.dma_start(dng[:, :, :], T["dn_norm_g_2"].partition_broadcast(P)).then_inc(sem("misc_in"), 16)

            for p, (w, index, k0, kt, (c0, c1)) in enumerate(panels):
                if p >= n_panels:
                    break
                src = T[w]
                for i in index:
                    src = src[i]
                src = src[k0 * P:(k0 + kt) * P, :].rearrange("(k p) n -> p k n", p=P)
                if p == 1:
                    mixer_parameters()
                if p == RAW:
                    parameters()
                if p >= RAW:
                    sp.wait_ge(lo_ready, p - RAW + 1)
                slot, half = raw[:, p % RAW, 0:kt, :], PN // 2
                if c1 == c0 + half:
                    sp.dma_start(slot, src[:, :, c0:c0 + PN]).then_inc(raw_loaded[p % RAW], 32)
                else:
                    sp.dma_start(slot[:, :, 0:half], src[:, :, c0:c0 + half]).then_inc(raw_loaded[p % RAW], 16)
                    sp.dma_start(slot[:, :, half:PN], src[:, :, c1:c1 + half]).then_inc(raw_loaded[p % RAW], 16)
            for t in range(TT):
                sp.wait_ge(sem("out_ready"), t + 1)
                sp.dma_start(out[0, t * P:t * P + P, :], x[:, t, :]).then_inc(sem("out_stored"), 16)
            sp.wait_ge(sem("out_stored"), 16 * TT)

        @block.gpsimd
        def _(pool):
            step = Steps(pool, "pool_steps")
            tt = nc.gpsimd.tensor_tensor
            ts = nc.gpsimd.tensor_scalar

            def s(i):
                return pn[:, i, :]

            def do(ins):
                step(ins)
                step.settle()

            for i, ((name, n, first),) in enumerate(COLUMN_TILES[2:], 2):
                pool.dma_start(stage[0:n, i, :], rows_of(name)[first:first + n, :]).then_inc(sem("conv_cols_in"), 16)
            step(nc.gpsimd.memset(Bm[:, :, :, :], 0.0))
            pool.wait_ge(sem("dt_ready"), 1)
            pool.wait_ge(sem("ssm_a_in"), 48)
            dt = bc(pn[:, 12, 2:4], 2, ST)

            def halves(i):
                return s(i).rearrange("k (a p) -> k a p", a=2)

            step(tt(halves(13), halves(9), dt, ALU.mult))
            do(tt(halves(14), halves(10), dt, ALU.mult))
            pool.wait_ge(step.sem, step.n)
            nc.gpsimd.tensor_copy(s(19), s(13)).then_inc(sem("mag_in"), 1)
            do(ts(s(15), s(14), 1 / TWO_PI, MAGIC, ALU.mult, ALU.add))
            do(ts(s(15), s(15), -MAGIC, None, ALU.add))
            for part in two_pi_parts():
                do(ts(s(16), s(15), -part, None, ALU.mult))
                do(tt(s(14), s(14), s(16), ALU.add))
            ts(s(14), s(14), 3.1415925, -3.1415925, ALU.min, ALU.max).then_inc(sem("angle_ready"), 1)
            pool.wait_ge(sem("trig_ready"), 3)
            do(tt(s(17), s(16), s(16), ALU.mult))
            do(ts(s(17), s(17), -2.0, 1.0, ALU.mult, ALU.add))
            step(tt(s(0), s(13), s(17), ALU.mult))
            do(tt(s(2), s(13), s(15), ALU.mult))
            step(ts(s(1), s(2), -1.0, None, ALU.mult))
            step(ts(s(3), s(2), -1.0, None, ALU.mult))
            step(tt(s(17), s(9), s(9), ALU.mult))
            do(tt(s(18), s(10), s(10), ALU.mult))
            tt(s(19), s(17), s(18), ALU.add).then_inc(sem("den_ready"), 1)
            pool.wait_ge(sem("den_ready"), 1)
            re, im = 0, 2
            for n in range(int(math.log2(Q))):
                step(tt(s(17), s(re), s(re), ALU.mult))
                step(tt(s(18), s(im), s(im), ALU.mult))
                do(tt(s(16), s(re), s(im), ALU.mult))
                re, im = 4, 6
                step(tt(s(re), s(17), s(18), ALU.subtract))
                do(ts(s(im), s(16), 2.0, None, ALU.mult))
                if n == 0:
                    step(nc.gpsimd.tensor_copy(s(20), s(re)))
                    step(ts(s(21), s(im), -1.0, None, ALU.mult))
                    do(nc.gpsimd.tensor_copy(s(22), s(im)))
            step(ts(s(5), s(6), -1.0, None, ALU.mult))
            do(ts(s(16), s(0), -1.0, None, ALU.add))
            step(tt(s(13), s(16), s(9), ALU.mult))
            step(tt(s(14), s(2), s(10), ALU.mult))
            step(tt(s(17), s(2), s(9), ALU.mult))
            do(tt(s(18), s(16), s(10), ALU.mult))
            step(tt(s(13), s(13), s(14), ALU.add))
            do(tt(s(17), s(17), s(18), ALU.subtract))
            pool.wait_ge(sem("inv_ready"), 1)
            step(tt(s(7), s(13), s(19), ALU.mult))
            do(tt(s(8), s(17), s(19), ALU.mult))
            nc.gpsimd.tensor_copy(s(12), s(8)).then_inc(sem("powers_ready"), 1)

            pool.wait_ge(sem("pT_ready"), 1)
            pool.wait_ge(sem("CT_ready"), 4)
            pool.wait_ge(sem("BAm_ready"), 1)
            t1, t2 = (tmpv[:, i, :].rearrange("p (r k h) -> p r k h", r=2, h=GH) for i in range(2))
            for j in range(Q):
                prev = CA[:, j - 1] if j else CT[:, :, :, :]
                step(tt(t1, prev, bc(bc(pT[:, 0, :], 1, 2), 3, GH), ALU.mult))
                do(tt(t2, prev[:, ::-1], bc(pT[:, 2:4, :], 3, GH), ALU.mult))
                do(tt(CA[:, j], t1, t2, ALU.add))
            pool.sem_inc(sem("CA_ready"), 1)
            pool.wait_ge(sem("chunks_done"), 8)
            pool.wait_ge(sem("ftab_stored"), 16)
            nc.gpsimd.memset(CAm[:, :, :, :, :, :], 0.0).then_inc(sem("CAm_cleared"), 1)
            for f in range(8):
                pool.wait_ge(sem("lags_ready"), 2 * (f + 1))
                if f >= 2:
                    pool.wait_ge(sem("within_done"), f - 1)
                o = Kbd[:, f % 2].rearrange("p j (g h) -> p j g h", g=8)
                do(tt(o, bc(lags[:, f], 2, 8), bc(bc(const(C_PAIR, 8), 1, Q), 3, GH), ALU.mult))
                tt(Kbd[:, f % 2, 0, :], Kbd[:, f % 2, 0, :], skip[:, f], ALU.add).then_inc(sem("Kbd_ready"), 1)

            order = list(naturals)

            def load_gain(name):
                if name == "final":
                    pool.dma_start(gb[:, 0, :], T["norm_final"].partition_broadcast(P)).then_inc(sem("gain_in"), 32)
                else:
                    j, i = int(name[2]), int(name[4])
                    pool.dma_start(gb[:, 0, :], T["ln_g_2"][i, j].partition_broadcast(P)).then_inc(sem("gain_in"), 16)
                    pool.dma_start(gb[:, 1, :], T["ln_b_2"][i, j].partition_broadcast(P)).then_inc(sem("gain_in"), 16)

            def less_bias(name):
                bias = gain_of(name)[1]
                for g in range(4):
                    n = 4 * tsplits[name] + g
                    pool.wait_ge(sem("xhi_ready"), 2 * n + 2)
                    if g >= 2:
                        pool.wait_ge(sem("xlo_ready"), 2 * (n - 1))
                    ks = slice(2 * g, 2 * g + 2)
                    tt(hbuf[:, n % 2], xT_hi[:, ks, :].bitcast(F32), bc(bias[:, ks], 2, SEQ), ALU.subtract).then_inc(sem("less_bias"), 1)

            def natural(name):
                n = naturals[name]
                pool.wait_ge(sem("gain_in"), 32 * (n + 1))
                pool.wait_ge(sem("xn_ready"), TT * (norms[name] + 1))
                for t in range(TT):
                    step(tt(x[:, t, :], xn[:, t, :], gb[:, 0, :], ALU.mult))
                step.settle()
                if name != "final":
                    for t in range(TT):
                        step(tt(x[:, t, :], x[:, t, :], gb[:, 1, :], ALU.add))
                    step.settle()
                pool.sem_inc(sem("xnat_ready"), 1)
                if n + 1 < len(order) :
                    load_gain(order[n + 1])

            pool.wait_ge(sem("scan_done"), 1)
            load_gain("final")
            natural("final")
            for i in range(DEPTH):
                less_bias(f"ln0_{i}")
                natural(f"ln0_{i}")
                skew = bass.AP(ftab_d.tensor, P - 1, [[P - 1, P], [P * P, HEADS], [1, P]])
                pool.dma_start(biasL[:, :, :], skew).then_inc(sem("bias_in"), 16)
                pool.wait_ge(sem("bias_in"), 16 * (i + 1))
                do(tt(biasU[:, :, :], biasL[:, :, :], bc(const(C_NEGL), 1, HEADS), ALU.add))
                tt(biasL[:, :, :], biasL[:, :, :], bc(const(C_NEGU), 1, HEADS), ALU.add).then_inc(sem("bias_ready"), 1)
                pool.wait_ge(sem("alo_ready"), 2 * (i + 1))
                for t in range(TT):
                    nc.gpsimd.tensor_copy(Ti[:, t], bc(ident, 1, DH)).then_inc(sem("Ti_init"), 1)
                for t in range(TT):
                    pool.wait_ge(sem("decay_exp"), 2 * (TT * i + t + 1))
                    tt(AT[:, t], AT[:, t], bc(const(C_LE), 1, DH), ALU.mult).then_inc(sem("decay_ready"), 1)
                    do(tt(L[:, t], L[:, t], bc(const(C_GT), 1, DH), ALU.mult))
                    tt(L[:, t], L[:, t], bc(sm[:, 0, t, :], 2, P), ALU.mult).then_inc(sem("decay_ready"), 1)
                for lv in range(LEVELS):
                    for t in range(TT):
                        if lv == 0:
                            wait_evacuated(pool, use[f"kk{i}"] + t)
                            wait_filled(pool, use[f"qk{i}"] + 1)
                        else:
                            wait_filled(pool, use[f"Y{i}_{lv - 1}"] + t)
                        if lv == 1:
                            pool.wait_ge(sem("Ti_pairs"), TT * i + t + 1)
                        tt(Xm[:, t], L[:, t], bc(const(C_LVL + lv * P), 1, DH), ALU.mult).then_inc(sem("Xm_ready"), 1)
                        if lv == 0:
                            pool.wait_ge(sem("Xm_ready"), TT * LEVELS * i + t + 1)
                            pool.wait_ge(sem("Ti_init"), TT * i + t + 1)
                            tt(Ti[:, t], Ti[:, t], Xm[:, t], ALU.subtract).then_inc(sem("Ti_pairs"), 1)
                pool.wait_ge(sem("z_gate"), i + 1)
                szh = sz[:, :, :].rearrange("p t (h d) -> p (t h) d", d=DK)
                tt(szh, szh, bc(dng[:, i, :], 1, TT * DH), ALU.mult).then_inc(sem("sz_ready"), 1)
                less_bias(f"ln1_{i}")
                natural(f"ln1_{i}")
                if i < DEPTH - 1:
                    less_bias(f"ln2_{i}")
                    natural(f"ln2_{i}")

        @block.scalar
        def _(act):
            step = Steps(act, "act_steps")
            A = nc.scalar.activation

            act.dma_start(ident, T["const_masks"][:, C_ID:C_ID + P]).then_inc(sem("ident_in"), 16)
            for i, parts in enumerate(COLUMN_TILES[:2]):
                at = 0
                for name, n in parts:
                    act.dma_start(stage[at:at + n, i, :], rows_of(name)[:n, :]).then_inc(sem("cols_in"), 16)
                    at += n
            act.dma_start(relb[:, :], T["rel_bias_2"]).then_inc(sem("buckets_in"), 16)
            act.dma_start(bsel[:, :], T["const_buckets"]).then_inc(sem("buckets_in"), 16)

            def split_hi(p):
                if p >= n_panels:
                    return
                act.wait_ge(raw_loaded[p % RAW], 32 * (p // RAW + 1))
                if p >= SPL:
                    act.wait_ge(panel_used, p - SPL + 1)
                kt = panels[p][3]
                A(w_hi[:, p % SPL, 0:kt, :], raw[:, p % RAW, 0:kt, :], ACT.Copy).then_inc(hi_ready, 1)

            def gemm(name, evacuate, after=None, columns=None):
                for j, ps in enumerate(gemms[name][:columns]):
                    for p in ps[:-1]:
                        split_hi(p + SPL)
                    evacuate(j, use[name] + j)
                    split_hi(ps[-1] + SPL)
                    if after:
                        after(j, use[name] + j)

            def root(name):
                act.wait_ge(sem("var_ready"), norms[name] + 1)
                A(nrm[:, 1, :], nrm[:, 0, :], ACT.Sqrt).then_inc(sem("std_ready"), 1)

            def tsplit(name, gain=None, bias=None):
                for g in range(4):
                    n = 4 * tsplits[name] + g
                    act.wait_ge(sem("turned"), n + 1)
                    tr = trp[n % TRP][:, :].rearrange("p (k t) -> p k t", k=2)
                    if gain is None:
                        A(xT_hi[:, 2 * g:2 * g + 2, :], tr, ACT.Copy).then_inc(sem("xhi_ready"), 2)
                        continue
                    for k in range(2):
                        kk = 2 * g + k
                        if bias is None:
                            ins = A(xT_hi[:, kk, :], tr[:, k], ACT.Copy, scale=gain[:, kk:kk + 1])
                        else:
                            ins = A(xT_hi[:, kk, :], tr[:, k], ACT.Identity, scale=gain[:, kk:kk + 1], bias=bias[:, kk:kk + 1])
                        ins.then_inc(sem("xhi_ready"), 1)

            def ffn(f):
                def gate(j, u):
                    hn = f * 11 + j
                    if hn >= 2:
                        act.wait_ge(sem("hlo_ready"), hn - 1)
                    wait_filled(act, u)
                    h = hbuf[:, hn % 2]
                    if f < 2:
                        for n in range(2):
                            c = 2 * j + n
                            ins = A(h[:, n], A4(u)[:, n], ACT.Identity, scale=cols[:, 2 + f, 2 * FT + c:2 * FT + c + 1],
                                    bias=cols[:, 1, 48 + f * FT + c:48 + f * FT + c + 1])
                            ins.then_inc(sem("tap_ready"), 1)
                        act.wait_ge(sem("conv_ready"), 2 * hn + 2)
                        A(h, h, ACT.Silu).then_inc(sem("gate_ready"), 1)
                    else:
                        A(h, A4(u)[:, 0:2], ACT.Silu).then_inc(sem("gate_ready"), 1)

                def hidden(j, u):
                    wait_evacuated(act, u)
                    A(hT_hi[:, 2 * j:2 * j + 2, :], hbuf[:, (f * 11 + j) % 2], ACT.Copy).then_inc(sem("hhi_ready"), 1)

                gemm(f"up{f}", gate, hidden)
                gemm(f"down{f}", lambda j, u: None)

            act.wait_ge(sem("ssm_a_in"), 48)
            A(pn[:, 12, 2:4], pn[:, 12, 0:2], ACT.Exp).then_inc(sem("dt_ready"), 1)
            act.wait_ge(sem("mag_in"), 1)
            A(s_(13), s_(19), ACT.Exp).then_inc(sem("trig_ready"), 1)
            root("mix0")
            u = use["cols"]
            wait_filled(act, u)
            for i, parts in enumerate(COLUMN_TILES):
                n = sum(q[1] for q in parts)
                ins = A(cols[:, i, 0:n], acc[u % 2][:, i * P:i * P + n], ACT.Copy)
                if i < 5:
                    step(ins)
            step.settle()
            ins.then_inc(*freed(u))
            wait_evacuated(act, u)
            act.wait_ge(sem("angle_ready"), 1)
            A(s_(15), s_(14), ACT.Sin).then_inc(sem("trig_ready"), 1)
            A(s_(16), s_(14), ACT.Sin, scale=0.5).then_inc(sem("trig_ready"), 1)
            tsplit("mix0", *gain_of("mix0"))
            split_hi(0)
            split_hi(1)
            for r in range(2):
                u = use["CT"] + r
                wait_filled(act, u)
                v = acc[u % 2][:, :].rearrange("p (f k a h) -> p f k a h", f=8, k=4, a=2)
                for a in range(2):
                    rows = slice(a * ST, a * ST + ST)
                    A(CT[rows, r].rearrange("p (f k) h -> p f k h", f=8), v[rows, :, :, a, :], ACT.Copy,
                      scale=-1.0 if r else 1.0).then_inc(sem("CT_ready"), 1)
                act.wait_ge(sem("CT_ready"), 2 * r + 2)
                A(tb[:, 0, 0:1], acc[u % 2][:, 0:1], ACT.Copy).then_inc(*freed(u))
            u = use["ftab"]
            wait_filled(act, u)
            A(ftab[:, :], acc[u % 2][0:HEADS, 0:P], ACT.Copy).then_inc(*freed(u))
            wait_evacuated(act, u)
            act.dma_start(ftab_d, bc(ftab[:, :], 1, P)).then_inc(sem("ftab_stored"), 16)
            for p in range(2, SPL):
                split_hi(p)
            act.wait_ge(sem("bdw_in"), 16)
            A(bdw_hi[:, :, :, :], bdw[:, :, :, :], ACT.Copy).then_inc(sem("bdw_hi_ready"), 1)

            def ssm_in(j):
                def evacuate(_, u):
                    wait_filled(act, u)
                    A(uT[:, 4 * j:4 * j + 4, :], A4(u), ACT.Copy).then_inc(*freed(u))
                return evacuate

            gemm("ssm_in0", ssm_in(0))
            u = use["pT"]
            wait_filled(act, u)
            A(pT[:, :, :], acc[u % 2][:, 0:12 * PAIRS].rearrange("p (q k) -> p q k", q=12), ACT.Copy).then_inc(*freed(u))
            wait_evacuated(act, u)
            act.sem_inc(sem("pT_ready"), 1)
            gemm("ssm_in1", ssm_in(1))
            for j in range(4):
                u = use["BT"] + j
                wait_filled(act, u)
                A(BT[:, j // 2, 4 * (j % 2):4 * (j % 2) + 4].rearrange("p f r m -> p (f r m)"), acc[u % 2][:, :], ACT.Copy).then_inc(*freed(u))
                wait_evacuated(act, u)
                act.sem_inc(sem("BT_ready"), 1)
            for r in range(16):
                b, u = r // 2, use["bu"] + r
                if r % 2 == 0 and b >= 2:
                    act.wait_ge(sem("chunks_done"), b - 1)
                wait_filled(act, u)
                v = acc[u % 2][:, :].rearrange("p (k r t) -> p r k t", r=4, k=2)[:, 0:2, :, 0:SEQ // 2]
                A(bu[:, b % 2, :, 2 * (r % 2):2 * (r % 2) + 2, :], v, ACT.Copy).then_inc(*freed(u))
                wait_evacuated(act, u)
                act.sem_inc(sem("bu_ready"), 1)

            for f in range(8):
                act.wait_ge(sem("K_ready"), f + 1)
                A(lags[:, f].rearrange("p j h -> p (j h)"), trp[f % TRP][:, 0:P], ACT.Copy).then_inc(sem("lags_ready"), 1)
                A(skip[:, f], ident, ACT.Copy, scale=cols[:, 0, 40 + f:41 + f]).then_inc(sem("lags_ready"), 1)
            act.wait_ge(sem("CAm_cleared"), 1)

            def cam(f):
                if f >= 2:
                    act.wait_ge(sem("across_done"), f - 1)
                for a in range(2):
                    rows = slice(a * ST, a * ST + ST)
                    for c in range(2 if f < 2 else 1):
                        A(CAm[rows, f % 2, c, :, :, a * GH:a * GH + GH], CA[rows, :, c, 4 * f:4 * f + 4, :], ACT.Copy)\
                            .then_inc(sem("CAm_ready"), 1)

            cam(0)
            cam(1)
            for q in range(4):
                if q < 3:
                    cam(2 * q + 2)
                    cam(2 * q + 3)
                if q:
                    act.wait_ge(sem("ylo_ready"), q)
                act.wait_ge(sem("across_done"), 2 * q + 2)
                ins = A(tb[:, :, :], y_tiles(2 * q, 2), ACT.Gelu_apprx_tanh)
                if q % 2:
                    ins.then_inc(*freed(use["y"] + q // 2))
                    wait_evacuated(act, use["y"] + q // 2)
                else:
                    step(ins)
                    step.settle()
                A(xT_hi[:, 2 * q:2 * q + 2, :], tb[:, :, :], ACT.Copy).then_inc(sem("yhi_ready"), 1)

            def glu(j, u):
                if j >= 2:
                    act.wait_ge(sem("glu_added"), j - 1)
                wait_filled(act, u)
                A(hbuf[:, j % 2], A2(u)[:, :, PN // 2:PN], ACT.Sigmoid).then_inc(sem("glu_gate"), 1)

            gemm("glu", glu)
            root("ffn0")
            tsplit("ffn0", *gain_of("ffn0"))
            ffn(0)
            root("kv")
            tsplit("kv", *gain_of("kv"))

            def kv(j, u):
                wait_filled(act, u)
                if j < 2:
                    ins = A(kT[:, 4 * j:4 * j + 4, :], A4(u), ACT.Copy)
                else:
                    ins = A(vn_[:, :, (j - 2) * PN:(j - 1) * PN], A2(u), ACT.Copy)
                ins.then_inc(*freed(u))

            gemm("kv", kv)
            tsplit("mix1", *gain_of("mix1"))
            for half in range(2):
                def queries(j, u):
                    wait_filled(act, u)
                    A(qT[:, 4 * half:4 * half + 4, :], A4(u), ACT.Copy, scale=HD ** -0.5).then_inc(*freed(u))

                gemm(f"q{half}", queries)
                for n in range(4):
                    i, u = 4 * half + n, use[f"z{half}"] + n
                    wait_filled(act, u)
                    v = acc[u % 2][:, :].rearrange("p (h n) -> p h n", h=2)[:, :, 0:SW]
                    A(spS[:, 2 * i:2 * i + 2, :], v, ACT.Abs).then_inc(sem("z_abs"), 1)
                    act.wait_ge(sem("z_abs"), i + 1)
                    step(A(spS[:, 2 * i:2 * i + 2, :], spS[:, 2 * i:2 * i + 2, :], ACT.Exp, scale=-1.0))
                step.settle()
                for n in range(2):
                    i = 2 * half + n
                    A(spS[:, 4 * i:4 * i + 4, :], spS[:, 4 * i:4 * i + 4, :], ACT.Ln, bias=1.0).then_inc(sem("ln_ready"), 1)
            for i in range(8):
                act.wait_ge(sem("logw_ready"), i + 1)
                A(zS[:, 2 * i:2 * i + 2, :], zS[:, 2 * i:2 * i + 2, :], ACT.Exp).then_inc(sem("wexp_ready"), 1)
            for j in range(2):
                u = use["oT"] + j
                wait_filled(act, u)
                A(xT_hi[:, 4 * j:4 * j + 4, :], A4(u), ACT.Copy).then_inc(sem("ohi_ready"), 1)
            gemm("o", lambda j, u: None)
            root("ffn1")
            tsplit("ffn1", *gain_of("ffn1"))
            ffn(1)
            root("final")
            tsplit("final", *gain_of("final"))
            for i in range(DEPTH):
                ffn(2 + 2 * i)
                root(f"ln0_{i}")
                tsplit(f"ln0_{i}", *gain_of(f"ln0_{i}"))

                def win(j, u):
                    if j < CONV_COLS:
                        wait_filled(act, u)
                        for n in range(4):
                            c = 4 * j + n
                            A(qkT[:, c, :], A4(u)[:, n], ACT.Copy, scale=cols[:, 4 + i, 3 * CONV_T + c:3 * CONV_T + c + 1]).then_inc(sem("tap4_ready"), 1)
                    elif j < CONV_COLS + 2:
                        wait_filled(act, u)
                        c = 4 * (j - CONV_COLS)
                        A(qaT[:, c:c + 4, :], A4(u), ACT.Copy, scale=HD ** -0.5).then_inc(*freed(u))
                    else:
                        wait_filled(act, u)
                        for src in range(2):
                            for dst in range(2):
                                step(A(kaT[dst * HD:dst * HD + HD, src::2, :], A4(u)[src * HD:src * HD + HD, 0:2], ACT.Copy))
                        step.settle()
                        A(va[:, :, :], acc[u % 2][:, 512:1024].rearrange("p (t n) -> p t n", t=TT), ACT.Copy).then_inc(*freed(u))

                def conv_silu(j, u):
                    if 1 <= j <= CONV_COLS:
                        wait_evacuated(act, u - 1)
                        c = slice(4 * j - 4, 4 * j)
                        A(qkT[:, c, :], qkT[:, c, :], ACT.Silu).then_inc(sem("qkv_ready"), 1)

                gemm(f"win{i}", win, conv_silu, columns=SIDE)

                u = use[f"bd{i}"]
                wait_filled(act, u)
                b = acc[u % 2][:, 0:2 * TT * 8].rearrange("p (t n) -> p t n", t=TT)
                A(sm[:, 8], b[:, :, 0:8], ACT.Exp, scale=-1.0).then_inc(sem("beta_exp"), 1)
                act.wait_ge(sem("misc_in"), 64)
                step(A(sm[:, 9, 0, :], row[:, i, 0, :], ACT.Exp))
                act.wait_ge(sem("dt_raw"), i + 1)
                step(A(sm[:, 2], sm[:, 1], ACT.Abs))
                step.settle()
                step(A(sm[:, 2], sm[:, 2], ACT.Exp, scale=-1.0))
                step.settle()
                A(sm[:, 2], sm[:, 2], ACT.Ln, bias=1.0).then_inc(sem("dt_ln"), 1)

                def weights_exp(n):
                    act.wait_ge(sem("s_shifted"), 8 * i + n + 1)
                    A(zA[:, n % 2], zA[:, n % 2], ACT.Exp).then_inc(sem("s_exp"), 1)
                    A(red[:, 2, :], red[:, 2, :], ACT.Exp).then_inc(sem("s_exp"), 1)

                def attended(n):
                    u = use[f"oa{i}_{n}"]
                    wait_filled(act, u)
                    A(qaT[:, n, :], acc[u % 2][:, 0:SEQ], ACT.Copy).then_inc(*freed(u))

                def gate_columns(j):
                    for t in range(TT):
                        if j < SIDE + 2:
                            to = sz[:, t, (j - SIDE) * PN:(j - SIDE + 1) * PN]
                        else:
                            g, c = divmod(j - SIDE - 2, 2)
                            to = gates[:, t, g, c * PN:(c + 1) * PN]
                        A(to, trp[2 + t][:, :], ACT.Copy).then_inc(sem("gate_columns"), 1)

                def beside(n):
                    j, last, p = side_panel(i, n)
                    act.wait_ge(panel_used, p + 1)
                    if last:
                        gate_columns(j)
                    split_hi(p + SPL)

                beside(0)
                for n in range(8 + 2):
                    if n < 8:
                        weights_exp(n)
                    beside(n + 1)
                    if n >= 2:
                        attended(n - 2)
                    if n == 8:
                        act.wait_ge(sem("gate_columns"), 12 * i + 8)
                        A(gates[:, :, 0, :], gates[:, :, 0, :], ACT.Sigmoid).then_inc(sem("gate_a_ready"), 1)

                def unit_buffer(n):
                    return (kbg[:, :, :].rearrange("p h d -> p (h d)"), ktl[:, :, :].rearrange("p h d -> p (h d)"), xn[:, 0, :], xn[:, 1, :])[n]

                def squares(n):
                    g = (2, 3, 0, 1)[n]
                    A(unit_buffer(n), qkT[:, 4 * g:4 * g + 4, :].rearrange("p c t -> p (c t)"), ACT.Square).then_inc(sem("squares"), 1)

                act.wait_ge(sem("qkv_ready"), CONV_COLS * (i + 1))
                squares(0)
                squares(1)
                j, _, p = side_panel(i, 11)
                act.wait_ge(panel_used, p + 1)
                for h in range(2):
                    for n in range(2):
                        wait_evacuated(act, use[f"oa{i}_{4 * h + 2 + n}"])
                    A(xT_hi[:, 4 * h:4 * h + 4, :], qaT[:, 4 * h:4 * h + 4, :], ACT.Copy).then_inc(sem("ahi_ready"), 1)
                gate_columns(j)
                split_hi(p + SPL)
                act.wait_ge(sem("xnat_ready"), naturals[f"ln0_{i}"] + 1)
                squares(2)
                squares(3)
                for n in range(4):
                    u = use[f"ss{i}"] + n
                    wait_filled(act, u)
                    A(unit_buffer(n), acc[u % 2][:, :], ACT.Ln, bias=const(C_EPS, 1)).then_inc(*freed(u))
                act.wait_ge(sem("G_ready"), i + 1)
                step(A(sm[:, 5], sm[:, 4], ACT.Exp))
                A(sm[:, 7], sm[:, 7], ACT.Exp).then_inc(sem("G_exp"), 1)
                for t in range(TT):
                    act.wait_ge(sem("decay_log"), TT * i + t + 1)
                    A(AT[:, t], AT[:, t], ACT.Exp).then_inc(sem("decay_exp"), 1)
                    A(L[:, t], L[:, t], ACT.Exp, scale=-1.0).then_inc(sem("decay_exp"), 1)
                for n in range(4):
                    wait_evacuated(act, use[f"ss{i}"] + n)
                    A(unit_buffer(n), unit_buffer(n), ACT.Exp, scale=-0.5).then_inc(sem("inverse_norms"), 1)
                gemm(f"brA{i}_0", lambda j, u: None)
                for lv in range(1, LEVELS):
                    for t in range(TT):
                        u = use[f"Y{i}_{lv}"] + t
                        wait_filled(act, u)
                        A(Yp[:, t], A8(u), ACT.Copy).then_inc(*freed(u))
                    if lv == 2:
                        act.wait_ge(sem("gate_columns"), 12 * (i + 1))
                        A(sz[:, :, :], sz[:, :, :], ACT.Silu).then_inc(sem("z_gate"), 1)
                    if lv == 3:
                        A(gates[:, :, 1, :], gates[:, :, 1, :], ACT.Sigmoid).then_inc(sem("gate_b_ready"), 1)
                def copied(d, to):
                    u = use[f"dl{i}"] + d
                    wait_filled(act, u)
                    A(to, A8(u), ACT.Copy).then_inc(*freed(u))

                def output_squares(t):
                    act.wait_ge(sem("o_raw"), TT * i + t + 1)
                    A(Yp[:, t], L[:, t], ACT.Square).then_inc(sem("o_squares"), 1)

                def output_root(t):
                    act.wait_ge(sem("o_var"), TT * i + t + 1)
                    A(sm[:, 9, t], sm[:, 8, t], ACT.Sqrt).then_inc(sem("o_std"), 1)

                copied(0, Ti[:, 0])
                copied(2, Xm[:, 1])
                output_squares(0)
                copied(4, Ti[:, 1])
                output_root(0)
                output_squares(1)
                output_root(1)
                gemm(f"brA{i}_1", lambda j, u: None)
                tsplit(f"delta_{i}")
                gemm(f"brB{i}", lambda j, u: None)
                tsplit(f"mixed_{i}")
                gemm(f"wo{i}", lambda j, u: None)
                root(f"ln1_{i}")
                tsplit(f"ln1_{i}", *gain_of(f"ln1_{i}"))
                ffn(3 + 2 * i)
                root(f"ln2_{i}")
                if i < DEPTH - 1:
                    tsplit(f"ln2_{i}", *gain_of(f"ln2_{i}"))

        @block.vector
        def _(dve):
            step = Steps(dve, "dve_steps")
            V_ = nc.vector

            def do(ins):
                step(ins)
                step.settle()

            def split_lo(p):
                if p >= n_panels:
                    return
                dve.wait_ge(hi_ready, p + 1)
                kt = panels[p][3]
                V_.tensor_tensor(w_lo[:, p % SPL, 0:kt, :], raw[:, p % RAW, 0:kt, :], w_hi[:, p % SPL, 0:kt, :].bitcast(F32),
                                 ALU.subtract).then_inc(lo_ready, 1)

            late = []

            def gemm(name, evacuate, after=None, hold=0, columns=None):
                last = gemms[name][:columns][-1][-1]
                for j, ps in enumerate(gemms[name][:columns]):
                    for p in ps[:-1]:
                        if p <= last - hold:
                            split_lo(p + SPL)
                    evacuate(j, use[name] + j)
                    if ps[-1] <= last - hold:
                        split_lo(ps[-1] + SPL)
                    if after:
                        after(j, use[name] + j)
                late.extend(range(last - hold + 1 + SPL, last + 1 + SPL))

            def late_splits():
                for p in late:
                    split_lo(p)
                late.clear()

            def statistics(c, t0=0, t1=TT):
                for t in range(t0, t1):
                    step(V_.bn_stats(stat[:, t, c, :], x[:, t, c * PN:c * PN + PN]))

            def moments(eps, center):
                step.settle()
                for t in range(TT):
                    step(V_.bn_aggr(mv[:, t, :], stat[:, t].rearrange("p c s -> p (c s)")))
                step.settle()
                if center:
                    V_.tensor_scalar(nrm[:, 0, :], mv[:, :, 1], eps, None, ALU.add).then_inc(sem("var_ready"), 1)
                else:
                    do(V_.tensor_tensor(nrm[:, 2, :], mv[:, :, 0], mv[:, :, 0], ALU.mult))
                    V_.scalar_tensor_tensor(nrm[:, 0, :], nrm[:, 2, :], eps, mv[:, :, 1], ALU.add, ALU.add).then_inc(sem("var_ready"), 1)

            def inverse_root(name):
                dve.wait_ge(sem("std_ready"), norms[name] + 1)
                do(V_.reciprocal(nrm[:, 3, :], nrm[:, 1, :]))

            def norm(name, eps, center=False):
                moments(eps, center)
                inverse_root(name)
                for t in range(TT):
                    if center:
                        ins = V_.tensor_scalar(xn[:, t, :], x[:, t, :], mv[:, t, 0:1], nrm[:, 3, t:t + 1], ALU.subtract, ALU.mult)
                    else:
                        ins = V_.tensor_scalar(xn[:, t, :], x[:, t, :], nrm[:, 3, t:t + 1], None, ALU.mult)
                    ins.then_inc(sem("xn_ready"), 1)

            def norm_out(name, eps):
                moments(eps, True)
                dve.wait_ge(sem("gain_in"), 32 * (naturals[name] + 1))
                for t in range(TT):
                    step(V_.scalar_tensor_tensor(xn[:, t, :], x[:, t, :], mv[:, t, 0:1], gb[:, 0, :], ALU.subtract, ALU.mult))
                inverse_root(name)
                for t in range(TT):
                    V_.scalar_tensor_tensor(x[:, t, :], xn[:, t, :], nrm[:, 3, t:t + 1], gb[:, 1, :], ALU.mult, ALU.add).then_inc(sem("out_ready"), 1)

            def tsplit(name, gain=None, bias=None):
                for g in range(4):
                    n = 4 * tsplits[name] + g
                    dve.wait_ge(sem("xhi_ready"), 2 * n + 2)
                    tr = trp[n % TRP][:, :].rearrange("p (k t) -> p k t", k=2)
                    ks = slice(2 * g, 2 * g + 2)
                    if gain is None:
                        V_.tensor_tensor(xT_lo[:, ks, :], tr, xT_hi[:, ks, :].bitcast(F32), ALU.subtract).then_inc(sem("xlo_ready"), 2)
                        continue
                    leading = xT_hi[:, ks, :].bitcast(F32)
                    if bias is not None:
                        dve.wait_ge(sem("less_bias"), 4 * shifted[name] + g + 1)
                        leading = hbuf[:, n % 2]
                    for k in range(2):
                        kk = 2 * g + k
                        V_.scalar_tensor_tensor(xT_lo[:, kk, :], tr[:, k], gain[:, kk:kk + 1], leading[:, k],
                                                ALU.mult, ALU.subtract).then_inc(sem("xlo_ready"), 1)

            def add_to_x(name, scale=None, nat=None):
                def add(u, j, ts):
                    xs = x[:, ts, j * PN:j * PN + PN]
                    if scale is None:
                        return V_.tensor_tensor(xs, xs, A2(u)[:, ts], ALU.add)
                    return V_.scalar_tensor_tensor(xs, xs, scale, A2(u)[:, ts], ALU.mult, ALU.add)

                def evacuate(j, u):
                    if j < len(gemms[name]) - 1:
                        wait_filled(dve, u)
                        if nat is not None:
                            dve.wait_ge(sem("xnat_ready"), naturals[nat] + 1)
                        add(u, j, slice(0, TT)).then_inc(*freed(u))
                        wait_evacuated(dve, u)
                        statistics(j)
                        return
                    dve.wait_ge(sem("first_tokens"), residuals[name] + 1)
                    do(add(u, j, slice(0, 1)))
                    statistics(j, 0, 1)
                    wait_filled(dve, u)
                    add(u, j, slice(1, TT)).then_inc(*freed(u))
                    wait_evacuated(dve, u)
                    statistics(j, 1)
                return evacuate

            def ffn(f, scale=None, nat=None):
                def gate(j, u):
                    hn = f * 11 + j
                    h = hbuf[:, hn % 2]
                    if f < 2:
                        for n in range(2):
                            c = 2 * j + n
                            dve.wait_ge(sem("tap_ready"), 2 * hn + 2)
                            do(V_.scalar_tensor_tensor(h[:, n, 1:], A4(u)[:, n, 0:SEQ - 1], cols[:, 2 + f, FT + c:FT + c + 1], h[:, n, 1:], ALU.mult, ALU.add))
                            V_.scalar_tensor_tensor(h[:, n, 2:], A4(u)[:, n, 0:SEQ - 2], cols[:, 2 + f, c:c + 1], h[:, n, 2:], ALU.mult, ALU.add)\
                                .then_inc(sem("conv_ready"), 1)
                    dve.wait_ge(sem("gate_ready"), hn + 1)
                    V_.tensor_tensor(h, h, A4(u)[:, 2:4], ALU.mult).then_inc(*freed(u))

                def hidden(j, u):
                    hn = f * 11 + j
                    dve.wait_ge(sem("hhi_ready"), hn + 1)
                    ts_ = slice(2 * j, 2 * j + 2)
                    V_.tensor_tensor(hT_lo[:, ts_, :], hbuf[:, hn % 2], hT_hi[:, ts_, :].bitcast(F32), ALU.subtract).then_inc(sem("hlo_ready"), 1)

                gemm(f"up{f}", gate, hidden)
                gemm(f"down{f}", add_to_x(f"down{f}", scale, nat), hold=2)

            dve.wait_ge(sem("x_in"), 16)
            statistics(0)
            statistics(1)
            norm("mix0", EPS)
            tsplit("mix0", *gain_of("mix0"))
            split_lo(0)
            for p in range(1, SPL):
                split_lo(p)
            dve.wait_ge(sem("den_ready"), 1)
            V_.reciprocal(s_(19), s_(19)).then_inc(sem("inv_ready"), 1)
            dve.wait_ge(sem("bdw_hi_ready"), 1)
            V_.tensor_tensor(bdw_lo[:, :, :, :], bdw[:, :, :, :], bdw_hi[:, :, :, :].bitcast(F32), ALU.subtract).then_inc(sem("bdw_ready"), 1)
            gemm("ssm_in0", lambda j, u: None)

            dve.wait_ge(sem("pT_ready"), 1)
            dve.wait_ge(sem("ssm_b_in"), 32)
            t = [tmpv[:, i // 2, (i % 2) * 512:(i % 2) * 512 + 512].rearrange("p (k h) -> p k h", h=GH) for i in range(4)]
            for i, (r, f) in enumerate([(0, 7), (1, 8), (1, 7), (0, 8)]):
                step(V_.tensor_tensor(t[i], b_n[:, r], bc(pT[:, f, :], 2, GH), ALU.mult))
            step.settle()
            dve.wait_ge(sem("powers_ready"), 1)
            for a in range(2):
                rows = slice(a * ST, a * ST + ST)
                for r in range(2):
                    V_.tensor_tensor(Bm[rows, r, :, a * GH:a * GH + GH], t[2 * r][rows], t[2 * r + 1][rows],
                                     ALU.add if r else ALU.subtract).then_inc(sem("Bm_ready"), 1)
            dve.wait_ge(sem("Bm_ready"), 4)
            wait_filled(dve, use["CT"] + 1)
            for r in range(2):
                t = [tmpv[:, i, :].rearrange("p (k c) -> p k c", c=32) for i in range(2)]
                step(V_.tensor_tensor(t[0], Bm[:, r], bc(pT[:, 0, :], 2, 32), ALU.mult))
                do(V_.tensor_tensor(t[1], Bm[:, 1 - r], bc(pT[:, 1 + r, :], 2, 32), ALU.mult))
                ins = V_.tensor_tensor(BAm[:, r], t[0], t[1], ALU.add)
                if r == 0:
                    do(ins)
                else:
                    ins.then_inc(sem("BAm_ready"), 1)
            gemm("ssm_in1", lambda j, u: None)
            t1, t2 = tmpp[:, 0], tmpp[:, 1]
            for b in range(8):
                k = slice(4 * b, 4 * b + 4)
                dve.wait_ge(sem("bu_ready"), 2 * (b + 1))
                v = V[:, :, k, :]
                added = bu[:, b % 2].rearrange("p r k (c j) -> p r k c j", j=Q // 2)
                for j in range(1, Q // 2):
                    src = added[:, :, :, :, 0] if j == 1 else v
                    step(V_.tensor_tensor(t1, src, bc(bc(pT[:, 9, k], 1, 2), 3, NC_), ALU.mult))
                    for r in range(2):
                        step(V_.tensor_tensor(t2[:, r], src[:, 1 - r], bc(pT[:, 10 + r, k], 2, NC_), ALU.mult))
                    step.settle(2)
                    step(V_.tensor_tensor(t1, t1, added[:, :, :, :, j], ALU.add))
                    step.settle()
                    ins = V_.tensor_tensor(v, t1, t2, ALU.add)
                    if j < Q // 2 - 1:
                        do(ins)
                    else:
                        ins.then_inc(sem("chunks_done"), 1)
                dve.wait_ge(sem("chunks_done"), b + 1)
            step(V_.memset(E[:, :, :, 0], 0.0))
            do(V_.tensor_copy(E[:, :, :, 1], V[:, :, :, 0]))
            t1, t2 = (tmpp[:, i].rearrange("p r k c -> p r (k c)")[:, :, 0:PAIRS] for i in range(2))
            for c in range(2, NC_):
                e = E[:, :, :, c - 1]
                step(V_.tensor_tensor(t1, e, bc(pT[:, 4, :], 1, 2), ALU.mult))
                step(V_.tensor_tensor(t2, E[:, ::-1, :, c - 1], pT[:, 5:7, :], ALU.mult))
                step.settle(1)
                do(V_.tensor_tensor(t1, t1, V[:, :, :, c - 1], ALU.add))
                ins = V_.tensor_tensor(E[:, :, :, c], t1, t2, ALU.add)
                if c < NC_ - 1:
                    do(ins)
                else:
                    ins.then_inc(sem("scan_done"), 1)

            dve.wait_ge(sem("CAm_cleared"), 1)
            for q in range(4):
                for f in range(2 * q + 2, min(2 * q + 4, 8)):
                    dve.wait_ge(sem("across_done"), f - 1)
                    for a in range(2):
                        rows = slice(a * ST, a * ST + ST)
                        V_.tensor_copy(CAm[rows, f % 2, 1, :, :, a * GH:a * GH + GH], CA[rows, :, 1, 4 * f:4 * f + 4, :])\
                            .then_inc(sem("CAm_im_ready"), 1)
                dve.wait_ge(sem("yhi_ready"), q + 1)
                ks = slice(2 * q, 2 * q + 2)
                V_.tensor_tensor(xT_lo[:, ks, :], tb[:, :, :], xT_hi[:, ks, :].bitcast(F32), ALU.subtract).then_inc(sem("ylo_ready"), 1)

            def glu(j, u):
                dve.wait_ge(sem("glu_gate"), j + 1)
                h = hbuf[:, j % 2]
                V_.tensor_tensor(h, h, A2(u)[:, :, 0:PN // 2], ALU.mult).then_inc(*freed(u))
                wait_evacuated(dve, u)
                xs = x[:, :, j * PN // 2:(j + 1) * PN // 2]
                V_.tensor_tensor(xs, xs, h, ALU.add).then_inc(sem("glu_added"), 1)
                if j % 2:
                    dve.wait_ge(sem("glu_added"), j + 1)
                    statistics(j // 2)

            gemm("glu", glu, hold=2)
            norm("ffn0", EPS)
            tsplit("ffn0", *gain_of("ffn0"))
            late_splits()
            ffn(0)
            norm("kv", EPS)
            tsplit("kv", *gain_of("kv"))
            late_splits()
            gemm("kv", lambda j, u: None)
            tsplit("mix1", *gain_of("mix1"))
            def diagonal(t, hs):
                return t[:, hs, :].rearrange("p h (b q) -> p h b q", b=3)[:, :, 0::2, :]

            for i in range(4):
                half = i // 2
                if i % 2 == 0:
                    gemm(f"q{half}", lambda j, u: None)
                    for n in range(4):
                        u = use[f"z{half}"] + n
                        dve.wait_ge(sem("z_abs"), 4 * half + n + 1)
                        v = acc[u % 2][:, :].rearrange("p (h n) -> p h n", h=2)[:, :, 0:SW]
                        hs = slice(8 * half + 2 * n, 8 * half + 2 * n + 2)
                        V_.tensor_copy(zS[:, hs, :], v).then_inc(*freed(u))
                    for n in range(2, 4):
                        wait_evacuated(dve, use[f"z{half}"] + n)
                hs = slice(4 * i, 4 * i + 4)
                dve.wait_ge(sem("ln_ready"), i + 1)
                do(V_.scalar_tensor_tensor(spS[:, hs, :], zS[:, hs, :], 0.0, spS[:, hs, :], ALU.max, ALU.add))
                do(V_.tensor_tensor(zS[:, hs, :], zS[:, hs, :], spS[:, hs, :], ALU.subtract))
                V_.tensor_tensor(diagonal(spS, hs), diagonal(spS, hs), bc(bc(const(C_LT), 1, 2), 1, 4), ALU.mult).then_inc(sem("sp_ready"), 1)
            for i in range(8):
                u = use["rem"] + i
                hs = slice(2 * i, 2 * i + 2)
                wait_filled(dve, u)
                v = acc[u % 2][:, :].rearrange("p (h n) -> p h n", h=2)[:, :, 0:SW]
                V_.tensor_tensor(zS[:, hs, :], zS[:, hs, :], v, ALU.subtract).then_inc(*freed(u))
                wait_evacuated(dve, u)
                V_.tensor_copy(mv[:, 0, 0:1], zS[:, 2 * i, 0:1]).then_inc(sem("logw_ready"), 1)
            for i in range(8):
                hs = slice(2 * i, 2 * i + 2)
                dve.wait_ge(sem("wexp_ready"), i + 1)
                V_.tensor_tensor(diagonal(zS, hs), diagonal(zS, hs), bc(bc(const(C_LT), 1, 2), 1, 2), ALU.mult).then_inc(sem("w_ready"), 1)
            for j in range(2):
                u = use["oT"] + j
                dve.wait_ge(sem("ohi_ready"), j + 1)
                V_.tensor_tensor(xT_lo[:, 4 * j:4 * j + 4, :], A4(u), xT_hi[:, 4 * j:4 * j + 4, :].bitcast(F32), ALU.subtract).then_inc(*freed(u))
            gemm("o", add_to_x("o"), hold=2)
            norm("ffn1", EPS)
            tsplit("ffn1", *gain_of("ffn1"))
            late_splits()
            ffn(1)
            norm("final", EPS)
            tsplit("final", *gain_of("final"))
            late_splits()
            for i in range(DEPTH):
                last = "final" if i == 0 else f"ln2_{i - 1}"
                ffn(2 + 2 * i, 2 * ALPHA, last)
                norm(f"ln0_{i}", 4 * LN_EPS, True)
                tsplit(f"ln0_{i}", *gain_of(f"ln0_{i}"))
                late_splits()

                def short_conv(j, u):
                    if j >= CONV_COLS:
                        return
                    dve.wait_ge(sem("tap4_ready"), 4 * (CONV_COLS * i + j + 1))
                    for back in (1, 2, 3):
                        for n in range(4):
                            c = 4 * j + n
                            w = (3 - back) * CONV_T + c
                            ins = V_.scalar_tensor_tensor(qkT[:, c, back:], A4(u)[:, n, 0:SEQ - back], cols[:, 4 + i, w:w + 1],
                                                          qkT[:, c, back:], ALU.mult, ALU.add)
                            if back < 3 or n < 3:
                                step(ins)
                        if back < 3:
                            step.settle()
                    step.settle()
                    ins.then_inc(*freed(u))

                gemm(f"win{i}", short_conv, columns=SIDE)

                u = use[f"bd{i}"]
                b = acc[u % 2][:, 0:2 * TT * 8].rearrange("p (t n) -> p t n", t=TT)
                dve.wait_ge(sem("beta_exp"), i + 1)
                dve.wait_ge(sem("misc_in"), 64)
                V_.tensor_tensor(sm[:, 1], b[:, :, 8:16], bc(row[:, i, 1, :], 1, TT), ALU.add).then_inc(*freed(u))
                wait_evacuated(dve, u)
                dve.sem_inc(sem("dt_raw"), 1)
                do(V_.tensor_scalar(sm[:, 8], sm[:, 8], 1.0, None, ALU.add))
                step(V_.reciprocal(sm[:, 0], sm[:, 8]))
                dve.wait_ge(sem("dt_ln"), i + 1)
                do(V_.scalar_tensor_tensor(sm[:, 3], sm[:, 1], 0.0, sm[:, 2], ALU.max, ALU.add))
                V_.scalar_tensor_tensor(sm[:, 3], sm[:, 3], -1.0, bc(sm[:, 9, 0, :], 1, TT), ALU.mult, ALU.mult).then_inc(sem("g_ready"), 1)

                def scores(n):
                    u = use[f"s{i}_{n}"]
                    v = acc[u % 2][:, :].rearrange("p (h b k) -> p h b k", h=2, b=4)
                    hs = slice(2 * n, 2 * n + 2)
                    z, zp = zA[:, n % 2], zB[:, n % 2]
                    if n >= 2:
                        dve.wait_ge(sem("s_turned"), 8 * i + n - 1)
                    wait_filled(dve, u)
                    step(V_.tensor_tensor(z, v[:, :, 0:3:2, :], bc(biasL[:, hs, :], 2, 2), ALU.add))
                    step.settle()
                    V_.tensor_tensor(zp, v[:, :, 1, :], biasU[:, hs, :], ALU.add).then_inc(*freed(u))
                    wait_evacuated(dve, u)
                    do(V_.tensor_tensor(z[:, :, 1, :], z[:, :, 1, :], zp, ALU.max))
                    do(V_.tensor_reduce(red[:, 0, :].rearrange("p (h b) -> p h b", h=2), z, AX_X, ALU.max))
                    r = [red[:, q, :].rearrange("p (h b) -> p h b", h=2) for q in range(4)]
                    sink = bc(snk[:, i, hs], 2, 2)
                    do(V_.tensor_tensor(r[1], r[0], sink, ALU.max))
                    do(V_.tensor_tensor(r[2], sink, r[1], ALU.subtract))
                    V_.tensor_tensor(z, z, bc(r[1], 3, P), ALU.subtract).then_inc(sem("s_shifted"), 1)

                def normalize(n):
                    z = zA[:, n % 2]
                    r = [red[:, q, :].rearrange("p (h b) -> p h b", h=2) for q in range(4)]
                    dve.wait_ge(sem("s_exp"), 2 * (8 * i + n + 1))
                    do(V_.tensor_reduce(r[0], z, AX_X, ALU.add))
                    do(V_.tensor_tensor(r[0], r[0], r[2], ALU.add))
                    do(V_.reciprocal(r[3], r[0]))
                    V_.tensor_tensor(z, z, bc(r[3], 3, P), ALU.mult).then_inc(sem("s_normed"), 1)

                def mask_turned(n):
                    tr = trp[n % 2][:, :].rearrange("p (h b q) -> p h b q", h=2, b=2)
                    dve.wait_ge(sem("s_turned"), 8 * i + n + 1)
                    if n >= 1:
                        wait_filled(dve, use[f"oa{i}_{n - 1}"])
                    step(V_.tensor_tensor(pT3[:, :, 0::2, :], tr, bc(bc(const(C_LE), 1, 2), 1, 2), ALU.mult))
                    step.settle()
                    V_.tensor_tensor(pT3[:, :, 1, :], tr[:, :, 1, :], bc(const(C_GT), 1, 2), ALU.mult).then_inc(sem("pT3_ready"), 1)

                dve.wait_ge(sem("bias_ready"), i + 1)
                split_lo(side_panel(i, 0)[2] + SPL)
                for n in range(8 + 2):
                    if n < 8:
                        scores(n)
                        normalize(n)
                    if 1 <= n < 9:
                        mask_turned(n - 1)
                    split_lo(side_panel(i, n + 1)[2] + SPL)

                def gate_a(j):
                    def evacuate(_, u):
                        wait_filled(dve, u)
                        g = gates[:, :, 0, j * PN:(j + 1) * PN]
                        dve.wait_ge(sem("gate_a_ready"), i + 1)
                        V_.tensor_tensor(g, g, A2(u), ALU.mult).then_inc(*freed(u))
                    return evacuate

                u = use[f"G{i}"]
                wait_filled(dve, u)
                v = acc[u % 2][:, 0:32].rearrange("p (q t h) -> p q t h", q=2, t=TT)
                do(V_.tensor_copy(sm[:, 4], v[:, 0]))
                V_.tensor_tensor(sm[:, 7], v[:, 1], sm[:, 4], ALU.subtract).then_inc(*freed(u))
                wait_evacuated(dve, u)
                dve.sem_inc(sem("G_ready"), 1)
                for h in range(2):
                    dve.wait_ge(sem("ahi_ready"), 2 * i + h + 1)
                    hs = slice(4 * h, 4 * h + 4)
                    V_.tensor_tensor(xT_lo[:, hs, :], qaT[:, hs, :], xT_hi[:, hs, :].bitcast(F32), ALU.subtract).then_inc(sem("alo_ready"), 1)
                dve.wait_ge(sem("alo_ready"), 2 * (i + 1))
                for t in range(TT):
                    u = use[f"Gr{i}"] + t
                    wait_filled(dve, u)
                    V_.tensor_tensor(L[:, t], A8(u), bc(sm[:, 4, t, :], 2, P), ALU.subtract).then_inc(*freed(u))
                for t in range(TT):
                    wait_evacuated(dve, use[f"Gr{i}"] + t)
                    do(V_.tensor_scalar(AT[:, t], L[:, t], 0.0, None, ALU.min))
                    V_.tensor_scalar(L[:, t], L[:, t], 0.0, None, ALU.max).then_inc(sem("decay_log"), 1)
                split_lo(side_panel(i, 11)[2] + SPL)
                for t in range(TT):
                    V_.tensor_copy(U[:, t], bc(ident, 1, DH)).then_inc(sem("U_init"), 1)

                def unit(n):
                    g = (2, 3, 0, 1)[n]
                    sq = (kbg[:, :, :].rearrange("p h d -> p (h d)"), ktl[:, :, :].rearrange("p h d -> p (h d)"), xn[:, 0, :], xn[:, 1, :])[n]
                    qk = qkT[:, 4 * g:4 * g + 4, :].rearrange("p c t -> p (c t)")
                    dve.wait_ge(sem("inverse_norms"), 4 * i + n + 1)
                    V_.scalar_tensor_tensor(qk, qk, DK ** -0.5 if g < 2 else 1.0, sq, ALU.mult, ALU.mult).then_inc(sem("qk_normed"), 1)

                def scaled_rows(u, to, by):
                    wait_filled(dve, u)
                    V_.tensor_tensor(to, A8(u), bc(by, 2, P), ALU.mult).then_inc(*freed(u))

                def decayed(name, m):
                    for t in range(TT):
                        u = use[f"{name}{i}"] + t
                        wait_filled(dve, u)
                        dve.wait_ge(sem("decay_ready"), 2 * (TT * i + TT))
                        V_.tensor_tensor(m[:, t], A8(u), m[:, t], ALU.mult).then_inc(*freed(u))

                for n in range(4):
                    unit(n)
                dve.wait_ge(sem("G_exp"), i + 1)
                do(V_.scalar_tensor_tensor(sm[:, 6], sm[:, 0], -1.0, sm[:, 5], ALU.mult, ALU.mult))
                gemm(f"brA{i}_0", gate_a(0))
                dve.wait_ge(sem("qk_normed"), 4 * i + 4)
                scaled_rows(use[f"nat{i}k"], ktl[:, :, :], sm[:, 7, 0])
                scaled_rows(use[f"nat{i}k"] + 1, kbg[:, :, :], sm[:, 6, 1])
                decayed("kk", L)
                decayed("qk", AT)
                for t in range(TT):
                    scaled_rows(use[f"nat{i}v"] + t, vb[:, t], sm[:, 0, t])
                dve.wait_ge(sem("U_init"), 2 * (i + 1))
                for t in range(TT):
                    u = use[f"Y{i}_0"] + t
                    wait_filled(dve, u)
                    V_.tensor_tensor(U[:, t], U[:, t], A8(u), ALU.subtract).then_inc(*freed(u))
                dve.wait_ge(sem("Ti_pairs"), TT * (i + 1))
                for lv in range(1, LEVELS):
                    for t in range(TT):
                        for name, m, side in (("ZU", U, 1), ("ZT", Ti, 0)):
                            if f"{name}{i}_{lv}_{t}" in use:
                                u = use[f"{name}{i}_{lv}_{t}"]
                                wait_filled(dve, u)
                                wait_evacuated(dve, doubled(i, lv - 1, t, name))
                                part = blocks(m[:, t].rearrange("p h c -> p (h c)"), lv, side)
                                v = acc[u % 2][:, 0:512].rearrange("p (m b) -> p m b", b=1 << lv)
                                V_.tensor_tensor(part, part, v, ALU.subtract).then_inc(*freed(u))
                u = use[f"dl{i}"] + 1
                wait_filled(dve, u)
                V_.tensor_copy(Xm[:, 0], A8(u)).then_inc(*freed(u))
                def variance(t):
                    dve.wait_ge(sem("o_squares"), TT * i + t + 1)
                    do(V_.tensor_reduce(sm[:, 10, t], Yp[:, t], AX_X, ALU.add))
                    V_.tensor_scalar(sm[:, 8, t], sm[:, 10, t], 1 / DK, NORM_EPS, ALU.mult, ALU.add).then_inc(sem("o_var"), 1)

                def gated(t):
                    dve.wait_ge(sem("o_std"), TT * i + t + 1)
                    do(V_.reciprocal(sm[:, 11, t], sm[:, 9, t]))
                    do(V_.tensor_tensor(L[:, t], L[:, t], bc(sm[:, 11, t], 2, P), ALU.mult))
                    V_.tensor_tensor(L[:, t], L[:, t], sz[:, t].rearrange("p (h d) -> p h d", d=DK), ALU.mult).then_inc(sem("o_ready"), 1)

                u = use[f"dl{i}"] + 3
                wait_filled(dve, u)
                V_.tensor_copy(L[:, 0], A8(u)).then_inc(*freed(u))
                wait_evacuated(dve, u)
                dve.sem_inc(sem("o_raw"), 1)
                variance(0)
                u = use[f"dl{i}"] + 5
                wait_filled(dve, u)
                V_.tensor_tensor(L[:, 1], A8(u), bc(sm[:, 5, 1], 2, P), ALU.mult).then_inc(*freed(u))
                wait_evacuated(dve, u)
                wait_filled(dve, u + 1)
                V_.tensor_tensor(L[:, 1], L[:, 1], A8(u + 1), ALU.add).then_inc(*freed(u + 1))
                wait_evacuated(dve, u + 1)
                dve.sem_inc(sem("o_raw"), 1)
                dve.wait_ge(sem("sz_ready"), i + 1)
                gated(0)
                variance(1)
                gated(1)
                gemm(f"brA{i}_1", gate_a(1), hold=2)
                tsplit(f"delta_{i}")
                late_splits()

                def gate_b(j, u):
                    wait_filled(dve, u)
                    dve.wait_ge(sem("gate_b_ready"), i + 1)
                    g = gates[:, :, 1, j * PN:(j + 1) * PN]
                    V_.tensor_tensor(g, g, A2(u), ALU.mult).then_inc(*freed(u))
                    wait_evacuated(dve, u)
                    wait_evacuated(dve, use[f"brA{i}_{j}"])
                    ga = gates[:, :, 0, j * PN:(j + 1) * PN]
                    V_.tensor_tensor(ga, ga, g, ALU.add).then_inc(sem("mix_ready"), 1)

                gemm(f"brB{i}", gate_b, hold=2)
                tsplit(f"mixed_{i}")
                late_splits()
                gemm(f"wo{i}", add_to_x(f"wo{i}", ALPHA, f"ln0_{i}"), hold=2)
                norm(f"ln1_{i}", LN_EPS, True)
                tsplit(f"ln1_{i}", *gain_of(f"ln1_{i}"))
                late_splits()
                ffn(3 + 2 * i, 2 * ALPHA, f"ln1_{i}")
                if i < DEPTH - 1:
                    norm(f"ln2_{i}", 4 * LN_EPS, True)
                    tsplit(f"ln2_{i}", *gain_of(f"ln2_{i}"))
                    late_splits()
                else:
                    norm_out(f"ln2_{i}", 4 * LN_EPS)

        @block.tensor
        def _(pe):
            mm = nc.tensor.matmul

            def claim(u):
                if u >= 2:
                    pe.wait_ge(acc_freed[u % 2], u // 2)
                return acc[u % 2]

            def product(out, pairs, first, last):
                (ah, al), (bh, bl) = pairs
                mm(out, ah, bh, start=first, stop=False, skip_group_check=True)
                mm(out, ah, bl, start=False, stop=False, skip_group_check=True)
                return mm(out, al, bh, start=False, stop=last, skip_group_check=True)

            def features(name, j, u, src, n0=0, n1=4, ready=None):
                out = A4(u)
                claim(u)
                for i, p in enumerate(gemms[name][j]):
                    pe.wait_ge(lo_ready, p + 1)
                    _, _, k0, kt, _ = panels[p]
                    if ready and j == 0:
                        ready(k0, kt)
                    for n in range(n0, n1):
                        for k in range(kt):
                            c = slice(n * P, n * P + P)
                            w = (w_hi[:, p % SPL, k, c], w_lo[:, p % SPL, k, c])
                            a = (src[0][:, k0 + k, :], src[1][:, k0 + k, :])
                            ins = product(out[:, n], (w, a), i == 0 and k == 0 and n % 2 == 0, i == len(gemms[name][j]) - 1 and k == kt - 1)
                    if n1 == 4:
                        ins.then_inc(panel_used, 1)
                    else:
                        values(name, j, u, src, p, i)

            def values(name, j, u, src, p, i):
                out = acc[u % 2][:, 512:1024].rearrange("p (t n) -> p t n", t=TT)
                _, _, k0, kt, _ = panels[p]
                for t in range(TT):
                    for k in range(kt):
                        tok = slice(t * P, t * P + P)
                        a = (src[0][:, k0 + k, tok], src[1][:, k0 + k, tok])
                        w = (w_hi[:, p % SPL, k, 256:512], w_lo[:, p % SPL, k, 256:512])
                        ins = product(out[:, t], (a, w), i == 0 and k == 0 and t == 0, i == len(gemms[name][j]) - 1 and k == kt - 1)
                ins.then_inc(panel_used, 1)

            def tokens(name, j, u, src, ready=None):
                out = A2(u)
                claim(u)
                for i, p in enumerate(gemms[name][j]):
                    pe.wait_ge(lo_ready, p + 1)
                    _, _, k0, kt, _ = panels[p]
                    if ready and j == 0:
                        ready(k0, kt)
                    last = i == len(gemms[name][j]) - 1
                    by_tokens = last and name in residuals and j == len(gemms[name]) - 1
                    order = [(t, k) for t in range(TT) for k in range(kt)] if by_tokens else [(t, k) for k in range(kt) for t in range(TT)]
                    for t, k in order:
                        tok = slice(t * P, t * P + P)
                        a = (src[0][:, k0 + k, tok], src[1][:, k0 + k, tok])
                        w = (w_hi[:, p % SPL, k, :], w_lo[:, p % SPL, k, :])
                        ins = product(out[:, t], (a, w), i == 0 and k == 0, last and k == kt - 1)
                        if by_tokens and (t, k) == (0, kt - 1):
                            ins.then_inc(sem("first_tokens"), 1)
                    ins.then_inc(panel_used, 1)

            xT, hT = (xT_hi, xT_lo), (hT_hi, hT_lo)

            def xT_ready(name):
                return lambda k0, kt: pe.wait_ge(sem("xlo_ready"), 8 * tsplits[name] + k0 + kt)

            def stay_warm(bank, n):
                for _ in range(n):
                    mm(bank[:, 0:512], ident, cst[:, 0:512], start=True, stop=True, skip_group_check=True)

            def turn(name, src, ready, value):
                if name not in ("mix0", "mix1"):
                    stay_warm(trp[3], 5 if src is xn else 0)
                pe.wait_ge(sem(ready), value)
                for g in range(4):
                    n = 4 * tsplits[name] + g
                    if n >= TRP:
                        pe.wait_ge(sem("xlo_ready"), 2 * (n - TRP + 1))
                    for k in range(2):
                        for t in range(TT):
                            ins = nc.tensor.transpose(trp[n % TRP][:, (2 * k + t) * P:(2 * k + t + 1) * P],
                                                      src[:, t, (2 * g + k) * P:(2 * g + k + 1) * P], ident)
                    ins.then_inc(sem("turned"), 1)

            def turn_norm(norm_name, name=None):
                turn(name or norm_name, xn, "xn_ready", TT * (norms[norm_name] + 1))

            def ffn(f, xname):
                stay_warm(claim(use[f"up{f}"]), 3 if f >= 2 else 0)
                for j in range(11):
                    features(f"up{f}", j, use[f"up{f}"] + j, xT, ready=xT_ready(xname))
                for j in range(2):
                    tokens(f"down{f}", j, use[f"down{f}"] + j, hT,
                           lambda k0, kt: pe.wait_ge(sem("hlo_ready"), f * 11 + (k0 + kt) // 2))

            pe.wait_ge(sem("ident_in"), 16)
            pe.wait_ge(sem("cols_in"), 16 * sum(len(t) for t in COLUMN_TILES[:2]))
            pe.wait_ge(sem("conv_cols_in"), 16 * len(COLUMN_TILES[2:]))
            a = claim(use["cols"])
            for i, parts in enumerate(COLUMN_TILES):
                n = sum(q[1] for q in parts)
                ins = nc.tensor.transpose(a[:, i * P:i * P + n], stage[0:n, i, :], cst[0:n, C_ID:C_ID + n])
            ins.then_inc(acc_ready, 1)
            turn_norm("mix0")
            pe.wait_ge(sem("ssm_c_in"), 64)
            for r in range(2):
                a = claim(use["CT"] + r)
                for f in range(8):
                    ins = nc.tensor.transpose(a[:, f * P:f * P + P], c_n[:, r, f].rearrange("p a b -> p (a b)"), ident)
                ins.then_inc(acc_ready, 1)
            pe.wait_ge(sem("buckets_in"), 32)
            a = claim(use["ftab"])
            mm(a[0:HEADS, 0:P], relb[:, :], bsel[:, :], start=True, stop=True).then_inc(acc_ready, 1)
            features("ssm_in0", 0, use["ssm_in0"], xT, ready=xT_ready("mix0"))
            pe.wait_ge(sem("masks_in"), 16)
            pe.wait_ge(sem("powers_ready"), 1)
            a = claim(use["pT"])
            for at, q in enumerate([*range(9), 20, 21, 22]):
                ins = nc.tensor.transpose(a[:, at * PAIRS:(at + 1) * PAIRS], pn[:, q, :], cst[0:PAIRS, C_ID:C_ID + PAIRS])
            ins.then_inc(acc_ready, 1)
            features("ssm_in1", 0, use["ssm_in1"], xT)
            pe.wait_ge(sem("Bm_ready"), 4)
            for j in range(4):
                a = claim(use["BT"] + j)
                if j == 2:
                    pe.wait_ge(sem("BAm_ready"), 1)
                for f in range(4):
                    for r in range(2):
                        k = 16 * (j % 2) + 4 * f
                        ins = nc.tensor.transpose(a[:, (2 * f + r) * P:(2 * f + r + 1) * P],
                                                  (Bm, BAm)[j // 2][:, r, k:k + 4, :].rearrange("p k c -> p (k c)"), ident)
                ins.then_inc(acc_ready, 1)
            wait_evacuated(pe, use["ssm_in0"])
            wait_evacuated(pe, use["ssm_in1"])
            pe.wait_ge(sem("BT_ready"), 4)
            for r in range(16):
                u = use["bu"] + r
                claim(u)
                a = acc[u % 2][:, :].rearrange("p (k r t) -> p r k t", r=4, k=2)
                for k in range(2):
                    pair = 2 * r + k
                    rows = slice(32 * (pair % 4), 32 * (pair % 4) + 32)
                    for c in range(2):
                        for lag in (1, 0):
                            ins = mm(a[:, c, k], BT[rows, lag, pair // 4, c, :], uT[rows, pair // 4, 1 - lag::2],
                                     start=lag == 1, stop=lag == 0, skip_group_check=True)
                ins.then_inc(acc_ready, 1)

            def response(f):
                if f >= TRP:
                    pe.wait_ge(sem("lags_ready"), 2 * (f - TRP + 1))
                for k in range(4):
                    pair = 4 * f + k
                    o = trp[f % TRP][32 * k:32 * k + 32, 0:P].rearrange("p (j h) -> p j h", j=Q)
                    for r in range(2):
                        mm(o[:, 0], Bm[:, r, pair, :], CT[:, r, pair, :], start=r == 0, stop=r == 1, skip_group_check=True)
                        ins = mm(o[:, 1:Q], Bm[:, r, pair, :], CA[:, 0:Q - 1, r, pair, :], start=False, stop=r == 1, skip_group_check=True)
                ins.then_inc(sem("K_ready"), 1)

            pe.wait_ge(sem("CA_ready"), 1)
            for f in range(TRP):
                response(f)
            for f in range(8):
                if f % 4 == 0:
                    claim(use["y"] + f // 4)
                y = y_tiles(f)[:, 0].rearrange("p (c j) -> p c j", j=Q)
                uc = uT[:, f, :].rearrange("p (c j) -> p c j", j=Q)
                pe.wait_ge(sem("Kbd_ready"), f + 1)
                for j in range(Q):
                    ins = mm(y[:, :, j:Q], Kbd[:, f % 2, j, :], uc[:, :, 0:Q - j], start=j == 0 and f % 2 == 0, stop=False, skip_group_check=True)
                ins.then_inc(sem("within_done"), 1)
                if f < 8 - TRP:
                    response(f + TRP)
            pe.wait_ge(sem("scan_done"), 1)
            for f in range(8):
                y = y_tiles(f)[:, 0].rearrange("p (c j) -> p c j", j=Q)
                pe.wait_ge(sem("CAm_ready"), 4 * (f + 1) if f < 2 else 8 + 2 * (f - 1))
                if f >= 2:
                    pe.wait_ge(sem("CAm_im_ready"), 2 * (f - 1))
                for k in range(4):
                    for j in range(Q):
                        for r in range(2):
                            ins = mm(y[32 * k:32 * k + 32, :, j], CAm[:, f % 2, r, j, k, :], E[:, r, 4 * f + k, :], start=False,
                                     stop=r == 1, skip_group_check=True)
                ins.then_inc(sem("across_done"), 1)
            for j in range(4):
                tokens("glu", j, use["glu"] + j, xT, lambda k0, kt: pe.wait_ge(sem("ylo_ready"), (k0 + kt) // 2))
            turn_norm("ffn0")
            ffn(0, "ffn0")
            turn_norm("kv")
            for j in range(2):
                features("kv", j, use["kv"] + j, xT, ready=xT_ready("kv"))
            for j in range(2, 4):
                tokens("kv", j, use["kv"] + j, xT)
            turn_norm("kv", "mix1")
            for i in range(8):
                half = i // 4
                if i % 4 == 0:
                    stay_warm(claim(use[f"q{half}"]), 4 if half == 0 else 0)
                    features(f"q{half}", 0, use[f"q{half}"], xT, ready=xT_ready("mix1"))
                    wait_evacuated(pe, use[f"q{half}"])
                u = use[f"z{half}"] + i % 4
                a = claim(u)
                for h in range(2):
                    rows = slice(HD * h, HD * h + HD)
                    mm(a[:, h * 512:h * 512 + SEQ], kT[rows, i, 0:P], qT[rows, i, :], start=True, stop=True, skip_group_check=True)
                    ins = mm(a[:, h * 512 + SEQ:h * 512 + SW], kT[rows, i, P:SEQ], qT[rows, i, P:SEQ], start=True, stop=True, skip_group_check=True)
                ins.then_inc(acc_ready, 1)
            stay_warm(claim(use["rem"]), 8)
            for i in range(8):
                u = use["rem"] + i
                a = claim(u)
                pe.wait_ge(sem("sp_ready"), i // 2 + 1)
                for h in range(2):
                    s0 = spS[:, 2 * i + h, :]
                    mm(a[:, h * 512:h * 512 + SEQ], const(C_GT), s0[:, 0:SEQ], start=True, stop=False, skip_group_check=True)
                    mm(a[:, h * 512 + P:h * 512 + SEQ], const(C_ONE), s0[:, SEQ:SW], start=False, stop=True, skip_group_check=True)
                    ins = mm(a[:, h * 512 + SEQ:h * 512 + SW], const(C_GT), s0[:, SEQ:SW], start=True, stop=True, skip_group_check=True)
                ins.then_inc(acc_ready, 1)
            for j in range(2):
                u = use["oT"] + j
                a = claim(u)
                for i in range(4 * j, 4 * j + 4):
                    pe.wait_ge(sem("w_ready"), i + 1)
                    for h in range(2):
                        head = 2 * i + h
                        o = a[HD * h:HD * h + HD, (i % 4) * SEQ:(i % 4 + 1) * SEQ]
                        d = slice(head * HD, head * HD + HD)
                        mm(o, vn_[:, 0, d], zS[:, head, 0:SEQ], start=True, stop=False, skip_group_check=True)
                        ins = mm(o[:, P:SEQ], vn_[:, 1, d], zS[:, head, SEQ:SW], start=False, stop=True, skip_group_check=True)
                ins.then_inc(acc_ready, 1)
            wait_evacuated(pe, use["oT"])
            wait_evacuated(pe, use["oT"] + 1)
            for j in range(2):
                tokens("o", j, use["o"] + j, xT)
            turn_norm("ffn1")
            ffn(1, "ffn1")
            turn_norm("final")
            for i in range(DEPTH):
                ffn(2 + 2 * i, "final" if i == 0 else f"ln2_{i - 1}")
                turn_norm(f"ln0_{i}")
                stay_warm(claim(use[f"win{i}"]), 3)
                for j in range(SIDE):
                    u = use[f"win{i}"] + j
                    if j == SIDE - 1:
                        features(f"win{i}", j, u, xT, 0, 2)
                    else:
                        features(f"win{i}", j, u, xT, ready=xT_ready(f"ln0_{i}"))
                pe.wait_ge(sem("bdw_ready"), 1)
                a = claim(use[f"bd{i}"])
                for t in range(TT):
                    for k in range(KT):
                        tok = slice(t * P, t * P + P)
                        ins = product(a[:, 16 * t:16 * t + 16], ((xT_hi[:, k, tok], xT_lo[:, k, tok]), (bdw_hi[:, i, k, :], bdw_lo[:, i, k, :])),
                                      t == 0 and k == 0, k == KT - 1)
                ins.then_inc(acc_ready, 1)

                def scores(n):
                    u = use[f"s{i}_{n}"]
                    a = claim(u)
                    for h in range(2):
                        rows = slice(HD * h, HD * h + HD)
                        mm(a[:, h * 512:h * 512 + P], qaT[rows, n, 0:P], kaT[rows, n // 2, 0:P], start=True, stop=True, skip_group_check=True)
                        ins = mm(a[:, h * 512 + P:h * 512 + 3 * P], qaT[rows, n, P:SEQ], kaT[rows, n // 2, :], start=True, stop=True, skip_group_check=True)
                    ins.then_inc(acc_ready, 1)

                def turn_weights(n):
                    pe.wait_ge(sem("s_normed"), 8 * i + n + 1)
                    if n >= 2:
                        pe.wait_ge(sem("pT3_ready"), 8 * i + n - 1)
                    for h in range(2):
                        for b in range(2):
                            ins = nc.tensor.transpose(trp[n % 2][:, (2 * h + b) * P:(2 * h + b + 1) * P], zA[:, n % 2, h, b, :], ident)
                    ins.then_inc(sem("s_turned"), 1)

                def attend(n):
                    a = claim(use[f"oa{i}_{n}"])
                    pe.wait_ge(sem("pT3_ready"), 8 * i + n + 1)
                    d = slice((n // 2) * HD, (n // 2) * HD + HD)
                    for h in range(2):
                        rows = slice(HD * h, HD * h + HD)
                        mm(a[rows, 0:P], va[:, 0, d], pT3[:, h, 0, :], start=True, stop=True, skip_group_check=True)
                        mm(a[rows, P:SEQ], va[:, 0, d], pT3[:, h, 1, :], start=True, stop=False, skip_group_check=True)
                        ins = mm(a[rows, P:SEQ], va[:, 1, d], pT3[:, h, 2, :], start=False, stop=True, skip_group_check=True)
                    ins.then_inc(acc_ready, 1)

                def beside(n):
                    j, last, p = side_panel(i, n)
                    pe.wait_ge(lo_ready, p + 1)
                    _, _, k0, kt, _ = panels[p]
                    if k0 == 0 and i + j > SIDE:
                        pe.wait_ge(sem("gate_columns"), 12 * i + 2 * (j - SIDE))
                    for k in range(kt):
                        for t in range(TT):
                            tok = slice(t * P, t * P + P)
                            a = (xT_hi[:, k0 + k, tok], xT_lo[:, k0 + k, tok])
                            w = (w_hi[:, p % SPL, k, :], w_lo[:, p % SPL, k, :])
                            ins = product(trp[2 + t][:, :], (a, w), k0 + k == 0, last and k == kt - 1)
                    ins.then_inc(panel_used, 1)

                beside(0)
                for j in range(CONV_COLS, SIDE):
                    wait_evacuated(pe, use[f"win{i}"] + j)
                for n in range(8 + 2):
                    if n < 8:
                        scores(n)
                    beside(n + 1)
                    if 1 <= n < 9:
                        turn_weights(n - 1)
                    if n >= 2:
                        attend(n - 2)
                a = claim(use[f"G{i}"])
                pe.wait_ge(sem("g_ready"), i + 1)
                mm(a[:, 0:16], const(C_LE), sm[:, 3].rearrange("p t h -> p (t h)"), start=True, stop=True, skip_group_check=True)
                mm(a[:, 16:32], const(C_ONE), sm[:, 3].rearrange("p t h -> p (t h)"), start=True, stop=True, skip_group_check=True).then_inc(acc_ready, 1)
                beside(11)

                def branch_a(j):
                    tokens(f"brA{i}_{j}", 0, use[f"brA{i}_{j}"], xT, lambda k0, kt: pe.wait_ge(sem("alo_ready"), 2 * i + (k0 + kt) // 4))

                for t in range(TT):
                    a = claim(use[f"Gr{i}"] + t)
                    for h in range(DH):
                        ins = mm(a[:, h * P:h * P + P], sm[:, 3, t, h:h + 1].to_broadcast([P, P]), const(C_LE), start=True, stop=True, skip_group_check=True)
                    ins.then_inc(acc_ready, 1)
                for n in range(4):
                    sq = (kbg[:, :, :].rearrange("p h d -> p (h d)"), ktl[:, :, :].rearrange("p h d -> p (h d)"), xn[:, 0, :], xn[:, 1, :])[n]
                    a = claim(use[f"ss{i}"] + n)
                    pe.wait_ge(sem("squares"), 4 * i + n + 1)
                    for c in range(2):
                        ins = mm(a[:, c * 512:c * 512 + 512], const(C_ONE), sq[:, c * 512:c * 512 + 512], start=True, stop=True, skip_group_check=True)
                    ins.then_inc(acc_ready, 1)

                branch_a(0)

                def rows(u, src):
                    for t in range(TT):
                        a = claim(u + t)
                        for h in range(DH):
                            ins = nc.tensor.transpose(a[:, h * P:h * P + P], src[:, h, t * P:t * P + P], ident)
                        ins.then_inc(acc_ready, 1)

                def with_keys(u, right):
                    for t in range(TT):
                        a = claim(u + t)
                        tok = slice(t * P, t * P + P)
                        for h in range(DH):
                            ins = mm(a[:, h * P:h * P + P], kh[:, h, tok], right[:, h, tok], start=True, stop=True, skip_group_check=True)
                        ins.then_inc(acc_ready, 1)

                pe.wait_ge(sem("qkv_ready"), CONV_COLS * (i + 1))
                pe.wait_ge(sem("qk_normed"), 4 * i + 2)
                rows(use[f"nat{i}k"], kh)
                with_keys(use[f"kk{i}"], kh)
                pe.wait_ge(sem("qk_normed"), 4 * i + 4)
                with_keys(use[f"qk{i}"], qh)
                rows(use[f"nat{i}v"], vh)

                def heads_blocks(u, left, right, lv, side):
                    a = claim(u)
                    for h in range(DH):
                        o = a[:, h * HD:h * HD + HD].rearrange("p (m b) -> p m b", b=1 << lv)
                        ins = mm(o, left[:, h, :], blocks(right[:, h, :], lv, side), start=True, stop=True, skip_group_check=True)
                    ins.then_inc(acc_ready, 1)

                def heads(u, *terms):
                    a = claim(u)
                    for h in range(DH):
                        for n, (left, right) in enumerate(terms):
                            ins = mm(a[:, h * P:h * P + P], left[:, h, :], right[:, h, :], start=n == 0, stop=n == len(terms) - 1, skip_group_check=True)
                    ins.then_inc(acc_ready, 1)

                pe.wait_ge(sem("U_init"), TT * (i + 1))
                stay_warm(claim(use[f"Y{i}_0"]), 5)
                for lv in range(LEVELS):
                    for t in range(TT):
                        pe.wait_ge(sem("Xm_ready"), TT * (LEVELS * i + lv) + t + 1)
                        if lv:
                            wait_evacuated(pe, doubled(i, lv - 1, t, "ZU"))
                        heads(use[f"Y{i}_{lv}"] + t, (Xm[:, t], U[:, t]))
                    if lv == 0:
                        continue
                    for t in range(TT):
                        wait_evacuated(pe, use[f"Y{i}_{lv}"] + t)
                        if lv == 1:
                            pe.wait_ge(sem("Ti_pairs"), TT * i + t + 1)
                        else:
                            wait_evacuated(pe, doubled(i, lv - 1, t, "ZT"))
                        heads_blocks(use[f"ZU{i}_{lv}_{t}"], Ti[:, t], Yp[:, t], lv, 1)
                        if lv < LEVELS - 1:
                            heads_blocks(use[f"ZT{i}_{lv}_{t}"], Yp[:, t], Ti[:, t], lv, 0)
                for t in range(TT):
                    wait_evacuated(pe, use[f"ZU{i}_{LEVELS - 1}_{t}"])
                d = use[f"dl{i}"]
                heads(d, (U[:, 0], vb[:, 0]))
                heads(d + 1, (kbg, U[:, 1]))
                wait_evacuated(pe, d)
                heads(d + 2, (ktl, Ti[:, 0]))
                heads(d + 3, (AT[:, 0], Ti[:, 0]))
                wait_evacuated(pe, d + 1)
                wait_evacuated(pe, d + 2)
                heads(d + 4, (U[:, 1], vb[:, 1]), (Xm[:, 0], Xm[:, 1]))
                heads(d + 5, (qh[:, :, P:SEQ], Xm[:, 1]))
                wait_evacuated(pe, d + 4)
                heads(d + 6, (AT[:, 1], Ti[:, 1]))
                branch_a(1)
                pe.wait_ge(sem("gate_columns"), 12 * (i + 1))
                turn(f"delta_{i}", L[:, :, :, :].rearrange("p t h d -> p t (h d)"), "o_ready", TT * (i + 1))
                for j in range(2):
                    tokens(f"brB{i}", j, use[f"brB{i}"] + j, xT, xT_ready(f"delta_{i}"))
                turn(f"mixed_{i}", gates[:, :, 0, :], "mix_ready", 2 * (i + 1))
                for j in range(2):
                    tokens(f"wo{i}", j, use[f"wo{i}"] + j, xT, xT_ready(f"mixed_{i}"))
                turn_norm(f"ln1_{i}")
                ffn(3 + 2 * i, f"ln1_{i}")
                if i < DEPTH - 1:
                    turn_norm(f"ln2_{i}")


INPUTS = """x norm_mix norm_ffn norm_kv norm_final ssm_w_in ssm_a_re ssm_a_im ssm_log_dt ssm_b_re ssm_b_im ssm_c_re
ssm_c_im ssm_d ssm_w_glu kv_w attn_w_q attn_w_o ffn_w_up ffn_conv_w ffn_conv_b ffn_w_down rel_bias_2 ln_g_2 ln_b_2
ffn_w13_2 ffn_w2_2 w_in_2 conv_w_2 a_log_2 dt_bias_2 dn_norm_g_2 sinks_2 w_branch_a_2 w_branch_b_2 w_out_2""".split()


def kernel(**inputs):
    import concourse.bacc as _bacc
    from concourse.bass_utils import run_bass_kernel_spmd as _run

    nc = _bacc.Bacc("TRN2", target_bir_lowering=False, num_devices=1)
    arrays = {name: np.ascontiguousarray(inputs[name]) for name in INPUTS}
    arrays["const_masks"] = constants()
    arrays["const_buckets"] = bucket_pattern()
    tensors = {name: nc.dram_tensor(f"in_{name}", a.shape, F32, kind="ExternalInput").ap() for name, a in arrays.items()}
    out = nc.dram_tensor("out_x", (1, SEQ, D), F32, kind="ExternalOutput").ap()
    build(nc, tensors, out)
    result = _run(nc, [{f"in_{name}": a for name, a in arrays.items()}], core_ids=[0])
    return result.results[0]["out_x"]
```
